# Optimizing a Trainium2 kernel written in Bass

```python
import math
import jax
import jax.numpy as jnp
from jax import lax
import numpy as np

D_MODEL = 1024
BATCH = 1
SEQ = 1024
DEPTH = 1
DEC_BATCH = 8
DEC_SEQ = 1
PAST_LEN = 2048
PAGE_SIZE = 128

N_HEADS = 8
N_KV_HEADS = 2
GQA = N_HEADS // N_KV_HEADS
HEAD_DIM = 64
NSA_WIDTH = N_HEADS * HEAD_DIM
KV_WIDTH = 2 * N_KV_HEADS * HEAD_DIM
N_GATES = 3 * N_HEADS
CMP_LEN = 32
CMP_STRIDE = 16
CMP_RATIO = CMP_LEN // CMP_STRIDE
SEL_BLOCK = 64
N_SELECT = 16
WINDOW = 512
Q_BLOCK = 128
SSM_WIDTH = D_MODEL - NSA_WIDTH
SSM_GROUP = 16
SSM_GROUPS = SSM_WIDTH // SSM_GROUP
SSM_STATE = 64
MIX_WIDTH = NSA_WIDTH + SSM_WIDTH
IN_WIDTH = NSA_WIDTH + 3 * KV_WIDTH + N_GATES + SSM_WIDTH
D_FF = (D_MODEL * 11 // 4 + 127) // 128 * 128
CONV_W = 3
EPS = 1e-6
NEG = -1e30
BIG = 1e30

kernel_name = 'nsa_s5_hybrid_convffn_step'

def rmsnorm(x, g):
    xf = x.astype(jnp.float32)
    y = xf * lax.rsqrt(jnp.mean(xf * xf, axis=-1, keepdims=True) + EPS)
    return (y * g.astype(jnp.float32)).astype(x.dtype)

def pad_rows(a, n):
    return jnp.pad(a, ((0, 0), (0, n)) + ((0, 0),) * (a.ndim - 2))

def project_in(h, w_in):
    b, t = h.shape[:2]
    z = h @ w_in
    c0 = NSA_WIDTH
    cuts = [c0, c0 + KV_WIDTH, c0 + 2 * KV_WIDTH, c0 + 3 * KV_WIDTH, c0 + 3 * KV_WIDTH + N_GATES]
    q, kv_c, kv_s, kv_w, gl, u = jnp.split(z, cuts, axis=-1)
    kv_shape = (b, t, 2, N_KV_HEADS, HEAD_DIM)
    return (q.reshape(b, t, N_KV_HEADS, GQA, HEAD_DIM), kv_c.reshape(kv_shape), kv_s.reshape(kv_shape),
            kv_w.reshape(kv_shape), gl.reshape(b, t, N_KV_HEADS, GQA, 3), u)

def cmp_partials(kv_rows, w_cmp):
    b, l = kv_rows.shape[:2]
    sub = kv_rows.reshape(b, l // CMP_STRIDE, CMP_STRIDE, 2, N_KV_HEADS, HEAD_DIM)
    w = w_cmp.reshape(2, CMP_RATIO, CMP_STRIDE, HEAD_DIM, HEAD_DIM)
    return jnp.einsum('bnsxhd,xrsde->rbnxhe', sub, w)

def cmp_finish(parts, pe_cmp, w_cmp):
    n_cmp = parts.shape[2] - CMP_RATIO + 1
    kv_c = jnp.einsum('xld,xlde->xe', pe_cmp, w_cmp)[None, None, :, None, :]
    for r in range(CMP_RATIO):
        kv_c = kv_c + parts[r][:, r:r + n_cmp]
    cmp_end = jnp.arange(n_cmp) * CMP_STRIDE + CMP_LEN - 1
    return kv_c, cmp_end

def sel_map(n_cmp, n_sel):
    c0 = (jnp.arange(n_cmp) * CMP_STRIDE)[:, None]
    s0 = (jnp.arange(n_sel) * SEL_BLOCK)[None, :]
    return ((c0 < s0 + SEL_BLOCK) & (c0 + CMP_LEN > s0)).astype(jnp.float32)

def dense_block_gather(kv_blocks):
    def gather(idx):
        b = jnp.arange(idx.shape[0])[:, None, None, None]
        h = jnp.arange(N_KV_HEADS)[None, None, :, None]
        return kv_blocks[b, idx, :, :, h]
    return gather

def paged_block_gather(pool, layer, page_table, new_blocks):
    bpp = PAGE_SIZE // SEL_BLOCK
    n_past = page_table.shape[1] * bpp
    n_new = new_blocks.shape[1]
    def gather(idx):
        b = jnp.arange(idx.shape[0])[:, None, None, None]
        h = jnp.arange(N_KV_HEADS)[None, None, :, None]
        past_idx = jnp.minimum(idx, n_past - 1)
        page = page_table[b, past_idx // bpp]
        rows = ((past_idx % bpp) * SEL_BLOCK)[..., None] + jnp.arange(SEL_BLOCK)
        past = pool[layer, page[..., None], rows, :, h[..., None]]
        new = new_blocks[b, jnp.clip(idx - n_past, 0, n_new - 1), :, :, h]
        return jnp.where((idx < n_past)[..., None, None, None], past, new)
    return gather

def masked_softmax(s, m):
    return jax.nn.softmax(jnp.where(m, s, NEG), axis=-1)

def nsa_attend(q, gate_logits, q_pos, kv_c, cmp_end, n_sel, gather_sel, kv_w, w_pos):
    b, tq = q.shape[:2]
    scale = HEAD_DIM ** -0.5
    s_c = jnp.einsum('bqhgd,bnhd->bqhgn', q, kv_c[:, :, 0]).astype(jnp.float32) * scale
    m_c = (cmp_end[None, :] <= q_pos[:, None])[None, :, None, None, :]
    p_c = jnp.where(m_c, masked_softmax(s_c, m_c), 0.0)
    o_c = jnp.einsum('bqhgn,bnhd->bqhgd', p_c.astype(q.dtype), kv_c[:, :, 1])
    imp = jnp.einsum('bqhn,ns->bqhs', p_c.sum(axis=3), sel_map(kv_c.shape[1], n_sel))
    blk = jnp.arange(n_sel)[None, :]
    allowed = (blk * SEL_BLOCK <= q_pos[:, None])[None, :, None, :]
    forced = ((blk == 0) | (blk == (q_pos // SEL_BLOCK)[:, None]))[None, :, None, :]
    score = jnp.where(forced, BIG, jnp.where(allowed, imp, NEG))
    top_val, top_idx = lax.top_k(score, min(N_SELECT, n_sel))
    k_sel = top_idx.shape[-1]
    kv_s = gather_sel(top_idx)
    tok_pos = top_idx[..., None] * SEL_BLOCK + jnp.arange(SEL_BLOCK)
    m_s = ((top_val > 0.5 * NEG)[..., None] & (tok_pos <= q_pos[None, :, None, None, None]))
    m_s = m_s.reshape(b, tq, N_KV_HEADS, 1, k_sel * SEL_BLOCK)
    k_s = kv_s[..., 0, :].reshape(b, tq, N_KV_HEADS, k_sel * SEL_BLOCK, HEAD_DIM)
    v_s = kv_s[..., 1, :].reshape(b, tq, N_KV_HEADS, k_sel * SEL_BLOCK, HEAD_DIM)
    s_s = jnp.einsum('bqhgd,bqhmd->bqhgm', q, k_s).astype(jnp.float32) * scale
    o_s = jnp.einsum('bqhgm,bqhmd->bqhgd', masked_softmax(s_s, m_s).astype(q.dtype), v_s)
    s_w = jnp.einsum('bqhgd,bwhd->bqhgw', q, kv_w[:, :, 0]).astype(jnp.float32) * scale
    m_w = ((w_pos[None, :] <= q_pos[:, None]) & (w_pos[None, :] >= q_pos[:, None] - WINDOW)
           & (w_pos[None, :] >= 0))[None, :, None, None, :]
    o_w = jnp.einsum('bqhgw,bwhd->bqhgd', masked_softmax(s_w, m_w).astype(q.dtype), kv_w[:, :, 1])
    g = jax.nn.sigmoid(gate_logits.astype(jnp.float32)).astype(q.dtype)
    return g[..., 0:1] * o_c + g[..., 1:2] * o_s + g[..., 2:3] * o_w

def _ssm_combine(e1, e2):
    ar1, ai1, br1, bi1 = e1
    ar2, ai2, br2, bi2 = e2
    return (ar1 * ar2 - ai1 * ai2, ar1 * ai2 + ai1 * ar2,
            ar2 * br1 - ai2 * bi1 + br2, ar2 * bi1 + ai2 * br1 + bi2)

def ssm_scan(u, h0_re, h0_im, p):
    b, t = u.shape[:2]
    ug = u.astype(jnp.float32).reshape(b, t, SSM_GROUPS, SSM_GROUP)
    dt = jnp.exp(p['ssm_log_dt'].astype(jnp.float32))[:, None]
    are = p['ssm_a_re'].astype(jnp.float32)
    aim = p['ssm_a_im'].astype(jnp.float32)
    mag = jnp.exp(dt * are)
    ab_re, ab_im = mag * jnp.cos(dt * aim), mag * jnp.sin(dt * aim)
    den = are * are + aim * aim
    zr, zi = ab_re - 1.0, ab_im
    f_re = (zr * are + zi * aim) / den
    f_im = (zi * are - zr * aim) / den
    b_re = p['ssm_b_re'].astype(jnp.float32)
    b_im = p['ssm_b_im'].astype(jnp.float32)
    bb_re = f_re[..., None] * b_re - f_im[..., None] * b_im
    bb_im = f_re[..., None] * b_im + f_im[..., None] * b_re
    bu_re = jnp.einsum('btgc,gpc->btgp', ug, bb_re)
    bu_im = jnp.einsum('btgc,gpc->btgp', ug, bb_im)
    if h0_re is not None:
        h0r = h0_re.astype(jnp.float32)
        h0i = h0_im.astype(jnp.float32)
        bu_re = bu_re.at[:, 0].add(ab_re * h0r - ab_im * h0i)
        bu_im = bu_im.at[:, 0].add(ab_re * h0i + ab_im * h0r)
    a_r = jnp.broadcast_to(ab_re, bu_re.shape)
    a_i = jnp.broadcast_to(ab_im, bu_im.shape)
    _, _, h_re, h_im = lax.associative_scan(_ssm_combine, (a_r, a_i, bu_re, bu_im), axis=1)
    c_re = p['ssm_c_re'].astype(jnp.float32)
    c_im = p['ssm_c_im'].astype(jnp.float32)
    y = (jnp.einsum('btgp,gcp->btgc', h_re, c_re) - jnp.einsum('btgp,gcp->btgc', h_im, c_im)
         + p['ssm_d'].astype(jnp.float32).reshape(SSM_GROUPS, SSM_GROUP) * ug)
    return y.reshape(b, t, SSM_WIDTH).astype(u.dtype), h_re[:, -1], h_im[:, -1]

def ssm_glu(y, p):
    z = jax.nn.gelu(y) @ p['w_glu'] + p['b_glu']
    za, zb = jnp.split(z, 2, axis=-1)
    return za * jax.nn.sigmoid(zb)

def ffn_block(x, hist, p):
    hu = rmsnorm(x, p['norm_ffn']) @ p['w_up']
    hp = jnp.concatenate([hist.astype(hu.dtype), hu], axis=1)
    c = lax.conv_general_dilated(hp, p['conv_w'][:, None, :], (1,), 'VALID',
                                 dimension_numbers=('NWC', 'WIO', 'NWC'),
                                 feature_group_count=hu.shape[-1]) + p['conv_b']
    a, g = jnp.split(c, 2, axis=-1)
    return x + (jax.nn.silu(a) * g) @ p['w_down'], hp[:, -(CONV_W - 1):]

def prompt_layer(x, p):
    b, t, _ = x.shape
    h = rmsnorm(x, p['norm_mix'])
    q, kvc_rows, kvs_rows, kvw_rows, gl, u = project_in(h, p['w_in'])
    kv_c, cmp_end = cmp_finish(cmp_partials(kvc_rows, p['w_cmp']), p['pe_cmp'], p['w_cmp'])
    n_sel = t // SEL_BLOCK
    gather = dense_block_gather(kvs_rows.reshape(b, n_sel, SEL_BLOCK, 2, N_KV_HEADS, HEAD_DIM))
    kvw_pad = pad_rows(kvw_rows[:, ::-1], WINDOW)[:, ::-1]
    n_qb = t // Q_BLOCK
    qb = q.reshape(b, n_qb, Q_BLOCK, N_KV_HEADS, GQA, HEAD_DIM).swapaxes(0, 1)
    gb = gl.reshape(b, n_qb, Q_BLOCK, N_KV_HEADS, GQA, 3).swapaxes(0, 1)

    def query_block(args):
        q_i, g_i, i = args
        start = i * Q_BLOCK
        kvw_i = lax.dynamic_slice_in_dim(kvw_pad, start, WINDOW + Q_BLOCK, axis=1)
        w_pos = start - WINDOW + jnp.arange(WINDOW + Q_BLOCK)
        return nsa_attend(q_i, g_i, start + jnp.arange(Q_BLOCK), kv_c, cmp_end, n_sel, gather, kvw_i, w_pos)

    o = lax.map(query_block, (qb, gb, jnp.arange(n_qb)))
    o_nsa = o.swapaxes(0, 1).reshape(b, t, NSA_WIDTH)
    y_ssm, h_re, h_im = ssm_scan(u, None, None, p)
    x = x + jnp.concatenate([o_nsa, ssm_glu(y_ssm, p)], axis=-1) @ p['w_out']
    x, conv_state = ffn_block(x, jnp.zeros((b, CONV_W - 1, 2 * D_FF), x.dtype), p)
    win_keep = min(WINDOW, t)
    return x, (kvc_rows, kvs_rows, kvw_rows[:, t - win_keep:], h_re, h_im, conv_state)

def sample_layer(x, layer, cache_kv_cmp, cache_kv_sel, kv_win_buf, h0_re, h0_im, conv_hist, page_table, p):
    bd, s, _ = x.shape
    past_len = page_table.shape[1] * PAGE_SIZE
    h = rmsnorm(x, p['norm_mix'])
    q, kvc_new, kvs_new, kvw_new, gl, u = project_in(h, p['w_in'])
    kvc_past = cache_kv_cmp[layer, page_table].reshape(bd, past_len, 2, N_KV_HEADS, HEAD_DIM)
    s_pad = -(-s // CMP_STRIDE) * CMP_STRIDE - s
    parts = jnp.concatenate([cmp_partials(kvc_past, p['w_cmp']),
                             cmp_partials(pad_rows(kvc_new, s_pad), p['w_cmp'])], axis=2)
    kv_c, cmp_end = cmp_finish(parts, p['pe_cmp'], p['w_cmp'])
    n_past_sel = past_len // SEL_BLOCK
    n_new_sel = -(-s // SEL_BLOCK)
    new_blocks = pad_rows(kvs_new, n_new_sel * SEL_BLOCK - s).reshape(
        bd, n_new_sel, SEL_BLOCK, 2, N_KV_HEADS, HEAD_DIM)
    gather = paged_block_gather(cache_kv_sel, layer, page_table, new_blocks)
    n_buf = kv_win_buf.shape[1]
    kv_w = jnp.concatenate([kv_win_buf.astype(kvw_new.dtype), kvw_new], axis=1)
    w_pos = past_len - n_buf + jnp.arange(n_buf + s)
    q_pos = past_len + jnp.arange(s)
    o = nsa_attend(q, gl, q_pos, kv_c, cmp_end, n_past_sel + n_new_sel, gather, kv_w, w_pos)
    o_nsa = o.reshape(bd, s, NSA_WIDTH)
    y_ssm, h_re, h_im = ssm_scan(u, h0_re, h0_im, p)
    x = x + jnp.concatenate([o_nsa, ssm_glu(y_ssm, p)], axis=-1) @ p['w_out']
    x, conv_state = ffn_block(x, conv_hist, p)
    win_keep = min(WINDOW, n_buf + s)
    return x, (kvc_new, kvs_new, kv_w[:, n_buf + s - win_keep:], h_re, h_im, conv_state)

def setup_inputs(seed: int = 0) -> dict:
    key = jax.random.key(seed)
    ks = iter(jax.random.split(key, 40))

    def nrm(shape, scale):
        return scale * jax.random.normal(next(ks), shape, jnp.float32)

    n_pages = PAST_LEN // PAGE_SIZE
    n_used = DEC_BATCH * n_pages
    n_pool = n_used + -(-n_used // 4)
    win_len = min(WINDOW, PAST_LEN)
    page_table = jax.random.permutation(next(ks), n_pool)[:n_used].reshape(DEC_BATCH, n_pages).astype(jnp.int32)
    L = DEPTH
    a_im0 = math.pi * jnp.arange(SSM_STATE, dtype=jnp.float32)
    log_dt = jax.random.uniform(next(ks), (L, SSM_GROUPS), jnp.float32, math.log(1e-3), math.log(1e-1))
    return {
        'x_prompt': nrm((BATCH, SEQ, D_MODEL), 1.0),
        'x_sample': nrm((DEC_BATCH, DEC_SEQ, D_MODEL), 1.0),
        'cache_kv_cmp': nrm((L, n_pool, PAGE_SIZE, 2, N_KV_HEADS, HEAD_DIM), 1.0),
        'cache_kv_sel': nrm((L, n_pool, PAGE_SIZE, 2, N_KV_HEADS, HEAD_DIM), 1.0),
        'cache_kv_win': nrm((L, DEC_BATCH, win_len, 2, N_KV_HEADS, HEAD_DIM), 1.0),
        'state_ssm_re': nrm((L, DEC_BATCH, SSM_GROUPS, SSM_STATE), 0.1),
        'state_ssm_im': nrm((L, DEC_BATCH, SSM_GROUPS, SSM_STATE), 0.1),
        'state_ffn_conv': nrm((L, DEC_BATCH, CONV_W - 1, 2 * D_FF), 1.0),
        'page_table': page_table,
        'norm_mix': 1.0 + nrm((L, D_MODEL), 0.01),
        'w_in': nrm((L, D_MODEL, IN_WIDTH), D_MODEL ** -0.5),
        'pe_cmp': nrm((L, 2, CMP_LEN, HEAD_DIM), 0.02),
        'w_cmp': nrm((L, 2, CMP_LEN, HEAD_DIM, HEAD_DIM), (CMP_LEN * HEAD_DIM) ** -0.5),
        'ssm_a_re': -0.5 + nrm((L, SSM_GROUPS, SSM_STATE), 0.01),
        'ssm_a_im': a_im0 + nrm((L, SSM_GROUPS, SSM_STATE), 0.01),
        'ssm_log_dt': log_dt,
        'ssm_b_re': nrm((L, SSM_GROUPS, SSM_STATE, SSM_GROUP), (2 * SSM_GROUP) ** -0.5),
        'ssm_b_im': nrm((L, SSM_GROUPS, SSM_STATE, SSM_GROUP), (2 * SSM_GROUP) ** -0.5),
        'ssm_c_re': nrm((L, SSM_GROUPS, SSM_GROUP, SSM_STATE), (2 * SSM_STATE) ** -0.5),
        'ssm_c_im': nrm((L, SSM_GROUPS, SSM_GROUP, SSM_STATE), (2 * SSM_STATE) ** -0.5),
        'ssm_d': nrm((L, SSM_WIDTH), 1.0),
        'w_glu': nrm((L, SSM_WIDTH, 2 * SSM_WIDTH), SSM_WIDTH ** -0.5),
        'b_glu': nrm((L, 2 * SSM_WIDTH), 0.01),
        'w_out': nrm((L, MIX_WIDTH, D_MODEL), MIX_WIDTH ** -0.5),
        'norm_ffn': 1.0 + nrm((L, D_MODEL), 0.01),
        'w_up': nrm((L, D_MODEL, 2 * D_FF), D_MODEL ** -0.5),
        'conv_w': nrm((L, CONV_W, 2 * D_FF), CONV_W ** -0.5),
        'conv_b': nrm((L, 2 * D_FF), 0.01),
        'w_down': nrm((L, D_FF, D_MODEL), D_FF ** -0.5),
        'norm_final': 1.0 + nrm((D_MODEL,), 0.01),
    }

def reference(x_prompt, x_sample, cache_kv_cmp, cache_kv_sel, cache_kv_win, state_ssm_re, state_ssm_im,
              state_ffn_conv, page_table, norm_mix, w_in, pe_cmp, w_cmp, ssm_a_re, ssm_a_im, ssm_log_dt,
              ssm_b_re, ssm_b_im, ssm_c_re, ssm_c_im, ssm_d, w_glu, b_glu, w_out, norm_ffn, w_up, conv_w,
              conv_b, w_down, norm_final):
    xp, xs = x_prompt, x_sample
    sp, ss = [], []
    for l in range(DEPTH):
        p = {'norm_mix': norm_mix[l], 'w_in': w_in[l], 'pe_cmp': pe_cmp[l], 'w_cmp': w_cmp[l],
             'ssm_a_re': ssm_a_re[l], 'ssm_a_im': ssm_a_im[l], 'ssm_log_dt': ssm_log_dt[l],
             'ssm_b_re': ssm_b_re[l], 'ssm_b_im': ssm_b_im[l], 'ssm_c_re': ssm_c_re[l], 'ssm_c_im': ssm_c_im[l],
             'ssm_d': ssm_d[l], 'w_glu': w_glu[l], 'b_glu': b_glu[l], 'w_out': w_out[l],
             'norm_ffn': norm_ffn[l], 'w_up': w_up[l], 'conv_w': conv_w[l], 'conv_b': conv_b[l],
             'w_down': w_down[l]}
        xp, st_p = prompt_layer(xp, p)
        sp.append(st_p)
        xs, st_s = sample_layer(xs, l, cache_kv_cmp, cache_kv_sel, cache_kv_win[l], state_ssm_re[l],
                                state_ssm_im[l], state_ffn_conv[l], page_table, p)
        ss.append(st_s)
    y_prompt = rmsnorm(xp, norm_final)
    y_sample = rmsnorm(xs, norm_final)
    p_kv_cmp, p_kv_sel, p_kv_win, p_ssm_re, p_ssm_im, p_ffn_conv = [jnp.stack(a) for a in zip(*sp)]
    s_kv_cmp, s_kv_sel, s_kv_win, s_ssm_re, s_ssm_im, s_ffn_conv = [jnp.stack(a) for a in zip(*ss)]
    return (y_prompt, y_sample, p_kv_cmp, p_kv_sel, p_kv_win, p_ssm_re, p_ssm_im, p_ffn_conv,
            s_kv_cmp, s_kv_sel, s_kv_win, s_ssm_re, s_ssm_im, s_ffn_conv)


_drawn_inputs = setup_inputs


def setup_inputs(seed=0):
    import zlib

    import numpy as np

    out = dict(_drawn_inputs(seed))
    spreads = {}
    factors = {'cache_kv_sel': 3.174,
     'norm_mix': 5.822,
     'pe_cmp': 7.76,
     'ssm_a_re': 3.861,
     'ssm_c_re': 3.825,
     'ssm_c_im': 3.751,
     'b_glu': 8.0,
     'norm_ffn': 5.755,
     'conv_b': 7.794,
     'norm_final': 5.833}
    for name, (base, spread) in spreads.items():
        noise = np.random.default_rng([zlib.crc32(name.encode()), seed]).standard_normal(out[name].shape)
        drawn = base * np.exp(spread * noise) if base else spread * noise
        out[name] = jnp.asarray(drawn.astype(out[name].dtype))
    for name, factor in factors.items():
        out[name] = (out[name] * factor).astype(out[name].dtype)
    return out
```

```python
import concourse.bass as bass
from concourse import mybir

F32 = mybir.dt.float32
BF16 = mybir.dt.bfloat16
I32 = mybir.dt.int32
U32 = mybir.dt.uint32
ALU = mybir.AluOpType
ACT = mybir.ActivationFunctionType
AX = mybir.AxisListType

P = 128
D_MODEL = 1024
SEQ = 1024
NB = 8
TOK = SEQ + NB
TG = TOK // 3
KD = D_MODEL // P
NT = SEQ // P
NH, NKV, HD = 8, 2, 64
GQA = NH // NKV
NSAW = NH * HD
KVW = 2 * NKV * HD
NGATE = 3 * NH
SSMW = D_MODEL - NSAW
CUT_KV = NSAW
CUT_U = NSAW + 3 * KVW + NGATE
KVG = 3 * KVW + NGATE
PAST, PAGE, NPAGE = 2048, 128, 16
SUB = 16
NSUB = PAST // SUB
NSUBP = SEQ // SUB
NCMP = NSUB - 1
NSEL = PAST // 64 + 1
WIN = 512
G, PS, GC = 32, 64, 16
NJ = G // 2
CH = 8
NCH = SEQ // CH
DFF = 2816
NF = DFF // P
SCALE = HD ** -0.5
EPS = 1e-6
NEG = -1e30


class Net:
    pass


def bc(ap, axis, n):
    a = ap.unsqueeze(axis)
    shape = list(a.shape)
    shape[axis] = n
    return a.broadcast_to(shape)


def plan(nc, k):
    def at(name, shape, dtype, offset):
        size = 4 if dtype in (F32, I32, U32) else 2
        for d in shape[1:]:
            size *= d
        assert BASE + offset + size <= nc.sbuf_usable_end, (name, offset, size)
        return nc.alloc_sbuf_tensor_at(name, shape, dtype, offset=BASE + offset), (offset + size + 31) // 32 * 32
    BASE = 16512
    k.at = at
    k.ident, o = at("ident", [P, P], F32, 0)
    k.ones, o = at("ones", [P, P], F32, o)
    k.identb, o = at("identb", [P, P], BF16, o)
    k.mask_new, o = at("mask_new", [P, P], BF16, o)
    k.mask_old, o = at("mask_old", [P, P], BF16, o)
    k.mask_cmp, o = at("mask_cmp", [P, NT, 64], BF16, o)
    k.seen_cmp, o = at("seen_cmp", [P, 64], F32, o)
    k.vcol, o = at("vcol", [P, 32], F32, o)
    k.ccol, o = at("ccol", [P, 4, 2 * NF], F32, o)
    k.gates, o = at("gates", [P, NT + 1, NGATE], F32, o)
    k.rows_of, o = at("rows_of", [P, NB], U32, o)
    k.wsum, o = at("wsum", [P, 64], F32, o)
    assert o <= 9216, o
    k.xT, o = at("xT", [P, KD, TOK], F32, 9216)
    k.off_mix = o
    k.mixT, o = at("mixT", [P, KD, TOK], F32, o)
    k.off_u = o
    k.U, o = at("U", [P, G, CH, GC], F32, o)
    k.us, o = at("us", [NB, SSMW], F32, o)
    k.off_q = o
    k.qT, o = at("qT", [HD, NH, TOK], F32, o)
    k.off_kv = o
    k.kv, o = at("kv", [P, NT + 1, KVG], F32, o)
    k.off_tmp = o


def stage_load(nc, k):
    at = k.at
    k.xtok, o = at("xtok", [P, NT, D_MODEL], F32, k.off_q)
    k.xs, o = at("xs", [NB, D_MODEL], F32, k.off_kv)
    k.vrow, o = at("vrow", [32, P], F32, o)
    k.crow, o = at("crow", [2 * NF, 4, P], F32, o)
    x_loaded = [nc.alloc_semaphore(f"x_loaded{n}") for n in range(2)]
    vec_loaded = nc.alloc_semaphore("vec_loaded")
    const_made = nc.alloc_semaphore("const_made")
    xt_ready = nc.alloc_semaphore("xt_ready")
    xt_act = nc.alloc_semaphore("xt_act")
    xt_dve = nc.alloc_semaphore("xt_dve")
    vt_ready = nc.alloc_semaphore("vt_ready")
    with nc.Block() as block:
        @block.sync
        def _(sp):
            xv = k.dram["x_prompt"][0].rearrange("(t p) d -> p t d", p=P)
            for n in range(2):
                sp.dma_start(k.xtok[:, 4 * n:4 * n + 4], xv[:, 4 * n:4 * n + 4]).then_inc(x_loaded[n], 16)
            sp.dma_start(k.xs[:], k.dram["x_sample"].rearrange("b s d -> (b s) d")).then_inc(x_loaded[1], 16)

        @block.gpsimd
        def _(pool):
            pool.memset(k.ident[:], 0.0).then_inc(const_made, 1)
            pool.memset(k.ones[:], 1.0)
            pool.memset(k.mask_new[:], 0.0)
            pool.memset(k.mask_old[:], 0.0)
            pool.memset(k.mask_cmp[:], 0.0)
            pool.memset(k.identb[:], 0.0).then_inc(const_made, 1)
            pool.wait_ge(const_made, 2)
            for m in (k.ident, k.identb):
                pool.affine_select(out=m[:], in_=m[:], compare_op=ALU.not_equal, fill=1.0,
                                   base=0, pattern=[[-1, P]], channel_multiplier=1)
            pool.affine_select(out=k.mask_new[:], in_=k.mask_new[:], compare_op=ALU.is_ge, fill=NEG,
                               base=0, pattern=[[-1, P]], channel_multiplier=1)
            pool.affine_select(out=k.mask_old[:], in_=k.mask_old[:], compare_op=ALU.is_ge, fill=NEG,
                               base=0, pattern=[[1, P]], channel_multiplier=-1)
            pool.affine_select(out=k.mask_cmp[:], in_=k.mask_cmp[:], compare_op=ALU.is_ge, fill=NEG,
                               base=-31, pattern=[[P, NT], [-SUB, 64]], channel_multiplier=1)
            pool.affine_select(out=k.seen_cmp[:], in_=k.ones[:, 0:64], compare_op=ALU.is_ge, fill=0.0,
                               base=-31, pattern=[[-SUB, 64]], channel_multiplier=1).then_inc(const_made, 1)

        @block.scalar
        def _(act):
            for n, v in enumerate((k.dram["norm_mix"][0], k.dram["norm_ffn"][0], k.dram["norm_final"], k.dram["b_glu"][0])):
                act.dma_start(k.vrow[8 * n:8 * n + 8], v.rearrange("(a p) -> a p", p=P)).then_inc(vec_loaded, 16)
            for n in range(3):
                act.dma_start(k.crow[:, n], k.dram["conv_w"][0, n].rearrange("(a p) -> a p", p=P)).then_inc(vec_loaded, 16)
            act.dma_start(k.crow[:, 3], k.dram["conv_b"][0].rearrange("(a p) -> a p", p=P)).then_inc(vec_loaded, 16)
            for t in range(NT):
                act.wait_ge(xt_ready, 2 * t + 1)
                act.activation(k.xT[:, 0:4, t * P:t * P + P], k.ps[:, (2 * t) % 8, :].rearrange("p (a b) -> p a b", a=4),
                               ACT.Copy).then_inc(xt_act, 1)
            act.wait_ge(vt_ready, 1)
            act.activation(k.vcol[:], k.ps[:, 1, 0:32], ACT.Copy)
            act.activation(k.ccol[:], k.ps[:, 1, 32:32 + 8 * NF].rearrange("p (a b) -> p a b", a=4), ACT.Copy)

        @block.tensor
        def _(pe):
            pe.wait_ge(const_made, 3)
            for t in range(NT):
                if t % 4 == 0:
                    pe.wait_ge(x_loaded[t // 4], 16 if t == 0 else 32)
                for half in range(2):
                    if t >= 4:
                        pe.wait_ge(xt_act if half == 0 else xt_dve, t - 3)
                    for a in range(4):
                        mm = pe.transpose(k.ps[:, (2 * t + half) % 8, a * P:a * P + P],
                                          k.xtok[:, t, (4 * half + a) * P:(4 * half + a + 1) * P], k.ident[:])
                    mm.then_inc(xt_ready, 1)
            pe.wait_ge(xt_act, 5)
            for a in range(KD):
                mm = pe.transpose(k.ps[:, 0, a * NB:a * NB + NB], k.xs[:, a * P:a * P + P], k.ident[0:NB, 0:NB])
            mm.then_inc(xt_ready, 1)
            pe.wait_ge(vec_loaded, 8 * 16)
            pe.wait_ge(xt_dve, 5)
            pe.transpose(k.ps[:, 1, 0:32], k.vrow[:], k.ident[0:32, 0:32])
            for n in range(4):
                mm = pe.transpose(k.ps[:, 1, 32 + 2 * NF * n:32 + 2 * NF * (n + 1)], k.crow[:, n],
                                  k.ident[0:2 * NF, 0:2 * NF])
            mm.then_inc(vt_ready, 1)

        @block.vector
        def _(dve):
            for t in range(NT):
                dve.wait_ge(xt_ready, 2 * t + 2)
                dve.tensor_copy(k.xT[:, 4:8, t * P:t * P + P],
                                k.ps[:, (2 * t + 1) % 8, :].rearrange("p (a b) -> p a b", a=4)).then_inc(xt_dve, 1)
            dve.wait_ge(xt_ready, 2 * NT + 1)
            dve.tensor_copy(k.xT[:, :, SEQ:TOK], k.ps[:, 0, 0:KD * NB].rearrange("p (a b) -> p a b", a=KD))


def stage_norm(nc, k, tag, dst, gain, tmp):
    at = k.at
    sq, o = at(f"sq_{tag}", [P, 2, TOK], F32, tmp)
    rs, o = at(f"rstd_{tag}", [P, 2, TOK], F32, o)
    squared = nc.alloc_semaphore(f"squared_{tag}")
    summed = nc.alloc_semaphore(f"summed_{tag}")
    inverted = nc.alloc_semaphore(f"inverted_{tag}")
    rooted = nc.alloc_semaphore(f"rooted_{tag}")
    with nc.Block() as block:
        @block.scalar
        def _(act):
            for a in range(KD):
                if a >= 2:
                    act.wait_ge(summed, a - 1)
                act.activation(sq[:, a % 2], k.xT[:, a], ACT.Square).then_inc(squared, 1)
            act.wait_ge(inverted, 2)
            act.activation(rs[:, 0], rs[:, 1], ACT.Sqrt).then_inc(rooted, 1)

        @block.tensor
        def _(pe):
            for a in range(KD):
                pe.wait_ge(squared, a + 1)
                for c in range(3):
                    mm = pe.matmul(k.ps[:, c, 0:TG], k.ones[:], sq[:, a % 2, c * TG:c * TG + TG],
                                   start=(a == 0), stop=(a == KD - 1))
                mm.then_inc(summed, 1)

        @block.vector
        def _(dve):
            dve.wait_ge(summed, KD)
            dve.tensor_scalar(rs[:, 0].rearrange("p (c t) -> p c t", c=3), k.ps[:, 0:3, 0:TG],
                              1.0 / D_MODEL, EPS, ALU.mult, ALU.add).then_inc(inverted, 1)
            dve.wait_ge(inverted, 1)
            dve.reciprocal(rs[:, 1], rs[:, 0]).then_inc(inverted, 1)
            dve.wait_ge(rooted, 1)
            for a in range(KD):
                dve.scalar_tensor_tensor(dst[:, a], k.xT[:, a], k.vcol[:, gain + a:gain + a + 1], rs[:, 0],
                                         ALU.mult, ALU.mult)


def stage_project(nc, k):
    at = k.at
    hT = k.mixT
    k.w_kvg, o = at("w_kvg", [P, KD, KVG], F32, k.off_tmp)
    k.w_qu, o = at("w_qu", [P, KD, NSAW], F32, o)
    wv = k.dram["w_in"][0].rearrange("(k p) n -> p k n", p=P)
    w_q = nc.alloc_semaphore("w_q")
    w_kv = nc.alloc_semaphore("w_kv")
    w_u = nc.alloc_semaphore("w_u")
    projected = nc.alloc_semaphore("projected")
    left_act = nc.alloc_semaphore("left_act")
    left_dve = nc.alloc_semaphore("left_dve")
    rows_out = nc.alloc_semaphore("rows_out")
    cmp_out = nc.alloc_semaphore("cmp_out")
    k.cmp_rows_stored = (cmp_out, 16 * NT)
    k.stores.append(k.cmp_rows_stored)
    n_rows_out = [0]
    NQ = NSAW // P
    JOBS = [("q", b) for b in range(NQ)] + [("kv", t) for t in range(NT + 1)] + [("u", t) for t in range(CH + 1)]
    KVH = KVG // 2
    with nc.Block() as block:
        @block.sync
        def _(sp):
            sp.dma_start(k.w_qu[:], wv[:, :, 0:NSAW]).then_inc(w_q, 16)
            sp.dma_start(k.w_kvg[:], wv[:, :, CUT_KV:CUT_U]).then_inc(w_kv, 16)
            sp.wait_ge(projected, NQ)
            sp.dma_start(k.w_qu[:], wv[:, :, CUT_U:CUT_U + SSMW]).then_inc(w_u, 16)

            def rows_to(dst, src, stored=rows_out):
                n_rows_out[0] += 16 * (stored is rows_out)
                sp.dma_start(dst, src).then_inc(stored, 16)
            outs = [k.dram["p_kv_cmp"], k.dram["p_kv_sel"], k.dram["p_kv_win"]]
            for t in range(NT):
                sp.wait_ge(left_act, NQ + t + 1)
                sp.wait_ge(left_dve, NQ + t + 1)
                for n, out in enumerate(outs):
                    first = 0 if n < 2 else SEQ - WIN
                    if t * P >= first:
                        rows_to(out[0, 0, t * P - first:(t + 1) * P - first].rearrange("t a h d -> t (a h d)"),
                                k.kv[:, t, n * KVW:(n + 1) * KVW], cmp_out if n == 0 else rows_out)
            sp.wait_ge(left_act, NQ + NT + 1)
            sp.wait_ge(left_dve, NQ + NT + 1)
            for n, out in enumerate((k.dram["s_kv_cmp"], k.dram["s_kv_sel"], None)):
                dst = k.dram["s_kv_win"][0, :, WIN - 1] if out is None else out[0, :, 0]
                rows_to(dst.rearrange("b a h d -> b (a h d)"), k.kv[0:NB, NT, n * KVW:(n + 1) * KVW])
            rows_to(k.dram["s_kv_win"][0, :, 0:WIN - 1].rearrange("b t a h d -> b t (a h d)"),
                    k.dram["cache_kv_win"][0, :, 1:WIN].rearrange("b t a h d -> b t (a h d)"))

        @block.tensor
        def _(pe):
            for j, (kind, t) in enumerate(JOBS):
                bank = 4 * (j % 2)
                if j >= 2:
                    pe.wait_ge(left_act, j - 1)
                    pe.wait_ge(left_dve, j - 1)
                if t == 0:
                    pe.wait_ge({"q": w_q, "kv": w_kv, "u": w_u}[kind], 16)
                for a in range(KD):
                    on = dict(start=(a == 0), stop=(a == KD - 1))
                    if kind == "q":
                        for c in range(3):
                            mm = pe.matmul(k.ps[:, bank + c, 0:TG], k.w_qu[:, a, t * P:t * P + P],
                                           hT[:, a, c * TG:c * TG + TG], **on)
                    elif kind == "kv":
                        n = P if t < NT else NB
                        for c in range(2):
                            mm = pe.matmul(k.ps[0:n, bank + c, 0:KVH], hT[:, a, t * P:t * P + n],
                                           k.w_kvg[:, a, c * KVH:(c + 1) * KVH], **on)
                    else:
                        n = P if t < CH else NB
                        tokens = hT[:, a, t:SEQ:CH] if t < CH else hT[:, a, SEQ:TOK]
                        for c in range(2):
                            mm = pe.matmul(k.ps[0:n, bank + c, 0:256], tokens, k.w_qu[:, a, c * 256:c * 256 + 256], **on)
                mm.then_inc(projected, 1)

        def leave(eng, copy, half, left):
            for j, (kind, t) in enumerate(JOBS):
                bank = 4 * (j % 2)
                eng.wait_ge(projected, j + 1)
                if kind == "q":
                    ins = copy(k.qT[:, 2 * t + half].rearrange("p (c t) -> p c t", c=3),
                               k.ps[HD * half:HD * half + HD, bank:bank + 3, 0:TG])
                elif kind == "kv":
                    n = P if t < NT else NB
                    ins = copy(k.kv[0:n, t, half * KVH:(half + 1) * KVH], k.ps[0:n, bank + half, 0:KVH])
                else:
                    s = slice(half * SSMW // 2, (half + 1) * SSMW // 2)
                    src = k.ps[0:(P if t < CH else NB), bank + half, 0:256]
                    if t < CH:
                        ins = copy(k.U[:, half * G // 2:(half + 1) * G // 2, CH - 1 - t, :],
                                   src.rearrange("p (g c) -> p g c", c=GC))
                    else:
                        ins = copy(k.us[:, s], src)
                ins.then_inc(left, 1)

        @block.scalar
        def _(act):
            leave(act, lambda o, i: act.activation(o, i, ACT.Copy), 0, left_act)

        @block.vector
        def _(dve):
            leave(dve, dve.tensor_copy, 1, left_dve)
    k.stores.append((rows_out, n_rows_out[0]))


class Link:

    def __init__(self, nc, eng, name):
        self.eng, self.sem, self.count = eng, nc.alloc_semaphore(name), 0

    def __call__(self, ins):
        self.count += 1
        ins.then_inc(self.sem, 1)
        self.eng.wait_ge(self.sem, self.count)


def stage_compress(nc, k):
    at = k.at
    k.tile, _ = at("tile", [P, 2, SUB, 2 * NKV, HD], F32, k.off_mix)
    k.kcs, o = at("kcs", [P, 2, NB, NSUB], F32, k.off_tmp)
    k.kcp, o = at("kcp", [HD, 2 * NKV, 2, NSUBP], F32, o)
    k.cbias, o = at("cbias", [HD, 2], F32, o)
    k.off_att = o
    k.w_c, o = at("w_c", [P, 2, SUB // 2, 2, HD], F32, o)
    k.rowsT, o = at("rowsT", [P, 4, NKV, 2, P], F32, o)
    k.late, o = at("late", [HD, 2, NKV, 2, P], F32, o)
    k.page_of, o = at("page_of", [P, NB], I32, o)
    k.lane, o = at("lane", [P, 1], I32, o)
    k.lanef, o = at("lanef", [P, 1], F32, o)
    NP_ROWS = NSUBP + 2
    wc_loaded = nc.alloc_semaphore("wc_loaded")
    pages_loaded = nc.alloc_semaphore("pages_loaded")
    lane_made = nc.alloc_semaphore("lane_made")
    rows_known = nc.alloc_semaphore("rows_known")
    prompt_in = nc.alloc_semaphore("prompt_in")
    tile_in = [nc.alloc_semaphore(f"tile_in{n}") for n in range(2)]
    transposed = nc.alloc_semaphore("c_transposed")
    moved_act = nc.alloc_semaphore("c_moved_act")
    moved_dve = nc.alloc_semaphore("c_moved_dve")
    multiplied = nc.alloc_semaphore("c_multiplied")
    shifted = nc.alloc_semaphore("c_shifted")
    combined = nc.alloc_semaphore("c_combined")
    FILLS = 8
    width = {0: NP_ROWS}
    with nc.Block() as block:
        @block.sync
        def _(sp):
            wv = k.dram["w_cmp"][0]
            for s2 in range(2):
                for x in range(2):
                    for r in range(2):
                        src = wv[x, r * SUB + s2:(r + 1) * SUB:2].rearrange("s d e -> d s e")
                        sp.dma_start(k.w_c[HD * s2:HD * s2 + HD, x, :, r, :], src).then_inc(wc_loaded, 16)
            for x in range(2):
                for h in range(NKV):
                    sp.dma_start(k.tile[NSUBP:NP_ROWS, 0, :, 2 * x + h, :],
                                 k.dram["pe_cmp"][0, x].rearrange("(r s) d -> r s d", r=2)).then_inc(prompt_in, 16)
            sp.wait_ge(*k.cmp_rows_stored)
            sp.dma_start(k.tile[0:NSUBP, 0].rearrange("n s c d -> n (s c d)"),
                         k.dram["p_kv_cmp"][0, 0].rearrange("(n s) x h d -> n (s x h d)", s=SUB)).then_inc(prompt_in, 16)
            for g in range(NPAGE):
                sp.dma_start(k.page_of[8 * g:8 * g + 8, :], k.dram["page_table"][:, g:g + 1].rearrange("b o -> o b").broadcast_to([8, NB]),
                             allow_slow_non_contiguous=True
                             ).then_inc(pages_loaded, 16)

        @block.gpsimd
        def _(pool):
            pool.iota(k.lane[:], pattern=[[0, 1]], base=0, channel_multiplier=1).then_inc(lane_made, 1)
            pool.wait_ge(rows_known, 1)
            rows = k.dram["cache_kv_cmp"][0].rearrange("n (r s) x h d -> (n r) (s x h d)", s=SUB)
            for b in range(NB):
                j = b + 1
                if j >= 2:
                    pool.wait_ge(transposed, FILLS * (j - 1))
                pool.indirect_dma_start(k.tile[:, j % 2].rearrange("n s c d -> n (s c d)"), None, rows,
                                        bass.IndirectOffsetOnAxis(ap=k.rows_of[:, b:b + 1], axis=0)
                                        ).then_inc(tile_in[j % 2], 16)

        @block.tensor
        def _(pe):
            def turn(j, f, n):
                x, quad = f // 4, f % 4
                for a in range(4):
                    mm = pe.transpose(k.ps[:, f % 4, a * P:a * P + n],
                                      k.tile[0:n, j % 2, 4 * quad + a, 2 * x:2 * x + 2, :].rearrange("n h d -> n (h d)"),
                                      k.ident[0:n, 0:n])
                mm.then_inc(transposed, 1)

            def multiply(j, f, n):
                x, quad = f // 4, f % 4
                for h in range(NKV):
                    for a in range(2):
                        mm = pe.matmul(k.ps[:, 4 + 2 * (j % 2) + h, x * P:x * P + n],
                                       k.w_c[:, x, 2 * quad + a].rearrange("p r e -> p (r e)"),
                                       k.rowsT[:, f % 4, h, a, 0:n], start=(quad == 0 and a == 0), stop=(quad == 3 and a == 1))
                mm.then_inc(multiplied, 1)
            pe.wait_ge(wc_loaded, 8 * 16)
            for j in range(NB + 1):
                n = width.get(j, P)
                if j == 0:
                    pe.wait_ge(prompt_in, 5 * 16)
                else:
                    pe.wait_ge(tile_in[j % 2], 16 * ((j + 1) // 2))
                for f in range(FILLS + 2):
                    F = FILLS * j + f
                    if f < FILLS:
                        if F >= 4:
                            pe.wait_ge(moved_act, F - 3)
                            pe.wait_ge(moved_dve, F - 3)
                        turn(j, f, n)
                    if f >= 2:
                        if f == 2 and j >= 2:
                            pe.wait_ge(combined, j - 1)
                        pe.wait_ge(moved_act, F - 1)
                        pe.wait_ge(moved_dve, F - 1)
                        multiply(j, f - 2, n)

        def move(eng, copy, h, moved, finish):
            for j in range(NB + 1):
                n = width.get(j, P)
                for f in range(FILLS):
                    F = FILLS * j + f
                    eng.wait_ge(transposed, F + 1)
                    if F >= 4:
                        eng.wait_ge(multiplied, F - 3)
                    rows = k.ps[HD * h:HD * h + HD, f % 4, :].rearrange("p (a s n) -> p s a n", a=2, s=2)
                    for s2 in range(2):
                        ins = copy(k.rowsT[HD * s2:HD * s2 + HD, f % 4, h, :, 0:n], rows[:, s2, :, 0:n])
                    ins.then_inc(moved, 1)
                finish(j, n)

        @block.scalar
        def _(act):
            def shift(j, n):
                act.wait_ge(multiplied, FILLS * (j + 1))
                if j >= 2:
                    act.wait_ge(combined, j - 1)
                act.activation(k.late[:, j % 2, :, :, 0:n],
                               k.ps[HD:P, 4 + 2 * (j % 2):6 + 2 * (j % 2), 0:2 * P].rearrange("p h (x n) -> p h x n", x=2)[:, :, :, 0:n],
                               ACT.Copy).then_inc(shifted, 1)
            move(act, lambda o, i: act.activation(o, i, ACT.Copy), 0, moved_act, shift)

        @block.vector
        def _(dve):
            link = Link(nc, dve, "c_link")
            dve.memset(k.kcp[:], 0.0)
            dve.wait_ge(lane_made, 1)
            link(dve.tensor_scalar(k.lane[:], k.lane[:], 7, None, ALU.bitwise_and))
            link(dve.tensor_copy(k.lanef[:], k.lane[:]))
            dve.wait_ge(pages_loaded, 16 * NPAGE)
            dve.tensor_scalar(k.rows_of[:], k.page_of[:], float(PAGE // SUB), k.lanef[:], ALU.mult, ALU.add
                              ).then_inc(rows_known, 1)

            def combine(j, n):
                dve.wait_ge(shifted, j + 1)
                if j == 0:
                    link(dve.tensor_tensor(k.cbias[:], k.ps[0:HD, 4, NSUBP:2 * P:P], k.late[:, 0, 0, :, NSUBP + 1], ALU.add))
                    n = NSUBP
                for c in range(4):
                    x, h = c // 2, c % 2
                    first = k.ps[0:HD, 4 + 2 * (j % 2) + h, x * P:x * P + n - 1]
                    last = k.late[:, j % 2, h, x, 1:n]
                    if j == 0:
                        for copy in range(2):
                            ins = dve.scalar_tensor_tensor(k.kcp[:, c, copy, 0:n - 1], first, k.cbias[:, x:x + 1], last,
                                                           ALU.add, ALU.add)
                    else:
                        ins = dve.scalar_tensor_tensor(k.kcs[HD * h:HD * h + HD, x, j - 1, 0:n - 1], first,
                                                       k.cbias[:, x:x + 1], last, ALU.add, ALU.add)
                ins.then_inc(combined, 1)
            move(dve, dve.tensor_copy, 1, moved_dve, combine)


def stage_prompt_compressed(nc, k):
    at = k.at
    k.oacc, _ = at("oacc", [P, NT, NSAW], F32, k.off_mix + 4 * TOK * 4)
    k.vcp, o = at("vcp", [P, NKV, HD], F32, k.off_att)
    k.sc, o = at("sc", [P, 2, NH, 64], F32, o)
    k.pc, o = at("pc", [P, 2, NH, 64], F32, o)
    k.pcT, o = at("pcT", [P, 2, 4, P], F32, o)
    k.st, o = at("st", [P, NT, 4, NH], F32, o)
    k.glog, o = at("glog", [P, NT + 1, NGATE], F32, o)
    scored = nc.alloc_semaphore("pc_scored")
    less_max = nc.alloc_semaphore("pc_less_max")
    powered = nc.alloc_semaphore("pc_powered")
    weighed = nc.alloc_semaphore("pc_weighed")
    turned = nc.alloc_semaphore("pc_turned")
    turned_out = nc.alloc_semaphore("pc_turned_out")
    valued = nc.alloc_semaphore("pc_valued")
    kept = nc.alloc_semaphore("pc_kept")
    gated = nc.alloc_semaphore("gated")
    v_turned = nc.alloc_semaphore("pc_v_turned")
    with nc.Block() as block:
        @block.tensor
        def _(pe):
            for kvh in range(NKV):
                mm = pe.transpose(k.ps[:, 6, kvh * HD:kvh * HD + HD],
                                  k.kcp[:, NKV + kvh].rearrange("d c n -> d (c n)"), k.ident[0:HD, 0:HD])
            mm.then_inc(v_turned, 1)

            def scores(i):
                if i >= 2:
                    pe.wait_ge(less_max, i - 1)
                bank = i % 2
                for h in range(NH):
                    pe.matmul(k.ps[:, bank, h * 64:h * 64 + 64], k.identb[:], k.mask_cmp[:, i, :], start=True, stop=False)
                    mm = pe.matmul(k.ps[:, bank, h * 64:h * 64 + 64], k.qT[:, h, i * P:i * P + P],
                                   k.kcp[:, h // GQA, 0, :], start=False, stop=True)
                mm.then_inc(scored, 1)

            def values(i):
                pe.wait_ge(weighed, i + 1)
                if i >= 2:
                    pe.wait_ge(turned_out, i - 1)
                for a in range(4):
                    mm = pe.transpose(k.ps[:, 2 + i % 2, a * P:a * P + P],
                                      k.pc[:, i % 2, 2 * a:2 * a + 2, :].rearrange("p h n -> p (h n)"), k.ident[:])
                mm.then_inc(turned, 1)
                pe.wait_ge(turned_out, i + 1)
                if i >= 2:
                    pe.wait_ge(kept, i - 1)
                if i == 0:
                    pe.wait_ge(v_turned, 2)
                for h in range(NH):
                    half = slice(64 * (h % 2), 64 * (h % 2) + 64)
                    mm = pe.matmul(k.ps[:, 4 + 2 * (i % 2) + h % 2, h // 2 * HD:h // 2 * HD + HD], k.pcT[half, i % 2, h // 2, :],
                                   k.vcp[half, h // GQA, :], start=True, stop=True)
                mm.then_inc(valued, 1)
            scores(0)
            for i in range(NT):
                if i + 1 < NT:
                    scores(i + 1)
                values(i)

        @block.scalar
        def _(act):
            def keep(i):
                bank = 4 + 2 * (i % 2)
                act.activation(k.oacc[:, i].rearrange("p (a b d) -> p a b d", a=4, b=2),
                               k.ps[:, bank:bank + 2, 0:4 * HD].rearrange("p b (a d) -> p a b d", a=4),
                               ACT.Copy).then_inc(kept, 1)
            act.wait_ge(v_turned, 1)
            act.activation(k.vcp[:], k.ps[:, 6, 0:P].rearrange("p (h d) -> p h d", h=NKV), ACT.Copy).then_inc(v_turned, 1)
            act.activation(k.glog[:, 0:NT], k.kv[:, 0:NT, 3 * KVW:], ACT.Exp, scale=-1.0)
            act.activation(k.glog[0:NB, NT], k.kv[0:NB, NT, 3 * KVW:], ACT.Exp, scale=-1.0).then_inc(gated, 1)
            for i in range(NT):
                act.wait_ge(less_max, i + 1)
                if i >= 2:
                    act.wait_ge(turned, i - 1)
                act.activation(k.pc[:, i % 2], k.sc[:, i % 2], ACT.Exp, scale=SCALE).then_inc(powered, 1)
                if i >= 1:
                    act.wait_ge(valued, i)
                    keep(i - 1)
            act.wait_ge(valued, NT)
            keep(NT - 1)

        @block.vector
        def _(dve):
            link = Link(nc, dve, "pc_link")
            dve.wait_ge(gated, 1)
            link(dve.tensor_scalar(k.glog[:, 0:NT], k.glog[:, 0:NT], 1.0, None, ALU.add))
            link(dve.tensor_scalar(k.glog[0:NB, NT], k.glog[0:NB, NT], 1.0, None, ALU.add))
            dve.reciprocal(k.gates[:, 0:NT], k.glog[:, 0:NT])
            link(dve.reciprocal(k.gates[0:NB, NT], k.glog[0:NB, NT]))

            def less(i):
                dve.wait_ge(scored, i + 1)
                s = k.ps[:, i % 2, :].rearrange("p (h n) -> p h n", h=NH)
                link(dve.tensor_reduce(k.st[:, i, 0], s, AX.X, ALU.max))
                if i >= 2:
                    dve.wait_ge(powered, i - 1)
                dve.tensor_tensor(k.sc[:, i % 2], s, bc(k.st[:, i, 0], 2, 64), ALU.subtract).then_inc(less_max, 1)

            def weigh(i):
                dve.wait_ge(powered, i + 1)
                p = k.pc[:, i % 2]
                if i == 0:
                    link(dve.tensor_tensor(p, p, bc(k.seen_cmp[:], 1, NH), ALU.mult))
                link(dve.tensor_reduce(k.st[:, i, 1], p, AX.X, ALU.add))
                link(dve.tensor_scalar(k.st[:, i, 2], k.st[:, i, 1], 1e-30, None, ALU.max))
                link(dve.reciprocal(k.st[:, i, 3], k.st[:, i, 2]))
                link(dve.tensor_tensor(k.st[:, i, 1], k.st[:, i, 3], k.gates[:, i, 0::3], ALU.mult))
                dve.tensor_tensor(p, p, bc(k.st[:, i, 1], 2, 64), ALU.mult).then_inc(weighed, 1)

            def turn_out(i):
                dve.wait_ge(turned, i + 1)
                if i >= 2:
                    dve.wait_ge(valued, i - 1)
                dve.tensor_copy(k.pcT[:, i % 2], k.ps[:, 2 + i % 2, :].rearrange("p (a q) -> p a q", a=4)).then_inc(turned_out, 1)
            less(0)
            for i in range(NT):
                if i + 1 < NT:
                    less(i + 1)
                weigh(i)
                turn_out(i)


def stage_attend(nc, k):
    at = k.at
    k.kT, o = at("kT", [HD, 2, NKV, SEQ], F32, k.off_att)
    k.q_now, o = at("q_now", [HD, 2, P], F32, o)
    k.prob, o = at("prob", [P, 2, SEQ], F32, o)
    k.probT, o = at("probT", [P, 4, 4, P], F32, o)
    k.ast, o = at("ast", [P, 2, 2, 4], F32, o)
    k_turned = nc.alloc_semaphore("k_turned")
    k_act = nc.alloc_semaphore("k_act")
    k_dve = nc.alloc_semaphore("k_dve")
    staged = nc.alloc_semaphore("q_staged")
    scored = nc.alloc_semaphore("a_scored")
    maxed = nc.alloc_semaphore("a_maxed")
    powered = nc.alloc_semaphore("a_powered")
    turned = nc.alloc_semaphore("a_turned")
    out_act = nc.alloc_semaphore("a_out_act")
    out_dve = nc.alloc_semaphore("a_out_dve")
    valued = nc.alloc_semaphore("a_valued")
    added = nc.alloc_semaphore("a_added")
    SEL0, WIN0, T0, O0 = 0, 2, 4, 6

    def jobs_of(i):
        blocks = [list(range(i + 1)), list(range(max(0, i - WIN // P), i + 1))]
        return blocks, [(br, bl[c:c + 4]) for br, bl in enumerate(blocks) for c in range(0, len(bl), 4)]
    JOBS = [jobs_of(i)[1] for i in range(NT)]

    def runs(i, br, bl):
        masks = {i: k.mask_new}
        if br == 1:
            masks[i - WIN // P] = k.mask_old
        out = []
        for b in bl:
            if b in masks:
                out.append((b, 1, masks[b]))
            elif out and out[-1][2] is None:
                out[-1] = (out[-1][0], out[-1][1] + 1, None)
            else:
                out.append((b, 1, None))
        return out
    before = [NH * sum(len(j) for j in JOBS[:i]) for i in range(NT)]
    before_dve = [NH * sum((len(j) + 1) // 2 for j in JOBS[:i]) for i in range(NT)]
    before_act = [NH * sum(len(j) // 2 for j in JOBS[:i]) for i in range(NT)]

    def heads(eng, body):
        for i in range(NT):
            with eng.Fori(0, NKV) as kvh:
                with eng.Fori(0, GQA) as g:
                    h = kvh * GQA + g
                    body(i, h, kvh)

    with nc.Block() as block:
        @block.tensor
        def _(pe):
            for c in range(4):
                src = KVW * (1 + c // 2)
                for a in range(4):
                    t = 4 * (c % 2) + a
                    mm = pe.transpose(k.ps[:, c, a * P:a * P + P], k.kv[:, t, src:src + P], k.ident[:])
                mm.then_inc(k_turned, 1)
            pe.wait_ge(k_act, 4)
            pe.wait_ge(k_dve, 4)
            pe.sem_inc(scored, 1)

            def body(i, h, kvh):
                blocks, jobs = jobs_of(i)
                nj = len(jobs)
                pe.wait_ge(staged, h + (NH * i + 1))
                for br, base in ((0, SEL0), (1, WIN0)):
                    bl = blocks[br]
                    pe.wait_ge(powered, 2 * h + (2 * NH * i + 1 + br))
                    for c in range(0, len(bl), 4):
                        for b0, nb, mask in runs(i, br, bl[c:c + 4]):
                            out = k.ps[:, base + c // 4, (b0 - bl[c]) * P:(b0 - bl[c] + nb) * P]
                            mm = pe.matmul(out, k.q_now[:, 0, :], k.kT[:, br, kvh, b0 * P:(b0 + nb) * P],
                                           start=True, stop=mask is None)
                            if mask is not None:
                                mm = pe.matmul(out, k.identb[:], mask[:], start=False, stop=True)
                    mm.then_inc(scored, 1)
                for x, (br, bl) in enumerate(jobs):
                    first = x == 0 or jobs[x - 1][0] != br
                    last = x == nj - 1 or jobs[x + 1][0] != br
                    if first:
                        pe.wait_ge(powered, 2 * h + (2 * NH * i + 3 + br))
                    nd, na = (nj + 1) // 2, nj // 2
                    if x % 2 == 0:
                        val, per = before_dve[i] + x // 2, nd
                        sem = out_dve
                    else:
                        val, per = before_act[i] + x // 2, na
                        sem = out_act
                    pe.wait_ge(sem, h * per + (val + 1))
                    for a, b in enumerate(bl):
                        o = (b - blocks[br][0]) * P
                        mm = pe.transpose(k.ps[:, T0 + x % 2, a * P:a * P + P], k.prob[:, br, o:o + P], k.ident[:])
                    mm.then_inc(turned, 1)
                    pe.wait_ge(sem, h * per + (val + 2))
                    if first:
                        pe.wait_ge(added, 2 * h + (2 * NH * i + 1 + br))
                    for a, b in enumerate(bl):
                        v = KVW * (1 + br) + P
                        mm = pe.matmul(k.ps[:, O0 + br, 0:HD], k.probT[:, x, a, :],
                                       k.kv[:, b, bass.ds(kvh * HD + v, HD)],
                                       start=(first and a == 0), stop=(last and a == len(bl) - 1))
                    if last:
                        mm.then_inc(valued, 1)
            heads(pe, body)

        @block.gpsimd
        def _(pool):
            def body(i, h, kvh):
                pool.wait_ge(scored, 2 * h + (2 * NH * i + 1))
                pool.tensor_copy(k.q_now[:, 0, :], k.qT[:, bass.ds(h, 1), i * P:i * P + P].rearrange("p a q -> p (a q)")
                                 ).then_inc(staged, 1)
            heads(pool, body)

        @block.scalar
        def _(act):
            for c in range(4):
                act.wait_ge(k_turned, c + 1)
                act.activation(k.kT[:, c // 2, 0, 4 * P * (c % 2):4 * P * (c % 2 + 1)], k.ps[0:HD, c, :], ACT.Copy).then_inc(k_act, 1)
            act.sem_inc(out_act, 1)
            act.sem_inc(powered, 2)

            def body(i, h, kvh):
                blocks, jobs = jobs_of(i)
                for br, base in ((0, SEL0), (1, WIN0)):
                    n = len(blocks[br]) * P
                    act.wait_ge(maxed, 2 * h + (2 * NH * i + 1 + br))
                    act.activation(k.prob[:, br, 0:n], k.ps[:, base:base + 2, :].rearrange("p a n -> p (a n)")[:, 0:n],
                                   ACT.Exp, bias=k.ast[:, br, 0, 1:2], scale=SCALE,
                                   accum_out=k.ast[:, br, 0, 2:3]).then_inc(powered, 1)
                for x in range(1, len(jobs), 2):
                    br, bl = jobs[x]
                    act.wait_ge(turned, h * len(jobs) + (before[i] + x + 1))
                    n = len(bl)
                    act.activation(k.probT[:, x, 0:n, :], k.ps[:, T0 + 1, 0:n * P].rearrange("p (a q) -> p a q", a=n),
                                   ACT.Copy).then_inc(out_act, 1)
            heads(act, body)

        @block.vector
        def _(dve):
            for c in range(4):
                dve.wait_ge(k_turned, c + 1)
                dve.tensor_copy(k.kT[:, c // 2, 1, 4 * P * (c % 2):4 * P * (c % 2 + 1)], k.ps[HD:P, c, :]).then_inc(k_dve, 1)
            own = nc.alloc_semaphore("a_own")
            dve.sem_inc(out_dve, 1)
            dve.sem_inc(added, 2)

            def body(i, h, kvh):
                blocks, jobs = jobs_of(i)
                steps = 6
                done = 0
                def link(ins):
                    nonlocal done
                    done += 1
                    ins.then_inc(own, 1)
                    dve.wait_ge(own, h * steps + (steps * NH * i + done))
                for br, base in ((0, SEL0), (1, WIN0)):
                    n = len(blocks[br]) * P
                    dve.wait_ge(scored, 2 * h + (2 * NH * i + 2 + br))
                    link(dve.tensor_reduce(k.ast[:, br, 0, 0:1], k.ps[:, base:base + 2, :].rearrange("p a n -> p (a n)")[:, 0:n],
                                           AX.X, ALU.max))
                    dve.tensor_scalar(k.ast[:, br, 0, 1:2], k.ast[:, br, 0, 0:1], -SCALE, None, ALU.mult).then_inc(maxed, 1)
                for x in range(0, len(jobs), 2):
                    br, bl = jobs[x]
                    dve.wait_ge(turned, h * len(jobs) + (before[i] + x + 1))
                    n = len(bl)
                    dve.tensor_copy(k.probT[:, x, 0:n, :], k.ps[:, T0, 0:n * P].rearrange("p (a q) -> p a q", a=n)).then_inc(out_dve, 1)
                for br in range(2):
                    dve.wait_ge(powered, 2 * h + (2 * NH * i + 3 + br))
                    link(dve.reciprocal(k.ast[:, br, 0, 3:4], k.ast[:, br, 0, 2:3]))
                    link(dve.tensor_tensor(k.ast[:, br, 1, 0:1], k.ast[:, br, 0, 3:4], k.gates[:, i, bass.ds(h * 3 + (1 + br), 1)], ALU.mult))
                    dve.wait_ge(valued, 2 * h + (2 * NH * i + 1 + br))
                    if br == 1:
                        dve.wait_ge(added, 2 * h + (2 * NH * i + 3))
                    acc = k.oacc[:, i, bass.ds(h * HD, HD)]
                    dve.scalar_tensor_tensor(acc, k.ps[:, O0 + br, 0:HD], k.ast[:, br, 1, 0:1], acc, ALU.mult, ALU.add
                                             ).then_inc(added, 1)
            heads(dve, body)


def stage_turn_attention(nc, k):
    turned = nc.alloc_semaphore("t_turned")
    kept_act = nc.alloc_semaphore("t_kept_act")
    kept_dve = nc.alloc_semaphore("t_kept_dve")
    with nc.Block() as block:
        @block.tensor
        def _(pe):
            for i in range(NT):
                for a in range(4):
                    mm = pe.transpose(k.ps[:, i, a * P:a * P + P], k.oacc[:, i, a * P:a * P + P], k.ident[:])
                mm.then_inc(turned, 1)

        @block.scalar
        def _(act):
            for i in range(0, NT, 2):
                act.wait_ge(turned, i + 1)
                act.activation(k.mixT[:, 0:4, i * P:i * P + P], k.ps[:, i, :].rearrange("p (a q) -> p a q", a=4), ACT.Copy)

        @block.vector
        def _(dve):
            for i in range(1, NT, 2):
                dve.wait_ge(turned, i + 1)
                dve.tensor_copy(k.mixT[:, 0:4, i * P:i * P + P], k.ps[:, i, :].rearrange("p (a q) -> p a q", a=4))


class Steps:

    def __init__(self, nc, name, steps):
        self.sem, self.steps, self.base = nc.alloc_semaphore(name), steps, 0

    def mark(self, ins, step):
        ins.then_inc(self.sem, 1)

    def wait(self, eng, step):
        eng.wait_ge(self.sem, self.base + self.steps.index(step) + 1)

    def again(self):
        self.base += len(self.steps)


NH2 = NB // 2
R = NH2 * NH
SLOTS = SUB + WIN // P


def stage_sample_prepare(nc, k):
    at = k.at
    o = k.off_q + 33024 + NT * KVG * 4
    k.off_s1 = k.off_q + 0
    o = (k.off_att + 31) // 32 * 32
    k.qsm, o = at("qsm", [P, NB, NH], F32, o)
    k.knT, o = at("knT", [P, 2, NB], F32, o)
    k.diag, o = at("diag", [R, 2, NB], F32, o)
    k.smap, o = at("smap", [P, NSEL], F32, o)
    k.grow, o = at("grow", [R, 2, 3], F32, o)
    k.off_s2 = o
    made = nc.alloc_semaphore("s_made")
    grow_in = nc.alloc_semaphore("grow_in")
    kn_turned = nc.alloc_semaphore("kn_turned")
    zeroed = nc.alloc_semaphore("qsm_zeroed")
    with nc.Block() as block:
        @block.sync
        def _(sp):
            for b in range(NB):
                for h in range(NH):
                    r = NH * (b % NH2) + h
                    sp.dma_start(k.grow[r:r + 1, b // NH2, :], k.gates[b:b + 1, NT, 3 * h:3 * h + 3]).then_inc(grow_in, 16)
            sp.wait_ge(grow_in, 16 * NB * NH)

        @block.gpsimd
        def _(pool):
            pool.memset(k.smap[:], 1.0)
            pool.memset(k.diag[:], 1.0).then_inc(made, 1)
            pool.wait_ge(made, 1)
            pool.affine_select(out=k.smap[:], in_=k.smap[:], compare_op=ALU.is_ge, fill=0.0, base=63,
                               pattern=[[64, NSEL]], channel_multiplier=-SUB)
            pool.affine_select(out=k.diag[:], in_=k.diag[:], compare_op=ALU.is_ge, fill=0.0, base=0,
                               pattern=[[NH * NH2, 2], [-NH, NB]], channel_multiplier=1).then_inc(made, 1)
            pool.wait_ge(made, 2)
            pool.affine_select(out=k.smap[:], in_=k.smap[:], compare_op=ALU.is_ge, fill=0.0, base=31,
                               pattern=[[-64, NSEL]], channel_multiplier=SUB)
            pool.affine_select(out=k.diag[:], in_=k.diag[:], compare_op=ALU.is_ge, fill=0.0, base=NH - 1,
                               pattern=[[-NH * NH2, 2], [NH, NB]], channel_multiplier=-1)

        @block.tensor
        def _(pe):
            for br in range(2):
                mm = pe.transpose(k.ps[:, 0, br * NB:br * NB + NB], k.kv[0:NB, NT, KVW * (1 + br):KVW * (1 + br) + P],
                                  k.ident[0:NB, 0:NB])
            mm.then_inc(kn_turned, 1)

        @block.vector
        def _(dve):
            dve.memset(k.qsm[:], 0.0).then_inc(zeroed, 1)
            dve.wait_ge(zeroed, 1)
            for kvh in range(NKV):
                hs = slice(kvh * GQA, (kvh + 1) * GQA)
                dve.tensor_copy(k.qsm[HD * kvh:HD * kvh + HD, :, hs], k.qT[:, hs, SEQ:TOK].rearrange("d h b -> d b h"))
            dve.wait_ge(kn_turned, 1)
            dve.tensor_copy(k.knT[:].rearrange("p a b -> p (a b)"), k.ps[:, 0, 0:2 * NB])


def stage_sample_attention(nc, k):
    at = k.at
    k.vrows, o = at("vrows", [P, NH2, SUB, P], F32, k.off_q)
    k.stile0, o = at("stile0", [P, SUB, 2 * P], F32, o)
    assert o <= k.off_kv + NT * KVG * 4, o
    k.stile1, o = at("stile1", [P, SUB, 2 * P], F32, k.off_s2)
    k.wrows, o = at("wrows", [P, NH2, WIN // P, 2 * P], F32, o)
    k.sT, o = at("sT", [P, SLOTS, R], F32, o)
    k.scT, o = at("scT", [P, R], F32, o)
    k.pcs, o = at("pcs", [R, 2, P], F32, o)
    k.pcsT, o = at("pcsT", [P, 3, R], F32, o)
    k.dT, o = at("dT", [NB, 2, R], F32, o)
    k.imp, o = at("imp", [R, 4, 40], F32, o)
    k.m8, o = at("m8", [R, 2, 8], F32, o)
    k.ss, o = at("ss", [R, 3, 8], F32, o)
    k.sd, o = at("sd", [R, 4, NB], F32, o)
    k.sbuf, _ = at("sbuf", [R, PAST + 32], F32, k.off_mix + 4 * TOK * 4)
    k.keyT, _ = at("keyT", [P, 4, 4, P], F32, k.off_mix + 4 * TOK * 4 + (PAST + 32) * 4)
    k.wbuf, o = at("wbuf", [R, WIN + 32], F32, o)
    k.vcs, o = at("vcs", [P, NH2, P], F32, o)
    k.pT = k.sT
    tiles = [k.stile0, k.stile1]
    t_in = [nc.alloc_semaphore(f"s_tile_in{n}") for n in range(2)]
    w_in = nc.alloc_semaphore("s_win_in")
    turned = nc.alloc_semaphore("s_turned")
    moved_act = nc.alloc_semaphore("s_moved_act")
    moved_dve = nc.alloc_semaphore("s_moved_dve")
    scored = nc.alloc_semaphore("s_scored")
    taken = nc.alloc_semaphore("s_taken")
    v_kept = nc.alloc_semaphore("s_v_kept")
    vt = nc.alloc_semaphore("s_mix")
    FILLS = SLOTS // 4
    tensor = Steps(nc, "s_pe", ["cmp scores", "new scores", "cmp rows", "probT", "importance", "rows", "vc", "probabilities", "values"])
    vector = Steps(nc, "s_dve", ["cmp kept", "cmp max", "cmp p", "probT kept", "heads summed", "sel max", "win max",
                                 "sel p", "win p", "pT kept", "vc kept", "done"])
    scalar = Steps(nc, "s_act", ["cmp exp", "sel exp", "win exp"])
    own = nc.alloc_semaphore("s_link")

    with nc.Block() as block:
        @block.sync
        def _(sp):
            for n in range(2):
                if n:
                    sp.wait_ge(vt, n)
                sp.dma_start(k.wrows[:].rearrange("p b s c -> p b (s c)"),
                             k.dram["cache_kv_win"][0, NH2 * n:NH2 * n + NH2].rearrange("b (p s) x h d -> p b (s x h d)", p=P)
                             ).then_inc(w_in, 16)

        @block.gpsimd
        def _(pool):
            rows = k.dram["cache_kv_sel"][0].rearrange("n (r s) x h d -> (n r) (s x h d)", s=SUB)

            def gather(b):
                if b >= 2:
                    pool.wait_ge(turned, FILLS * (b - 1))
                pool.indirect_dma_start(tiles[b % 2][:].rearrange("p s c -> p (s c)"), None, rows,
                                        bass.IndirectOffsetOnAxis(ap=k.rows_of[:, b:b + 1], axis=0)
                                        ).then_inc(t_in[b % 2], 16)
            gather(0)
            for b in range(NB):
                if b + 1 < NB:
                    if b >= 1:
                        pool.wait_ge(v_kept, b)
                    gather(b + 1)
                pool.wait_ge(t_in[b % 2], 16 * (b // 2 + 1))
                if b == NH2:
                    pool.wait_ge(vt, 1)
                pool.tensor_copy(k.vrows[:, b % NH2], tiles[b % 2][:, :, P:2 * P]).then_inc(v_kept, 1)

        @block.tensor
        def _(pe):
            for n in range(2):
                def fill(F):
                    b, f = F // FILLS, F % FILLS
                    if f == 0:
                        pe.wait_ge(t_in[b % 2], 16 * (b // 2 + 1))
                    if F == n * NH2 * FILLS:
                        pe.wait_ge(w_in, 16 * (n + 1))
                    if F >= 4:
                        pe.wait_ge(moved_act if F % 2 == 0 else moved_dve, (F - 4) // 2 + 1)
                    for a in range(4):
                        src = tiles[b % 2][:, 4 * f + a, 0:P] if f < 4 else k.wrows[:, b % NH2, a, 0:P]
                        mm = pe.transpose(k.ps[:, F % 4, a * P:a * P + P], src, k.ident[:])
                    mm.then_inc(turned, 1)

                def score(F):
                    b, f = F // FILLS, F % FILLS
                    if f == 0 and b >= 2:
                        pe.wait_ge(taken, b - 1)
                    pe.wait_ge(moved_act if F % 2 == 0 else moved_dve, F // 2 + 1)
                    for a in range(4):
                        slot = 4 * f + a
                        mm = pe.matmul(k.ps[:, 4 + b % 2, slot * NH:slot * NH + NH], k.keyT[:, F % 4, a, :], k.qsm[:, b, :],
                                       start=True, stop=True)
                    mm.then_inc(scored, 1)
                F0, F1 = n * NH2 * FILLS, (n + 1) * NH2 * FILLS
                if n:
                    vector.base -= len(vector.steps)
                    vector.wait(pe, "done")
                    vector.base += len(vector.steps)
                for F in range(F0, F1 + 2):
                    if F < F1:
                        fill(F)
                    if F >= F0 + 2:
                        score(F - 2)
                for b in range(NH2):
                    mm = pe.matmul(k.ps[0:NCMP, 6, b * NH:b * NH + NH], k.kcs[:, 0, NH2 * n + b, 0:NCMP],
                                   k.qsm[:, NH2 * n + b, :], start=True, stop=True)
                tensor.mark(mm, "cmp scores")
                q = k.qsm[:, NH2 * n:NH2 * n + NH2, :].rearrange("p b h -> p (b h)")
                for br in range(2):
                    mm = pe.matmul(k.ps[0:R, 7, br * NB:br * NB + NB], q, k.knT[:, br, :], start=True, stop=True)
                tensor.mark(mm, "new scores")
                vector.wait(pe, "cmp kept")
                tensor.mark(pe.transpose(k.ps[0:R, 6, 0:NCMP], k.scT[0:NCMP, :], k.ident[0:NCMP, 0:NCMP]), "cmp rows")
                vector.wait(pe, "cmp p")
                for a in range(2):
                    mm = pe.transpose(k.ps[0:NCMP, 5, a * R:a * R + R], k.pcs[:, a, 0:NCMP], k.ident[0:R, 0:R])
                tensor.mark(mm, "probT")
                vector.wait(pe, "heads summed")
                tensor.mark(pe.matmul(k.ps[0:R, 5, 0:NSEL], k.pcsT[0:NCMP, 2, :], k.smap[0:NCMP, :], start=True, stop=True),
                            "importance")
                pe.wait_ge(taken, NH2 * (n + 1))
                for slot in range(SLOTS):
                    mm = pe.transpose(k.ps[0:R, slot // 4, slot % 4 * P:slot % 4 * P + P], k.sT[:, slot, :], k.ident[:])
                tensor.mark(mm, "rows")
                for b in range(NH2):
                    mm = pe.transpose(k.ps[0:NCMP, 6, b * P:b * P + P], k.kcs[:, 1, NH2 * n + b, 0:NCMP], k.ident[:])
                tensor.mark(mm, "vc")
                vector.wait(pe, "win p")
                for slot in range(SLOTS):
                    src = k.sbuf[:, slot * P:slot * P + P] if slot < SUB else k.wbuf[:, (slot - SUB) * P:(slot - SUB + 1) * P]
                    mm = pe.transpose(k.ps[:, slot // 16, slot % 16 * R:slot % 16 * R + R], src, k.ident[0:R, 0:R])
                for br in range(2):
                    mm = pe.transpose(k.ps[0:NB, 2, br * R:br * R + R], k.sd[:, 2 + br, :], k.ident[0:R, 0:R])
                tensor.mark(mm, "probabilities")
                vector.wait(pe, "vc kept")
                pe.wait_ge(v_kept, NH2 * (n + 1))
                for b in range(NH2):
                    cols = slice(b * NH, b * NH + NH)
                    out = k.ps[:, 7, 64 + b * NH:64 + b * NH + NH]
                    for slot in range(SLOTS):
                        v = k.vrows[:, b, slot, :] if slot < SUB else k.wrows[:, b, slot - SUB, P:2 * P]
                        pe.matmul(out, v, k.pT[:, slot, cols], start=(slot == 0), stop=False)
                    pe.matmul(out, k.vcs[0:NCMP, b, :], k.pcsT[0:NCMP, 1, cols], start=False, stop=False)
                    for br in range(2):
                        mm = pe.matmul(out, k.kv[0:NB, NT, KVW * (1 + br) + P:KVW * (2 + br)], k.dT[:, br, cols],
                                       start=False, stop=(br == 1))
                tensor.mark(mm, "values")
                for st in (tensor, vector, scalar):
                    st.again()
        for st in (tensor, vector, scalar):
            st.base = 0

        @block.scalar
        def _(act):
            for n in range(2):
                for F in range(n * NH2 * FILLS, (n + 1) * NH2 * FILLS, 2):
                    act.wait_ge(turned, F + 1)
                    if F >= 4:
                        act.wait_ge(scored, F - 3)
                    act.activation(k.keyT[:, F % 4], k.ps[:, F % 4, :].rearrange("p (a q) -> p a q", a=4), ACT.Copy
                                   ).then_inc(moved_act, 1)
                vector.wait(act, "cmp max")
                scalar.mark(act.activation(k.pcs[:, 0, 0:NCMP], k.ps[0:R, 6, 0:NCMP], ACT.Exp, bias=k.ss[:, 0, 1:2], scale=SCALE,
                                           accum_out=k.ss[:, 0, 2:3]), "cmp exp")
                vector.wait(act, "sel max")
                scalar.mark(act.activation(k.sbuf[:, 0:PAST + 1], k.sbuf[:, 0:PAST + 1], ACT.Exp, bias=k.ss[:, 1, 1:2],
                                           scale=SCALE, accum_out=k.ss[:, 1, 2:3]), "sel exp")
                vector.wait(act, "win max")
                scalar.mark(act.activation(k.wbuf[:, 0:WIN + 1], k.wbuf[:, 0:WIN + 1], ACT.Exp, bias=k.ss[:, 2, 1:2],
                                           scale=SCALE, accum_out=k.ss[:, 2, 2:3]), "win exp")
                for st in (tensor, vector, scalar):
                    st.again()
        for st in (tensor, vector, scalar):
            st.base = 0

        @block.vector
        def _(dve):
            links = [0]

            def link(ins):
                links[0] += 1
                ins.then_inc(own, 1)
                dve.wait_ge(own, links[0])

            for n in range(2):
                def take(b):
                    dve.wait_ge(scored, FILLS * (b + 1))
                    dve.tensor_copy(k.sT[:, :, b % NH2 * NH:(b % NH2 + 1) * NH],
                                    k.ps[:, 4 + b % 2, 0:SLOTS * NH].rearrange("p (s h) -> p s h", h=NH)).then_inc(taken, 1)
                for F in range(n * NH2 * FILLS + (n * NH2 * FILLS + 1) % 2, (n + 1) * NH2 * FILLS, 2):
                    dve.wait_ge(turned, F + 1)
                    if F >= 4:
                        dve.wait_ge(scored, F - 3)
                    dve.tensor_copy(k.keyT[:, F % 4], k.ps[:, F % 4, :].rearrange("p (a q) -> p a q", a=4)).then_inc(moved_dve, 1)
                    b = F // FILLS
                    if F % FILLS >= 3 and b > n * NH2 and (F - 2) // FILLS == b:
                        take(b - 1)
                take((n + 1) * NH2 - 1)

                def weight(br, row):
                    link(dve.reciprocal(k.ss[:, row, 3:4], k.ss[:, row, 2:3]))
                    link(dve.tensor_tensor(k.ss[:, row, 4:5], k.ss[:, row, 3:4], k.grow[:, n, br:br + 1], ALU.mult))

                tensor.wait(dve, "cmp scores")
                vector.mark(dve.tensor_copy(k.scT[0:NCMP, :], k.ps[0:NCMP, 6, 0:R]), "cmp kept")
                tensor.wait(dve, "cmp rows")
                link(dve.tensor_reduce(k.ss[:, 0, 0:1], k.ps[0:R, 6, 0:NCMP], AX.X, ALU.max))
                vector.mark(dve.tensor_scalar(k.ss[:, 0, 1:2], k.ss[:, 0, 0:1], -SCALE, None, ALU.mult), "cmp max")
                scalar.wait(dve, "cmp exp")
                weight(0, 0)
                dve.tensor_scalar(k.pcs[:, 1, 0:NCMP], k.pcs[:, 0, 0:NCMP], k.ss[:, 0, 4:5], None, ALU.mult)
                vector.mark(dve.tensor_scalar(k.pcs[:, 0, 0:NCMP], k.pcs[:, 0, 0:NCMP], k.ss[:, 0, 3:4], None, ALU.mult), "cmp p")
                tensor.wait(dve, "probT")
                ins = dve.tensor_copy(k.pcsT[0:NCMP, 0:2, :].rearrange("p a r -> p (a r)"), k.ps[0:NCMP, 5, 0:2 * R])
                vector.mark(ins, "probT kept")
                vector.wait(dve, "probT kept")
                link(dve.tensor_reduce(k.scT[0:NCMP, 0:R // GQA], k.pcsT[0:NCMP, 0, :].rearrange("p (a g) -> p a g", g=GQA),
                                       AX.X, ALU.add))
                vector.mark(dve.tensor_copy(k.pcsT[0:NCMP, 2, :].rearrange("p (a g) -> p a g", g=GQA),
                                            bc(k.scT[0:NCMP, 0:R // GQA], 2, GQA)), "heads summed")
                tensor.wait(dve, "new scores")
                for br in range(2):
                    link(dve.tensor_tensor(k.sd[:, br], k.ps[0:R, 7, br * NB:br * NB + NB], k.diag[:, n], ALU.mult))
                link(dve.tensor_reduce(k.sbuf[:, PAST:PAST + 1], k.sd[:, 0], AX.X, ALU.add))
                link(dve.tensor_reduce(k.wbuf[:, WIN:WIN + 1], k.sd[:, 1], AX.X, ALU.add))
                tensor.wait(dve, "importance")
                link(dve.tensor_copy(k.imp[:, 0, 0:NSEL], k.ps[0:R, 5, 0:NSEL]))
                link(dve.memset(k.imp[:, 0, 0:NSEL:NSEL - 1], -NEG))
                link(dve.max(k.m8[:, 0], k.imp[:, 0, 0:NSEL]))
                link(dve.match_replace(k.imp[:, 1, 0:NSEL], k.m8[:, 0], k.imp[:, 0, 0:NSEL], -1.0))
                link(dve.max(k.m8[:, 1], k.imp[:, 1, 0:NSEL]))
                link(dve.match_replace(k.imp[:, 2, 0:NSEL], k.m8[:, 1], k.imp[:, 1, 0:NSEL], -1.0))
                link(dve.tensor_scalar(k.imp[:, 3, 0:NSEL], k.imp[:, 2, 0:NSEL], -1.0, None, ALU.is_equal))
                link(dve.tensor_scalar(k.imp[:, 3, 0:NSEL], k.imp[:, 3, 0:NSEL], 1.0, -NEG, ALU.subtract, ALU.mult))
                tensor.wait(dve, "rows")
                link(dve.tensor_tensor(k.sbuf[:, 0:PAST].rearrange("r (s a b) -> r s a b", s=SUB, b=4),
                                       k.ps[0:R, 0:4, :].rearrange("r k (s n) -> r (k s) n", s=4).rearrange("r s (a b) -> r s a b", b=4),
                                       bc(bc(k.imp[:, 3, 0:NSEL - 1], 1, SUB), 3, 4), ALU.add))
                link(dve.tensor_reduce(k.ss[:, 1, 0:1], k.sbuf[:, 0:PAST + 1], AX.X, ALU.max))
                vector.mark(dve.tensor_scalar(k.ss[:, 1, 1:2], k.ss[:, 1, 0:1], -SCALE, None, ALU.mult), "sel max")
                link(dve.tensor_copy(k.wbuf[:, 0:WIN], k.ps[0:R, 4, :]))
                link(dve.tensor_reduce(k.ss[:, 2, 0:1], k.wbuf[:, 0:WIN + 1], AX.X, ALU.max))
                vector.mark(dve.tensor_scalar(k.ss[:, 2, 1:2], k.ss[:, 2, 0:1], -SCALE, None, ALU.mult), "win max")
                for br, (buf, last, name) in enumerate(((k.sbuf, PAST, "sel"), (k.wbuf, WIN, "win"))):
                    scalar.wait(dve, name + " exp")
                    weight(br + 1, br + 1)
                    link(dve.tensor_scalar(buf[:, 0:last + 1], buf[:, 0:last + 1], k.ss[:, br + 1, 4:5], None, ALU.mult))
                    vector.mark(dve.tensor_scalar(k.sd[:, 2 + br], k.diag[:, n], buf[:, last:last + 1], None, ALU.mult), name + " p")
                tensor.wait(dve, "probabilities")
                dve.tensor_copy(k.pT[:, 0:SUB].rearrange("p s r -> p (s r)"), k.ps[:, 0, :])
                dve.tensor_copy(k.pT[:, SUB:SLOTS].rearrange("p s r -> p (s r)"), k.ps[:, 1, 0:4 * R])
                vector.mark(dve.tensor_copy(k.dT[:].rearrange("b a r -> b (a r)"), k.ps[0:NB, 2, 0:2 * R]), "pT kept")
                vector.mark(dve.tensor_copy(k.vcs[0:NCMP].rearrange("p b r -> p (b r)"), k.ps[0:NCMP, 6, :]), "vc kept")
                tensor.wait(dve, "values")
                for h in range(NH):
                    src = k.ps[HD * (h // GQA):HD * (h // GQA) + HD, 7, 64:64 + R].rearrange("d (b h) -> d b h", h=NH)[:, :, h]
                    ins = dve.tensor_copy(k.mixT[HD * (h % 2):HD * (h % 2) + HD, h // 2, SEQ + NH2 * n:SEQ + NH2 * n + NH2], src)
                vector.mark(ins, "done")
                vector.wait(dve, "done")
                dve.sem_inc(vt, 1)
                for st in (tensor, vector, scalar):
                    st.again()


def cmul(link, dve, out, a, b, tmp, conj=False):
    link(dve.tensor_tensor(tmp[0], a[0], b[0], ALU.mult))
    link(dve.tensor_tensor(tmp[1], a[1], b[1], ALU.mult))
    link(dve.tensor_tensor(out[0], tmp[0], tmp[1], ALU.add if conj else ALU.subtract))
    link(dve.tensor_tensor(tmp[0], a[0], b[1], ALU.mult))
    link(dve.tensor_tensor(tmp[1], a[1], b[0], ALU.mult))
    link(dve.tensor_tensor(out[1], tmp[0], tmp[1], ALU.subtract if conj else ALU.add))


def plan_ssm(nc, k):
    at = k.at
    k.BT, o = at("BT", [P, 2, NJ, P], F32, k.off_q)
    k.CW, o = at("CW", [P, 2, NJ, CH + 1, GC], F32, o)
    k.TZ, o = at("TZ", [P, G, P], F32, o)
    k.uc, o = at("uc", [P, G, NCH], F32, o)
    k.off_z = o
    k.Z, o = at("Z", [P, 2, NJ, NCH], F32, o)
    k.H, _ = at("H", [P, 2, NJ, NCH + 1], F32, k.off_z)
    k.Bw, _ = at("Bw", [P, 2, NJ, CH, GC], F32, k.off_z)
    k.H_end, o = at("H_end", [P, 2], F32, k.off_z + 2 * NJ * (NCH + 1) * 4)
    k.KK, _ = at("KK", [GC, G, P], F32, o)
    k.off_tt = o
    k.tt, o = at("tt", [P, 2, NJ, NCH], F32, o)
    k.decay, o = at("decay", [P, NJ, NCH], F32, o)
    k.E, _ = at("E", [P, 2, NJ, NCH], F32, k.off_mix + 4 * TOK * 4)
    k.PB, o = at("PB", [P, 11, NJ], F32, o)
    k.pw, o = at("pw", [P, 2, CH + 1, NJ], F32, o)
    k.ph, o = at("ph", [P, 2, 2, NJ], F32, o)
    k.h0, o = at("h0", [P, 2, NB * NJ], F32, o)
    k.h1, o = at("h1", [P, 2, NJ * NB], F32, o)
    k.usT, o = at("usT", [GC, G, NB], F32, o)
    k.K0, o = at("K0", [GC, G, GC], F32, o)
    k.Bb, o = at("Bb", [P, 2, NJ, GC], F32, o)
    k.off_ssm_end = o
    k.Bin, _ = at("Bin", [P, 2, NJ, GC], F32, k.off_tt + 2 * NJ * NCH * 4)
    k.PA, o = at("PA", [NJ, 20, P], F32, k.off_tt)


def stage_ssm_parameters(nc, k):
    at = k.at
    k.Cin, _ = at("Cin", [GC, 2, G, PS], F32, k.off_mix + 4 * TOK * 4)
    ldt_in = nc.alloc_semaphore("p_in")
    b_in = nc.alloc_semaphore("b_in")
    h_in = nc.alloc_semaphore("h_in")
    sined = nc.alloc_semaphore("sined")
    to_sine = nc.alloc_semaphore("to_sine")
    params = nc.alloc_semaphore("params")
    formed = nc.alloc_semaphore("formed")
    PAR, C_T, H_T, B_T, KK_T = 1, 2, 3, 4, 5
    h_kept = nc.alloc_semaphore("h_kept")
    bw_made = nc.alloc_semaphore("bw_made")
    cw_made = nc.alloc_semaphore("cw_made")
    b_kept = nc.alloc_semaphore("b_kept")
    kk_kept = nc.alloc_semaphore("kk_kept")
    d_in = nc.alloc_semaphore("d_in")
    k.hrow, _ = at("hrow", [P, 2, P], F32, k.off_z + 2 * NJ * NCH * 4 - 1024)
    k.dcol, _ = at("dcol", [GC, G], F32, k.off_ssm_end)
    k.ldt, _ = at("ldt", [NJ, 2], F32, k.off_ssm_end + 128)
    DT, X, MAG, TH, COS, SIN, ABR, ABI, FR, FI, DEN, ZR, T0, T1, T2, ARE, AIM = range(17)
    SHORT = (ABR, ABI, FR, FI, MAG, COS, SIN)
    with nc.Block() as block:
        @block.sync
        def _(sp):
            for n, a in ((ARE, k.dram["ssm_a_re"]), (AIM, k.dram["ssm_a_im"])):
                sp.dma_start(k.PA[:, n], a[0].rearrange("(j g) p -> j (g p)", g=2)).then_inc(ldt_in, 16)
            sp.dma_start(k.ldt[:], k.dram["ssm_log_dt"][0].rearrange("(j g) -> j g", g=2)).then_inc(ldt_in, 16)
            for n, c in enumerate((k.dram["ssm_c_re"], k.dram["ssm_c_im"])):
                sp.dma_start(k.Cin[:, n], c[0].rearrange("g c p -> c g p")).then_inc(b_in, 16)
            for n, b in enumerate((k.dram["ssm_b_re"], k.dram["ssm_b_im"])):
                for g2 in range(2):
                    sp.dma_start(k.Bin[PS * g2:PS * g2 + PS, n], b[0, g2::2].rearrange("j p c -> p j c")).then_inc(b_in, 16)
            for n, h in enumerate((k.dram["state_ssm_re"], k.dram["state_ssm_im"])):
                sp.dma_start(k.hrow[:, n], h[0].rearrange("b (j g) p -> (b j) (g p)", g=2)).then_inc(h_in, 16)
            sp.dma_start(k.dcol[:], k.dram["ssm_d"][0].rearrange("(g c) -> c g", c=GC), allow_slow_non_contiguous=True).then_inc(d_in, 16)
            sp.wait_ge(kk_kept, 3)
            for s in range(CH):
                sp.dma_start(k.TZ[GC * s:GC * s + GC, :, (CH - 1 - s) * GC:], k.KK[:, :, 0:(s + 1) * GC]).then_inc(d_in, 16)
            sp.wait_ge(d_in, 16 * (CH + 1))

        @block.scalar
        def _(act):
            act.wait_ge(ldt_in, 48)
            act.activation(k.ldt[:], k.ldt[:], ACT.Exp).then_inc(sined, 1)
            act.wait_ge(to_sine, 1)
            act.activation(k.PA[:, MAG], k.PA[:, X], ACT.Exp).then_inc(sined, 1)
            act.wait_ge(to_sine, 2)
            act.activation(k.PA[:, SIN], k.PA[:, T2], ACT.Sin)
            act.activation(k.PA[:, T1], k.PA[:, T2], ACT.Sin, scale=0.5).then_inc(sined, 1)
            act.wait_ge(formed, H_T)
            act.activation(k.h0[:].rearrange("p a b -> p (a b)"), k.ps[:, 7, 0:2 * P], ACT.Copy).then_inc(h_kept, 1)
            act.wait_ge(formed, B_T)
            for n in range(2):
                act.activation(k.BT[:, n].rearrange("p (x a) q -> p x (a q)", x=4), k.ps[:, 4 * n:4 * n + 4, :], ACT.Copy
                               ).then_inc(b_kept, 1)
            act.wait_ge(formed, KK_T)
            for g2 in range(2):
                act.activation(k.KK[:].rearrange("c (x a g) q -> c g x a q", x=4, g=2)[:, g2],
                               k.ps[0:GC, g2::2, :].rearrange("c x (a q) -> c x a q", a=4), ACT.Copy).then_inc(kk_kept, 1)

        @block.tensor
        def _(pe):
            pe.wait_ge(params, 1)
            for n, q in enumerate(SHORT):
                mm = pe.transpose(k.ps[:, 0, n * NJ:n * NJ + NJ], k.PA[:, q], k.ident[0:NJ, 0:NJ])
            mm.then_inc(formed, 1)
            pe.wait_ge(b_in, 16 * 6)
            for n in range(2):
                for j in range(NJ):
                    mm = pe.transpose(k.ps[:, 1 + n, j * GC:j * GC + GC], k.Cin[:, n, 2 * j:2 * j + 2].rearrange("c g p -> c (g p)"),
                                      k.ident[0:GC, 0:GC])
            mm.then_inc(formed, 1)
            pe.wait_ge(h_in, 32)
            for n in range(2):
                mm = pe.transpose(k.ps[:, 7, n * P:n * P + P], k.hrow[:, n], k.ident[:])
            mm.then_inc(formed, 1)
            pe.wait_ge(bw_made, 1)
            pe.wait_ge(cw_made, 1)
            pe.wait_ge(h_kept, 1)
            for n in range(2):
                for j in range(NJ):
                    mm = pe.transpose(k.ps[:, 4 * n + j // 4, j % 4 * P:j % 4 * P + P],
                                      k.Bw[:, n, j].rearrange("p s c -> p (s c)"), k.ident[:])
            mm.then_inc(formed, 1)
            pe.wait_ge(b_kept, 2)
            for j in range(NJ):
                for g2 in range(2):
                    half = slice(PS * g2, PS * g2 + PS)
                    for n in range(2):
                        mm = pe.matmul(k.ps[0:GC, 2 * (j // 4) + g2, j % 4 * P:j % 4 * P + P], k.Bb[half, n, j],
                                       k.CW[half, n, j, 0:CH].rearrange("p s c -> p (s c)"), start=(n == 0), stop=(n == 1))
            mm.then_inc(formed, 1)

        @block.vector
        def _(dve):
            link = Link(nc, dve, "p_link")
            link(dve.memset(k.TZ[:], 0.0))

            def t(n):
                return k.PA[:, n]

            def tt(o, a, b, op):
                link(dve.tensor_tensor(t(o), t(a), t(b), op))
            MAGIC, TWO_PI = 1.5 * 2.0 ** 23, 6.283185307179586
            C1 = 6.28125
            C2 = 0.0019350051879882812
            C3 = TWO_PI - C1 - C2
            PI = 3.1415925
            dve.wait_ge(sined, 1)
            for dst, a in ((X, ARE), (TH, AIM)):
                ins = dve.tensor_tensor(t(dst).rearrange("j (g p) -> j g p", g=2), t(a).rearrange("j (g p) -> j g p", g=2),
                                        bc(k.ldt[:], 2, PS), ALU.mult)
                if dst == X:
                    ins.then_inc(to_sine, 1)
                else:
                    link(ins)
            link(dve.tensor_scalar(t(T0), t(TH), 1 / TWO_PI, MAGIC, ALU.mult, ALU.add))
            link(dve.tensor_scalar(t(T0), t(T0), MAGIC, None, ALU.subtract))
            link(dve.scalar_tensor_tensor(t(T1), t(T0), -C1, t(TH), ALU.mult, ALU.add))
            link(dve.scalar_tensor_tensor(t(T2), t(T0), -C2, t(T1), ALU.mult, ALU.add))
            link(dve.scalar_tensor_tensor(t(T1), t(T0), -C3, t(T2), ALU.mult, ALU.add))
            dve.tensor_scalar(t(T2), t(T1), PI, -PI, ALU.min, ALU.max).then_inc(to_sine, 1)
            dve.wait_ge(sined, 3)
            tt(T0, T1, T1, ALU.mult)
            link(dve.tensor_scalar(t(COS), t(T0), -2.0, 1.0, ALU.mult, ALU.add))
            tt(ABR, MAG, COS, ALU.mult)
            tt(ABI, MAG, SIN, ALU.mult)
            tt(T0, ARE, ARE, ALU.mult)
            tt(T1, AIM, AIM, ALU.mult)
            tt(T2, T0, T1, ALU.add)
            link(dve.reciprocal(t(DEN), t(T2)))
            link(dve.tensor_scalar(t(ZR), t(ABR), 1.0, None, ALU.subtract))
            tt(T0, ZR, ARE, ALU.mult)
            tt(T1, ABI, AIM, ALU.mult)
            tt(T2, T0, T1, ALU.add)
            tt(FR, T2, DEN, ALU.mult)
            tt(T0, ABI, ARE, ALU.mult)
            tt(T1, ZR, AIM, ALU.mult)
            tt(T2, T0, T1, ALU.subtract)
            dve.tensor_tensor(t(FI), t(T2), t(DEN), ALU.mult).then_inc(params, 1)
            dve.wait_ge(formed, PAR)
            B = lambda n: k.PB[:, n]
            link(dve.tensor_copy(k.PB[:, 0:7].rearrange("p a j -> p (a j)"), k.ps[:, 0, 0:7 * NJ]))
            dve.memset(k.pw[:, 0, 0], 1.0)
            dve.memset(k.pw[:, 1, 0], 0.0)
            dve.tensor_copy(k.pw[:, 0, 1], B(0))
            link(dve.tensor_copy(k.pw[:, 1, 1], B(1)))
            for m in (1, 2, 4):
                a = [k.pw[:, n, 1:m + 1] for n in range(2)]
                b = [bc(k.pw[:, n, m], 1, m) for n in range(2)]
                tmp = [k.tt[:, n].rearrange("p j c -> p (j c)")[:, 1024:1024 + m * NJ].rearrange("p (a j) -> p a j", j=NJ) for n in range(2)]
                cmul(link, dve, [k.pw[:, n, m + 1:2 * m + 1] for n in range(2)], a, b, tmp)
            for n in (4,):
                link(dve.tensor_tensor(B(7), B(4), B(4), ALU.mult))
                link(dve.tensor_tensor(B(8), B(7), B(7), ALU.mult))
                link(dve.tensor_tensor(B(4), B(8), B(8), ALU.mult))
            cur = [B(5), B(6)]
            for m in range(3):
                nxt = [k.ph[:, m % 2, n] for n in range(2)]
                cmul(link, dve, nxt, cur, cur, [B(7), B(8)])
                cur = nxt
            dve.wait_ge(b_in, 16 * 6)
            shape = [P, NJ, GC]
            tmp = [k.tt[:, n].rearrange("p j c -> p (j c)")[:, 1024:1024 + NJ * GC].rearrange("p (j c) -> p j c", c=GC) for n in range(2)]
            cmul(link, dve, [k.Bb[:, n] for n in range(2)], [bc(B(2 + n), 2, GC) for n in range(2)], [k.Bin[:, n] for n in range(2)], tmp)
            dve.wait_ge(formed, H_T)
            for s in range(CH):
                cmul(link, dve, [k.Bw[:, n, :, s] for n in range(2)], [bc(k.pw[:, n, s], 2, GC) for n in range(2)],
                     [k.Bb[:, n] for n in range(2)], tmp)
            dve.sem_inc(bw_made, 1)
            dve.wait_ge(formed, C_T)
            link(dve.tensor_copy(k.Bin[:].rearrange("p a j c -> p a (j c)"), k.ps[:, 1:3, 0:NJ * GC]))
            for s in range(CH + 1):
                cmul(link, dve, [k.CW[:, n, :, s] for n in range(2)], [bc(k.pw[:, n, s], 2, GC) for n in range(2)],
                     [k.Bin[:, n] for n in range(2)], tmp)
            link(dve.tensor_scalar(k.CW[:, 1], k.CW[:, 1], -1.0, None, ALU.mult))
            dve.sem_inc(cw_made, 1)
            dve.wait_ge(kk_kept, 2)
            dve.wait_ge(d_in, 16)
            link(dve.tensor_tensor(k.Bin[0:GC].rearrange("p a j c -> p (a j) c"), bc(k.ident[0:GC, 0:GC], 1, G), bc(k.dcol[:], 2, GC), ALU.mult))
            link(dve.tensor_tensor(k.K0[:], k.KK[:, :, 0:GC], k.Bin[0:GC].rearrange("p a j c -> p (a j) c"), ALU.add))
            dve.tensor_copy(k.KK[:, :, 0:GC], k.K0[:]).then_inc(kk_kept, 1)


def stage_ssm_states(nc, k):
    uc_turned = nc.alloc_semaphore("uc_turned")
    uc_kept = nc.alloc_semaphore("uc_kept")
    us_turned = nc.alloc_semaphore("us_turned")
    us_kept = nc.alloc_semaphore("us_kept")
    bu = nc.alloc_semaphore("bu")
    bu_kept = nc.alloc_semaphore("bu_kept")
    bus = nc.alloc_semaphore("bus")
    ends_made = nc.alloc_semaphore("ends_made")
    ends_turned = nc.alloc_semaphore("ends_turned")
    ends_kept = nc.alloc_semaphore("ends_kept")
    decayed = nc.alloc_semaphore("decayed")
    ssm_out = nc.alloc_semaphore("ssm_out")
    at = k.at
    k.ends, _ = at("ends", [P, 3, 2, P], F32, k.off_tt)
    k.stores.append((ssm_out, 64))
    with nc.Block() as block:
        @block.tensor
        def _(pe):
            for x in range(8):
                for a in range(4):
                    mm = pe.transpose(k.ps[:, x, a * P:a * P + P],
                                      k.U[:].rearrange("p g s c -> p (g s c)")[:, (4 * x + a) * P:(4 * x + a + 1) * P], k.ident[:])
                mm.then_inc(uc_turned, 1)
            pe.wait_ge(uc_kept, 8)
            for g in range(G):
                mm = pe.transpose(k.ps[0:GC, 0, g * NB:g * NB + NB], k.us[:, g * GC:g * GC + GC], k.ident[0:NB, 0:NB])
            mm.then_inc(us_turned, 1)
            pe.wait_ge(us_kept, 1)
            for n in range(2):
                for j in range(NJ):
                    for g2 in range(2):
                        mm = pe.matmul(k.ps[PS * g2:PS * g2 + PS, 4 * n + j // 4, j % 4 * P:j % 4 * P + P],
                                       k.BT[:, n, j, PS * g2:PS * g2 + PS], k.uc[:, 2 * j + g2, :], start=True, stop=True)
            mm.then_inc(bu, 1)
            pe.wait_ge(bu_kept, 1)
            for n in range(2):
                for j in range(NJ):
                    for g2 in range(2):
                        c = (n * NJ + j) * NB
                        mm = pe.matmul(k.ps[PS * g2:PS * g2 + PS, 0, c:c + NB], k.BT[0:GC, n, j, PS * g2:PS * g2 + PS],
                                       k.usT[:, 2 * j + g2, :], start=True, stop=True)
            mm.then_inc(bus, 1)
            pe.wait_ge(ends_made, 1)
            for n in range(2):
                pe.transpose(k.ps[0:NJ, 1, n * P:n * P + P], k.ends[:, 2, n, 0:NJ], k.ident[:])
            for n in range(2):
                mm = pe.transpose(k.ps[:, 2, n * P:n * P + P], k.ends[:, 0, n, :], k.ident[:])
            mm.then_inc(ends_turned, 1)

        @block.gpsimd
        def _(pool):
            pool.tensor_copy(k.decay[:], bc(k.PB[:, 4], 2, NCH)).then_inc(decayed, 1)
            pool.wait_ge(decayed, 1)
            pool.memset(k.decay[:, :, 0:1], 0.0).then_inc(decayed, 1)

        @block.scalar
        def _(act):
            for x in range(8):
                act.wait_ge(uc_turned, x + 1)
                act.activation(k.uc[:, 4 * x:4 * x + 4, :].rearrange("p g n -> p (g n)"), k.ps[:, x, :], ACT.Copy).then_inc(uc_kept, 1)
            act.wait_ge(us_turned, 1)
            act.activation(k.usT[:].rearrange("c g b -> c (g b)"), k.ps[0:GC, 0, 0:G * NB], ACT.Copy).then_inc(us_kept, 1)
            act.wait_ge(ends_turned, 1)
            act.activation(k.ends[0:NJ, 1], k.ps[0:NJ, 1, 0:2 * P].rearrange("p (n q) -> p n q", n=2), ACT.Copy).then_inc(ends_kept, 1)
            act.wait_ge(ends_kept, 1)
            for n, out in enumerate((k.dram["p_ssm_re"], k.dram["p_ssm_im"])):
                act.dma_start(out[0, 0].rearrange("(j g) p -> j (g p)", g=2), k.ends[0:NJ, 1, n]).then_inc(ssm_out, 16)
            act.activation(k.ends[:, 2], k.ps[:, 2, 0:2 * P].rearrange("p (n q) -> p n q", n=2), ACT.Copy).then_inc(ends_kept, 1)
            act.wait_ge(ends_kept, 2)
            for n, out in enumerate((k.dram["s_ssm_re"], k.dram["s_ssm_im"])):
                act.dma_start(out[0].rearrange("b (j g) p -> (b j) (g p)", g=2), k.ends[:, 2, n]).then_inc(ssm_out, 16)
            act.wait_ge(ssm_out, 64)

        @block.vector
        def _(dve):
            link = Link(nc, dve, "st_link")
            E = [k.E[:, n] for n in range(2)]
            tmp = [k.tt[:, n] for n in range(2)]
            dve.memset(k.E[:, 0, :, 0], 1.0)
            link(dve.memset(k.E[:, 1, :, 0], 0.0))
            cur = [k.ph[:, 0, n] for n in range(2)]
            for m in range(7):
                w = 1 << m
                cmul(link, dve, [e[:, :, w:2 * w] for e in E], [e[:, :, 0:w] for e in E], [bc(c, 2, w) for c in cur],
                     [t[:, :, 0:w] for t in tmp])
                nxt = [k.ph[:, (m + 1) % 2, n] for n in range(2)]
                cmul(link, dve, nxt, cur, cur, [k.PB[:, 7], k.PB[:, 8]])
                cur = nxt
            dve.wait_ge(bu, 1)
            S = [k.ps[:, 4 * n:4 * n + 4, :].rearrange("p x (a c) -> p (x a) c", c=NCH) for n in range(2)]
            Z = [k.Z[:, n] for n in range(2)]
            cmul(link, dve, Z, E, S, tmp, conj=True)
            dve.sem_inc(bu_kept, 1)
            dve.wait_ge(decayed, 2)
            flat = lambda a: a.rearrange("p j c -> p (j c)")
            for n in range(2):
                link(dve.tensor_tensor_scan(flat(tmp[n]), flat(k.decay[:]), flat(Z[n]), 0.0, ALU.mult, ALU.add))
            H = [k.H[:, n, :, 1:] for n in range(2)]
            link(dve.tensor_tensor(k.decay[:], E[0], tmp[0], ALU.mult))
            link(dve.tensor_tensor(H[0], E[1], tmp[1], ALU.mult))
            link(dve.tensor_tensor(H[0], k.decay[:], H[0], ALU.subtract))
            link(dve.tensor_tensor(k.decay[:], E[0], tmp[1], ALU.mult))
            link(dve.tensor_tensor(H[1], E[1], tmp[0], ALU.mult))
            link(dve.tensor_tensor(H[1], k.decay[:], H[1], ALU.add))
            link(dve.memset(k.H[:, :, :, 0:1], 0.0))
            dve.wait_ge(bus, 1)
            h0 = [k.h0[:, n].rearrange("p (b j) -> p b j", j=NJ) for n in range(2)]
            A = [bc(k.PB[:, n], 1, NB) for n in range(2)]
            h1 = [k.h1[:, n].rearrange("p (b j) -> p b j", j=NJ) for n in range(2)]
            t2 = [k.decay[:, n].rearrange("p (b j) -> p b j", j=NJ) for n in range(2)]
            cmul(link, dve, h1, A, h0, t2)
            for n in range(2):
                link(dve.tensor_tensor(k.ends[:, 0, n].rearrange("p (b j) -> p b j", j=NJ), h1[n],
                                       k.ps[:, 0, n * P:n * P + P].rearrange("p (j b) -> p b j", b=NB), ALU.add))
            link(dve.tensor_copy(k.ends[:, 2, :, 0:NJ], k.H[:, :, :, NCH]))
            dve.sem_inc(ends_made, 1)


def stage_ssm_outputs(nc, k):
    at = k.at
    k.Y, _ = at("Y", [P, CH, SSMW], F32, k.off_u)
    k.gT, o = at("gT", [P, 4, TOK], F32, k.off_z + 2 * NJ * (NCH + 1) * 4)
    k.ys, o = at("ys", [NB, SSMW], F32, o)
    k.w_glu_sb, _ = at("w_glu_sb", [P, 4, 2 * SSMW], F32, k.off_q)
    k.sig, _ = at("sig", [P, 2, TOK], F32, k.off_q + 16384)
    y_ready = nc.alloc_semaphore("y_ready")
    y_act = nc.alloc_semaphore("y_act")
    g_turned = nc.alloc_semaphore("g_turned")
    g_act = nc.alloc_semaphore("g_act")
    g_dve = nc.alloc_semaphore("g_dve")
    w_in = nc.alloc_semaphore("w_glu_in")
    glu = nc.alloc_semaphore("glu")
    sigm = nc.alloc_semaphore("sigm")
    glu_out = nc.alloc_semaphore("glu_out")
    with nc.Block() as block:
        @block.sync
        def _(sp):
            sp.dma_start(k.w_glu_sb[:], k.dram["w_glu"][0].rearrange("(a p) n -> p a n", p=P)).then_inc(w_in, 16)

        @block.tensor
        def _(pe):
            for x in range(4):
                for g2 in range(2):
                    for a in range(4):
                        j = 4 * x + a
                        half = slice(PS * g2, PS * g2 + PS)
                        out = k.ps[:, 2 * x + g2, a * P:a * P + P]
                        pe.matmul(out, k.uc[:, 2 * j + g2, :], k.TZ[:, 2 * j + g2, :], start=True, stop=False)
                        for n in range(2):
                            mm = pe.matmul(out, k.H[half, n, j, 0:NCH], k.CW[half, n, j, 1:].rearrange("p s c -> p (s c)"),
                                           start=False, stop=(n == 1))
                    mm.then_inc(y_ready, 1)
            pe.wait_ge(y_act, 2)
            for g2 in range(2):
                for j in range(NJ):
                    half = slice(PS * g2, PS * g2 + PS)
                    out = k.ps[0:NB, g2, j * GC:j * GC + GC]
                    pe.matmul(out, k.usT[:, 2 * j + g2, :], k.K0[:, 2 * j + g2, :], start=True, stop=False)
                    for n in range(2):
                        mm = pe.matmul(out, k.h0[half, n, j::NJ], k.CW[half, n, j, 1], start=False, stop=(n == 1))
                mm.then_inc(y_ready, 1)
            pe.wait_ge(y_act, 10)
            for t in range(CH):
                for a in range(4):
                    mm = pe.transpose(k.ps[:, t, a * P:a * P + P], k.Y[:, t, a * P:a * P + P], k.ident[:])
                mm.then_inc(g_turned, 1)
            pe.wait_ge(g_act, 1)
            for a in range(4):
                mm = pe.transpose(k.ps[:, 0, a * NB:a * NB + NB], k.ys[:, a * P:a * P + P], k.ident[0:NB, 0:NB])
            mm.then_inc(g_turned, 1)
            pe.wait_ge(w_in, 16)
            pe.wait_ge(g_act, 4)
            pe.wait_ge(g_dve, 5)
            for b in range(4):
                if b:
                    pe.wait_ge(glu_out, b)
                for z in range(2):
                    for a in range(4):
                        for c in range(3):
                            mm = pe.matmul(k.ps[:, 4 * z + c, 0:TG], k.w_glu_sb[:, a, z * SSMW + b * P:z * SSMW + (b + 1) * P],
                                           k.gT[:, a, c * TG:c * TG + TG], start=(a == 0), stop=(a == 3))
                mm.then_inc(glu, 1)

        @block.scalar
        def _(act):
            Y = k.Y[:].rearrange("p t (x a g c) -> p x g a t c", x=4, a=4, g=2)
            for x in range(4):
                for g2 in range(2):
                    act.wait_ge(y_ready, 2 * x + g2 + 1)
                    for a in range(4):
                        ins = act.activation(Y[:, x, g2, a], k.ps[:, 2 * x + g2, a * P:a * P + P].rearrange("p (t c) -> p t c", c=GC),
                                             ACT.Gelu_apprx_tanh)
                    ins.then_inc(y_act, 1)
            for g2 in range(2):
                act.wait_ge(y_ready, 9 + g2)
                act.activation(k.ys[:].rearrange("b (j g c) -> b g j c", g=2, c=GC)[:, g2],
                               k.ps[0:NB, g2, 0:NJ * GC].rearrange("b (j c) -> b j c", c=GC), ACT.Gelu_apprx_tanh).then_inc(y_act, 1)
            for t in range(0, CH, 2):
                act.wait_ge(g_turned, t + 1)
                act.activation(k.gT[:, :, t:SEQ:CH], k.ps[:, t, :].rearrange("p (a n) -> p a n", a=4), ACT.Copy).then_inc(g_act, 1)
            for b in range(4):
                act.wait_ge(glu, b + 1)
                if b >= 2:
                    act.wait_ge(glu_out, b - 1)
                act.activation(k.sig[:, b % 2].rearrange("p (c t) -> p c t", c=3), k.ps[:, 4:7, 0:TG], ACT.Sigmoid,
                               bias=k.vcol[:, 28 + b:29 + b]).then_inc(sigm, 1)

        @block.vector
        def _(dve):
            for t in range(1, CH, 2):
                dve.wait_ge(g_turned, t + 1)
                dve.tensor_copy(k.gT[:, :, t:SEQ:CH], k.ps[:, t, :].rearrange("p (a n) -> p a n", a=4)).then_inc(g_dve, 1)
            dve.wait_ge(g_turned, CH + 1)
            dve.tensor_copy(k.gT[:, :, SEQ:TOK], k.ps[:, 0, 0:4 * NB].rearrange("p (a n) -> p a n", a=4)).then_inc(g_dve, 1)
            for b in range(4):
                dve.wait_ge(sigm, b + 1)
                dve.scalar_tensor_tensor(k.mixT[:, 4 + b].rearrange("p (c t) -> p c t", c=3), k.ps[:, 0:3, 0:TG],
                                         k.vcol[:, 24 + b:25 + b], k.sig[:, b % 2].rearrange("p (c t) -> p c t", c=3),
                                         ALU.add, ALU.mult).then_inc(glu_out, 1)


def stage_w_out(nc, k):
    at = k.at
    k.w_out_sb, _ = at("w_out_sb", [P, KD, D_MODEL], F32, k.off_u)
    w_in = nc.alloc_semaphore("w_out_in")
    product = nc.alloc_semaphore("o_product")
    added = nc.alloc_semaphore("o_added")
    with nc.Block() as block:
        @block.sync
        def _(sp):
            for q in range(4):
                sp.dma_start(k.w_out_sb[:, :, 2 * P * q:2 * P * (q + 1)],
                             k.dram["w_out"][0].rearrange("(a p) n -> p a n", p=P)[:, :, 2 * P * q:2 * P * (q + 1)]).then_inc(w_in, 16)
                sp.wait_ge(w_in, 16 * (q + 1))

        @block.tensor
        def _(pe):
            for d in range(KD):
                pe.wait_ge(w_in, 16 * (d // 2 + 1))
                if d >= 2:
                    pe.wait_ge(added, d - 1)
                for a in range(KD):
                    for c in range(3):
                        mm = pe.matmul(k.ps[:, 4 * (d % 2) + c, 0:TG], k.w_out_sb[:, a, d * P:d * P + P],
                                       k.mixT[:, a, c * TG:c * TG + TG], start=(a == 0), stop=(a == KD - 1))
                mm.then_inc(product, 1)

        @block.vector
        def _(dve):
            for d in range(KD):
                dve.wait_ge(product, d + 1)
                x = k.xT[:, d].rearrange("p (c t) -> p c t", c=3)
                dve.tensor_tensor(x, k.ps[:, 4 * (d % 2):4 * (d % 2) + 3, 0:TG], x, ALU.add).then_inc(added, 1)


def plan_ffn(nc, k):
    at = k.at
    k.gated, o = at("gated", [P, NF, TOK], F32, k.off_u)
    k.hist_row, _ = at("hist_row", [2 * NB, 2 * DFF], F32, k.off_u)
    k.off_down = o
    k.w_up_sb, o = at("w_up_sb", [P, 2, KD, 2, P], F32, o)
    k.hu, o = at("hu", [P, 2, TOK + 2], F32, o)
    k.cv, o = at("cv", [P, 2, TOK], F32, o)
    k.histT, o = at("histT", [P, 2 * NF, NB, 2], F32, o)
    k.last, o = at("last", [P, 2 * NF, NB + 2], F32, o)
    k.w_down_sb, _ = at("w_down_sb", [P, 2, NF, P], F32, k.off_down)
    k.last_row, _ = at("last_row", [NB + 2, 2 * DFF], F32, k.off_mix)


def stage_ffn_up(nc, k):
    hist_in = nc.alloc_semaphore("hist_in")
    hist_turned = nc.alloc_semaphore("hist_turned")
    hist_kept = nc.alloc_semaphore("hist_kept")
    w_in = [nc.alloc_semaphore(f"w_up_in{n}") for n in range(2)]
    product = [nc.alloc_semaphore(f"u_product{n}") for n in range(2)]
    left = [nc.alloc_semaphore(f"u_left{n}") for n in range(2)]
    noted = nc.alloc_semaphore("u_noted")
    convolved = nc.alloc_semaphore("u_convolved")
    silued = nc.alloc_semaphore("u_silued")
    gated = nc.alloc_semaphore("u_gated")
    own = nc.alloc_semaphore("u_own")
    hist_out = nc.alloc_semaphore("hist_out")
    k.stores.append((hist_out, 16))
    w_up = k.dram["w_up"][0].rearrange("(a p) (z f c) -> p a z f c", p=P, z=2, c=P)
    with nc.Block() as block:
        @block.sync
        def _(sp):
            sp.sem_inc(product[1], 2)
            with sp.Fori(0, NF // 2) as i:
                for u in range(2):
                    sp.wait_ge(product[1], i * 2 + (u + 1))
                    for z in range(2):
                        sp.dma_start(k.w_up_sb[:, u, :, z, :],
                                     w_up[:, :, z, bass.ds(i * 2 + u, 1), :].rearrange("p a f c -> p a (f c)")).then_inc(w_in[u], 16)

        @block.tensor
        def _(pe):
            pe.wait_ge(hist_in, 16)
            for f in range(2 * NF):
                mm = pe.transpose(k.ps[:, 3 + 4 * (f // 22), f % 22 * 16:f % 22 * 16 + 16], k.hist_row[:, f * P:f * P + P],
                                  k.ident[0:2 * NB, 0:2 * NB])
            mm.then_inc(hist_turned, 1)
            for z in range(2):
                pe.sem_inc(left[z], 1)
            with pe.Fori(0, NF // 2) as i:
                for u in range(2):
                    pe.wait_ge(w_in[u], i * 32 + 32)
                    for z in range(2):
                        pe.wait_ge(left[z], i * 2 + (u + 1))
                        for a in range(KD):
                            for c in range(3):
                                mm = pe.matmul(k.ps[:, 4 * z + c, 0:TG], k.w_up_sb[:, u, a, z, :],
                                               k.mixT[:, a, c * TG:c * TG + TG], start=(a == 0), stop=(a == KD - 1))
                        mm.then_inc(product[z], 1)

        @block.scalar
        def _(act):
            act.dma_start(k.hist_row[:], k.dram["state_ffn_conv"][0].rearrange("b r n -> (b r) n")).then_inc(hist_in, 16)
            act.dma_start(k.dram["s_ffn_conv"][0, :, 0], k.dram["state_ffn_conv"][0, :, 1]).then_inc(hist_out, 16)
            act.wait_ge(hist_turned, 1)
            for z in range(2):
                act.activation(k.histT[:, z * NF:(z + 1) * NF].rearrange("p f b r -> p (f b r)"), k.ps[:, 3 + 4 * z, 0:22 * 16], ACT.Copy
                               ).then_inc(hist_kept, 1)
            act.sem_inc(gated, 1)
            act.sem_inc(noted, 2)
            with act.Fori(0, NF // 2) as i:
                for u in range(2):
                    act.wait_ge(gated, i * 2 + (u + 1))
                    act.wait_ge(noted, i * 4 + (2 * u + 2))
                    for z in range(2):
                        act.wait_ge(product[z], i * 2 + (u + 1 + 2 * z))
                        src = k.ps[:, 4 * z:4 * z + 3, 0:TG]
                        act.activation(k.hu[:, z, 2:].rearrange("p (c t) -> p c t", c=3), src, ACT.Copy)
                        act.activation(k.cv[:, z].rearrange("p (c t) -> p c t", c=3), src, ACT.Identity,
                                       bias=k.ccol[:, 3, bass.ds(i * 2 + (u + z * NF), 1)],
                                       scale=k.ccol[:, 2, bass.ds(i * 2 + (u + z * NF), 1)]).then_inc(left[z], 1)
                    act.wait_ge(convolved, i * 4 + (2 * u + 1))
                    act.activation(k.cv[:, 0], k.cv[:, 0], ACT.Silu).then_inc(silued, 1)

        @block.gpsimd
        def _(pool):
            with pool.Fori(0, NF // 2) as i:
                for u in range(2):
                    for z in range(2):
                        pool.wait_ge(left[z], i * 2 + (u + 2))
                        pool.tensor_copy(k.last[:, bass.ds(i * 2 + (u + z * NF), 1), :].rearrange("p f t -> p (f t)"),
                                         k.hu[:, z, SEQ:TOK + 2]).then_inc(noted, 1)

        @block.vector
        def _(dve):
            dve.memset(k.hu[:, :, 0:2], 0.0).then_inc(own, 1)
            dve.wait_ge(own, 1)
            dve.wait_ge(hist_kept, 2)
            with dve.Fori(0, NF // 2) as i:
                for u in range(2):
                    for z in range(2):
                        f = i * 2 + (u + z * NF)
                        dve.wait_ge(left[z], i * 2 + (u + 2))
                        w1, w0 = k.ccol[:, 1, bass.ds(f, 1)], k.ccol[:, 0, bass.ds(f, 1)]
                        old = k.histT[:, bass.ds(f, 1), :, :].rearrange("p f b r -> p (f b) r")
                        dve.scalar_tensor_tensor(k.cv[:, z, 0:SEQ], k.hu[:, z, 1:SEQ + 1], w1, k.cv[:, z, 0:SEQ],
                                                 ALU.mult, ALU.add)
                        dve.scalar_tensor_tensor(k.cv[:, z, SEQ:TOK], old[:, :, 1], w1, k.cv[:, z, SEQ:TOK],
                                                 ALU.mult, ALU.add).then_inc(own, 1)
                        dve.wait_ge(own, i * 4 + (2 * u + z + 2))
                        dve.scalar_tensor_tensor(k.cv[:, z, 0:SEQ], k.hu[:, z, 0:SEQ], w0, k.cv[:, z, 0:SEQ],
                                                 ALU.mult, ALU.add)
                        dve.scalar_tensor_tensor(k.cv[:, z, SEQ:TOK], old[:, :, 0], w0, k.cv[:, z, SEQ:TOK],
                                                 ALU.mult, ALU.add).then_inc(convolved, 1)
                    dve.wait_ge(silued, i * 2 + (u + 1))
                    dve.wait_ge(convolved, i * 4 + (2 * u + 2))
                    dve.tensor_tensor(k.gated[:, bass.ds(i * 2 + u, 1), :].rearrange("p f t -> p (f t)"), k.cv[:, 0], k.cv[:, 1],
                                      ALU.mult).then_inc(gated, 1)


def stage_ffn_down(nc, k):
    w_in = [nc.alloc_semaphore(f"w_down_in{n}") for n in range(2)]
    turned = nc.alloc_semaphore("last_turned")
    kept = nc.alloc_semaphore("last_kept")
    out = nc.alloc_semaphore("last_out")
    product = nc.alloc_semaphore("d_product")
    added = nc.alloc_semaphore("d_added")
    w_down = k.dram["w_down"][0].rearrange("(f p) (d c) -> p f d c", p=P, c=P)
    k.stores.append((out, 32))
    NL = 2 * NF // 4
    with nc.Block() as block:
        @block.sync
        def _(sp):
            sp.sem_inc(product, 2)
            with sp.Fori(0, KD // 2) as i:
                for u in range(2):
                    sp.wait_ge(product, i * 2 + (u + 1))
                    sp.dma_start(k.w_down_sb[:, u], w_down[:, :, bass.ds(i * 2 + u, 1), :].rearrange("p f d c -> p f (d c)")
                                 ).then_inc(w_in[u], 16)

        @block.tensor
        def _(pe):
            for n in range(NL):
                if n >= 2:
                    pe.wait_ge(kept, n - 1)
                for a in range(4):
                    mm = pe.transpose(k.ps[0:NB + 2, 3 + 4 * (n % 2), a * P:a * P + P], k.last[:, 4 * n + a, :], k.ident[:])
                mm.then_inc(turned, 1)
            pe.sem_inc(added, 2)
            with pe.Fori(0, KD // 2) as i:
                for u in range(2):
                    pe.wait_ge(w_in[u], i * 16 + 16)
                    pe.wait_ge(added, i * 2 + (u + 1))
                    for f in range(NF):
                        for c in range(3):
                            mm = pe.matmul(k.ps[:, 4 * u + c, 0:TG], k.w_down_sb[:, u, f, :],
                                           k.gated[:, f, c * TG:c * TG + TG], start=(f == 0), stop=(f == NF - 1))
                    mm.then_inc(product, 1)

        @block.scalar
        def _(act):
            for n in range(NL):
                act.wait_ge(turned, n + 1)
                act.activation(k.last_row[:, 4 * P * n:4 * P * (n + 1)], k.ps[0:NB + 2, 3 + 4 * (n % 2), :], ACT.Copy).then_inc(kept, 1)
            act.wait_ge(kept, NL)
            act.dma_start(k.dram["p_ffn_conv"][0, 0], k.last_row[0:2, :]).then_inc(out, 16)
            act.dma_start(k.dram["s_ffn_conv"][0, :, 1], k.last_row[2:, :]).then_inc(out, 16)
            act.wait_ge(out, 32)

        @block.vector
        def _(dve):
            with dve.Fori(0, KD // 2) as i:
                for u in range(2):
                    dve.wait_ge(product, i * 2 + (u + 3))
                    x = k.xT[:, bass.ds(i * 2 + u, 1), :].rearrange("p a (c t) -> p (a c) t", c=3)
                    dve.tensor_tensor(x, k.ps[:, 4 * u:4 * u + 3, 0:TG], x, ALU.add).then_inc(added, 1)


def stage_results(nc, k):
    at = k.at
    k.y_row, o = at("y_row", [P, NT, D_MODEL], F32, k.off_u)
    k.ys_row, _ = at("ys_row", [NB, D_MODEL], F32, o)
    turned = nc.alloc_semaphore("y_turned")
    kept_act = nc.alloc_semaphore("y_kept_act")
    kept_dve = nc.alloc_semaphore("y_kept_dve")
    out = nc.alloc_semaphore("y_out")
    k.stores.append((out, 16 * (NT + 1)))
    with nc.Block() as block:
        @block.tensor
        def _(pe):
            for t in range(NT):
                for half in range(2):
                    if t >= 4:
                        pe.wait_ge(kept_dve if half else kept_act, t - 3)
                    for a in range(4):
                        mm = pe.transpose(k.ps[:, (2 * t + half) % 8, a * P:a * P + P], k.mixT[:, 4 * half + a, t * P:t * P + P], k.ident[:])
                    mm.then_inc(turned, 1)
            for half in range(2):
                pe.wait_ge(kept_dve if half else kept_act, 5)
                for a in range(4):
                    mm = pe.transpose(k.ps[0:NB, half, a * P:a * P + P], k.mixT[:, 4 * half + a, SEQ:TOK], k.ident[:])
                mm.then_inc(turned, 1)

        @block.scalar
        def _(act):
            for t in range(NT):
                act.wait_ge(turned, 2 * t + 1)
                act.activation(k.y_row[:, t, 0:512], k.ps[:, 2 * t % 8, :], ACT.Copy).then_inc(kept_act, 1)
            act.wait_ge(turned, 2 * NT + 1)
            act.activation(k.ys_row[:, 0:512], k.ps[0:NB, 0, :], ACT.Copy).then_inc(kept_act, 1)

        @block.vector
        def _(dve):
            for t in range(NT):
                dve.wait_ge(turned, 2 * t + 2)
                dve.tensor_copy(k.y_row[:, t, 512:], k.ps[:, (2 * t + 1) % 8, :]).then_inc(kept_dve, 1)
            dve.wait_ge(turned, 2 * NT + 2)
            dve.tensor_copy(k.ys_row[:, 512:], k.ps[0:NB, 1, :]).then_inc(kept_dve, 1)

        @block.sync
        def _(sp):
            for t in range(NT):
                sp.wait_ge(kept_act, t + 1)
                sp.wait_ge(kept_dve, t + 1)
                sp.dma_start(k.dram["y_prompt"][0, t * P:t * P + P, :], k.y_row[:, t]).then_inc(out, 16)
            sp.wait_ge(kept_act, NT + 1)
            sp.wait_ge(kept_dve, NT + 1)
            sp.dma_start(k.dram["y_sample"].rearrange("b s d -> (b s) d"), k.ys_row[:]).then_inc(out, 16)


def build(nc, k, upto=99):
    k.ps = nc.alloc_psum_tensor("ps", [P, 8, 512], F32)
    plan(nc, k)
    k.stores = []
    steps = [lambda: stage_load(nc, k),
             lambda: stage_norm(nc, k, "mix", k.mixT, 0, k.off_u),
             lambda: stage_project(nc, k),
             lambda: stage_compress(nc, k),
             lambda: stage_prompt_compressed(nc, k),
             lambda: stage_attend(nc, k),
             lambda: stage_turn_attention(nc, k),
             lambda: stage_sample_prepare(nc, k),
             lambda: stage_sample_attention(nc, k),
             lambda: (plan_ssm(nc, k), stage_ssm_parameters(nc, k)),
             lambda: stage_ssm_states(nc, k),
             lambda: stage_ssm_outputs(nc, k),
             lambda: stage_w_out(nc, k),
             lambda: stage_norm(nc, k, "ffn", k.mixT, 8, k.off_u),
             lambda: (plan_ffn(nc, k), stage_ffn_up(nc, k)),
             lambda: stage_ffn_down(nc, k),
             lambda: stage_norm(nc, k, "final", k.mixT, 16, k.off_u),
             lambda: stage_results(nc, k)]
    for n, s in enumerate(steps):
        if n < upto:
            s()
    with nc.Block() as block:
        @block.sync
        def _(sp):
            for stored, count in k.stores:
                sp.wait_ge(stored, count)


INPUTS = ["x_prompt", "x_sample", "cache_kv_cmp", "cache_kv_sel", "cache_kv_win", "state_ssm_re", "state_ssm_im",
          "state_ffn_conv", "page_table", "norm_mix", "w_in", "pe_cmp", "w_cmp", "ssm_a_re", "ssm_a_im", "ssm_log_dt",
          "ssm_b_re", "ssm_b_im", "ssm_c_re", "ssm_c_im", "ssm_d", "w_glu", "b_glu", "w_out", "norm_ffn", "w_up",
          "conv_w", "conv_b", "w_down", "norm_final"]
OUTPUTS = {"y_prompt": (1, SEQ, D_MODEL), "y_sample": (NB, 1, D_MODEL),
           "p_kv_cmp": (1, 1, SEQ, 2, NKV, HD), "p_kv_sel": (1, 1, SEQ, 2, NKV, HD), "p_kv_win": (1, 1, WIN, 2, NKV, HD),
           "p_ssm_re": (1, 1, G, PS), "p_ssm_im": (1, 1, G, PS), "p_ffn_conv": (1, 1, 2, 2 * DFF),
           "s_kv_cmp": (1, NB, 1, 2, NKV, HD), "s_kv_sel": (1, NB, 1, 2, NKV, HD), "s_kv_win": (1, NB, WIN, 2, NKV, HD),
           "s_ssm_re": (1, NB, G, PS), "s_ssm_im": (1, NB, G, PS), "s_ffn_conv": (1, NB, 2, 2 * DFF)}


def kernel(**inputs):
    import numpy as _np
    import concourse.bacc as _bacc
    from concourse import mybir as _mybir
    from concourse.bass_utils import run_bass_kernel_spmd as _run

    nc = _bacc.Bacc("TRN2", target_bir_lowering=False, num_devices=1)
    arrays = {}
    k = Net()
    k.dram = {}
    for name in INPUTS:
        a = _np.ascontiguousarray(inputs[name])
        arrays[f"in_{name}"] = a
        k.dram[name] = nc.dram_tensor(f"in_{name}", a.shape, _mybir.dt.from_np(a.dtype), kind="ExternalInput").ap()
    for name, shape in OUTPUTS.items():
        k.dram[name] = nc.dram_tensor(f"out_{name}", shape, _mybir.dt.float32, kind="ExternalOutput").ap()
    build(nc, k)
    r = _run(nc, [arrays], core_ids=[0])
    return tuple(r.results[0][f"out_{name}"] for name in OUTPUTS)
```

```python
import concourse.bass as bass
from concourse import mybir

F32 = mybir.dt.float32
F32R = mybir.dt.float32r
BF16 = mybir.dt.bfloat16
I32 = mybir.dt.int32
U32 = mybir.dt.uint32
ALU = mybir.AluOpType
ACT = mybir.ActivationFunctionType
AX = mybir.AxisListType

P = 128
D_MODEL = 1024
SEQ = 1024
NB = 8
TOK = SEQ + NB
TG = TOK // 3
KD = D_MODEL // P
NT = SEQ // P
NH, NKV, HD = 8, 2, 64
GQA = NH // NKV
NSAW = NH * HD
KVW = 2 * NKV * HD
NGATE = 3 * NH
SSMW = D_MODEL - NSAW
CUT_KV = NSAW
CUT_U = NSAW + 3 * KVW + NGATE
KVG = 3 * KVW + NGATE
PAST, PAGE, NPAGE = 2048, 128, 16
SUB = 16
NSUB = PAST // SUB
NSUBP = SEQ // SUB
NCMP = NSUB - 1
NSEL = PAST // 64 + 1
WIN = 512
G, PS, GC = 32, 64, 16
NJ = G // 2
CH = 8
NCH = SEQ // CH
DFF = 2816
NF = DFF // P
SCALE = HD ** -0.5
EPS = 1e-6
NEG = -1e30


class Net:
    pass


def bc(ap, axis, n):
    a = ap.unsqueeze(axis)
    shape = list(a.shape)
    shape[axis] = n
    return a.broadcast_to(shape)


def plan(nc, k):
    def at(name, shape, dtype, offset):
        size = 4 if dtype in (F32, F32R, I32, U32) else 2
        for d in shape[1:]:
            size *= d
        assert BASE + offset + size <= nc.sbuf_usable_end, (name, offset, size)
        return nc.alloc_sbuf_tensor_at(name, shape, dtype, offset=BASE + offset), (offset + size + 31) // 32 * 32
    BASE = 16512
    k.at = at
    k.ident, o = at("ident", [P, P], F32, 0)
    k.ones, o = at("ones", [P, P], F32, o)
    k.identb, o = at("identb", [P, P], BF16, o)
    k.mask_new, o = at("mask_new", [P, P], BF16, o)
    k.mask_old, o = at("mask_old", [P, P], BF16, o)
    k.mask_cmp, o = at("mask_cmp", [P, NT, 64], BF16, o)
    k.seen_cmp, o = at("seen_cmp", [P, 64], F32, o)
    k.vcol, o = at("vcol", [P, 32], F32, o)
    k.ccol, o = at("ccol", [P, 4, 2 * NF], F32, o)
    k.gates, o = at("gates", [P, NT + 1, NGATE], F32, o)
    k.rows_of, o = at("rows_of", [P, NB], U32, o)
    k.grow, o = at("grow", [NB // 2 * NH, 2, 3], F32, o)
    assert o <= 9216, o
    k.xT, o = at("xT", [P, KD, TOK], F32, 9216)
    k.off_mix = o
    k.mixT, o = at("mixT", [P, KD, TOK], F32, o)
    k.off_u = o
    k.U, o = at("U", [P, G, CH, GC], F32, o)
    k.us, o = at("us", [NB, SSMW], F32, o)
    k.off_q = o
    k.qT, o = at("qT", [HD, NH, TOK], F32, o)
    k.off_kv = o
    k.kv, o = at("kv", [P, NT + 1, KVG], F32, o)
    k.off_tmp = o


def stage_load(nc, k):
    at = k.at
    k.xtok, o = at("xtok", [P, NT, D_MODEL], F32, k.off_q)
    k.xs, o = at("xs", [NB, D_MODEL], F32, k.off_kv)
    k.vrow, o = at("vrow", [32, P], F32, o)
    k.crow, o = at("crow", [2 * NF, 4, P], F32, o)
    x_loaded = [nc.alloc_semaphore(f"x_loaded{n}") for n in range(2)]
    vec_loaded = nc.alloc_semaphore("vec_loaded")
    const_made = nc.alloc_semaphore("const_made")
    xt_ready = nc.alloc_semaphore("xt_ready")
    xt_act = nc.alloc_semaphore("xt_act")
    xt_dve = nc.alloc_semaphore("xt_dve")
    vt_ready = nc.alloc_semaphore("vt_ready")
    with nc.Block() as block:
        @block.sync
        def _(sp):
            xv = k.dram["x_prompt"][0].rearrange("(t p) d -> p t d", p=P)
            for n in range(2):
                sp.dma_start(k.xtok[:, 4 * n:4 * n + 4], xv[:, 4 * n:4 * n + 4]).then_inc(x_loaded[n], 16)
            sp.dma_start(k.xs[:], k.dram["x_sample"].rearrange("b s d -> (b s) d")).then_inc(x_loaded[1], 16)

        @block.gpsimd
        def _(pool):
            pool.memset(k.ident[:], 0.0).then_inc(const_made, 1)
            pool.memset(k.ones[:], 1.0)
            pool.memset(k.mask_new[:], 0.0)
            pool.memset(k.mask_old[:], 0.0)
            pool.memset(k.mask_cmp[:], 0.0)
            pool.memset(k.identb[:], 0.0).then_inc(const_made, 1)
            pool.wait_ge(const_made, 2)
            for m in (k.ident, k.identb):
                pool.affine_select(out=m[:], in_=m[:], compare_op=ALU.not_equal, fill=1.0,
                                   base=0, pattern=[[-1, P]], channel_multiplier=1)
            pool.affine_select(out=k.mask_new[:], in_=k.mask_new[:], compare_op=ALU.is_ge, fill=NEG,
                               base=0, pattern=[[-1, P]], channel_multiplier=1)
            pool.affine_select(out=k.mask_old[:], in_=k.mask_old[:], compare_op=ALU.is_ge, fill=NEG,
                               base=0, pattern=[[1, P]], channel_multiplier=-1)
            pool.affine_select(out=k.mask_cmp[:], in_=k.mask_cmp[:], compare_op=ALU.is_ge, fill=NEG,
                               base=-31, pattern=[[P, NT], [-SUB, 64]], channel_multiplier=1)
            pool.affine_select(out=k.seen_cmp[:], in_=k.ones[:, 0:64], compare_op=ALU.is_ge, fill=0.0,
                               base=-31, pattern=[[-SUB, 64]], channel_multiplier=1).then_inc(const_made, 1)

        @block.scalar
        def _(act):
            for n, v in enumerate((k.dram["norm_mix"][0], k.dram["norm_ffn"][0], k.dram["norm_final"], k.dram["b_glu"][0])):
                act.dma_start(k.vrow[8 * n:8 * n + 8], v.rearrange("(a p) -> a p", p=P)).then_inc(vec_loaded, 16)
            for n in range(3):
                act.dma_start(k.crow[:, n], k.dram["conv_w"][0, n].rearrange("(a p) -> a p", p=P)).then_inc(vec_loaded, 16)
            act.dma_start(k.crow[:, 3], k.dram["conv_b"][0].rearrange("(a p) -> a p", p=P)).then_inc(vec_loaded, 16)
            for t in range(NT):
                act.wait_ge(xt_ready, 2 * t + 1)
                act.activation(k.xT[:, 0:4, t * P:t * P + P], k.ps[:, (2 * t) % 8, :].rearrange("p (a b) -> p a b", a=4),
                               ACT.Copy).then_inc(xt_act, 1)
            act.wait_ge(vt_ready, 1)
            act.activation(k.vcol[:], k.ps[:, 1, 0:32], ACT.Copy)
            act.activation(k.ccol[:], k.ps[:, 1, 32:32 + 8 * NF].rearrange("p (a b) -> p a b", a=4), ACT.Copy)

        @block.tensor
        def _(pe):
            pe.wait_ge(const_made, 3)
            for t in range(NT):
                if t % 4 == 0:
                    pe.wait_ge(x_loaded[t // 4], 16 if t == 0 else 32)
                for half in range(2):
                    if t >= 4:
                        pe.wait_ge(xt_act if half == 0 else xt_dve, t - 3)
                    for a in range(4):
                        mm = pe.transpose(k.ps[:, (2 * t + half) % 8, a * P:a * P + P],
                                          k.xtok[:, t, (4 * half + a) * P:(4 * half + a + 1) * P], k.ident[:])
                    mm.then_inc(xt_ready, 1)
            pe.wait_ge(xt_act, 5)
            for a in range(KD):
                mm = pe.transpose(k.ps[:, 0, a * NB:a * NB + NB], k.xs[:, a * P:a * P + P], k.ident[0:NB, 0:NB])
            mm.then_inc(xt_ready, 1)
            pe.wait_ge(vec_loaded, 8 * 16)
            pe.wait_ge(xt_dve, 5)
            pe.transpose(k.ps[:, 1, 0:32], k.vrow[:], k.ident[0:32, 0:32])
            for n in range(4):
                mm = pe.transpose(k.ps[:, 1, 32 + 2 * NF * n:32 + 2 * NF * (n + 1)], k.crow[:, n],
                                  k.ident[0:2 * NF, 0:2 * NF])
            mm.then_inc(vt_ready, 1)

        @block.vector
        def _(dve):
            for t in range(NT):
                dve.wait_ge(xt_ready, 2 * t + 2)
                dve.tensor_copy(k.xT[:, 4:8, t * P:t * P + P],
                                k.ps[:, (2 * t + 1) % 8, :].rearrange("p (a b) -> p a b", a=4)).then_inc(xt_dve, 1)
            dve.wait_ge(xt_ready, 2 * NT + 1)
            dve.tensor_copy(k.xT[:, :, SEQ:TOK], k.ps[:, 0, 0:KD * NB].rearrange("p (a b) -> p a b", a=KD))


def stage_norm(nc, k, tag, dst, gain, tmp):
    at = k.at
    sq, o = at(f"sq_{tag}", [P, 2, TOK], F32, tmp)
    rs, o = at(f"rstd_{tag}", [P, 2, TOK], F32, o)
    squared = nc.alloc_semaphore(f"squared_{tag}")
    summed = nc.alloc_semaphore(f"summed_{tag}")
    inverted = nc.alloc_semaphore(f"inverted_{tag}")
    rooted = nc.alloc_semaphore(f"rooted_{tag}")
    with nc.Block() as block:
        @block.scalar
        def _(act):
            for a in range(KD):
                if a >= 2:
                    act.wait_ge(summed, a - 1)
                act.activation(sq[:, a % 2], k.xT[:, a], ACT.Square).then_inc(squared, 1)
            act.wait_ge(inverted, 2)
            act.activation(rs[:, 0], rs[:, 1], ACT.Sqrt).then_inc(rooted, 1)

        @block.tensor
        def _(pe):
            for a in range(KD):
                pe.wait_ge(squared, a + 1)
                for c in range(3):
                    mm = pe.matmul(k.ps[:, c, 0:TG], k.ones[:], sq[:, a % 2, c * TG:c * TG + TG],
                                   start=(a == 0), stop=(a == KD - 1))
                mm.then_inc(summed, 1)

        @block.vector
        def _(dve):
            dve.wait_ge(summed, KD)
            dve.tensor_scalar(rs[:, 0].rearrange("p (c t) -> p c t", c=3), k.ps[:, 0:3, 0:TG],
                              1.0 / D_MODEL, EPS, ALU.mult, ALU.add).then_inc(inverted, 1)
            dve.wait_ge(inverted, 1)
            dve.reciprocal(rs[:, 1], rs[:, 0]).then_inc(inverted, 1)
            dve.wait_ge(rooted, 1)
            for a in range(KD):
                dve.scalar_tensor_tensor(dst[:, a], k.xT[:, a], k.vcol[:, gain + a:gain + a + 1], rs[:, 0],
                                         ALU.mult, ALU.mult)


def stage_project(nc, k):
    at = k.at
    hT = k.mixT
    k.w_kvg, o = at("w_kvg", [P, KD, KVG], F32, k.off_tmp)
    k.w_qu, o = at("w_qu", [P, KD, NSAW], F32, o)
    wv = k.dram["w_in"][0].rearrange("(k p) n -> p k n", p=P)
    w_q = nc.alloc_semaphore("w_q")
    w_kv = nc.alloc_semaphore("w_kv")
    w_u = nc.alloc_semaphore("w_u")
    projected = nc.alloc_semaphore("projected")
    left_act = nc.alloc_semaphore("left_act")
    left_dve = nc.alloc_semaphore("left_dve")
    rows_out = nc.alloc_semaphore("rows_out")
    cmp_out = nc.alloc_semaphore("cmp_out")
    k.cmp_rows_stored = (cmp_out, 16 * NT)
    k.stores.append(k.cmp_rows_stored)
    n_rows_out = [0]
    NQ = NSAW // P
    JOBS = [("q", b) for b in range(NQ)] + [("kv", t) for t in range(NT + 1)] + [("u", t) for t in range(CH + 1)]
    KVH = KVG // 2
    with nc.Block() as block:
        @block.sync
        def _(sp):
            sp.dma_start(k.w_qu[:], wv[:, :, 0:NSAW]).then_inc(w_q, 16)
            sp.dma_start(k.w_kvg[:], wv[:, :, CUT_KV:CUT_U]).then_inc(w_kv, 16)
            sp.wait_ge(projected, NQ)
            sp.dma_start(k.w_qu[:], wv[:, :, CUT_U:CUT_U + SSMW]).then_inc(w_u, 16)

            def rows_to(dst, src, stored=rows_out):
                n_rows_out[0] += 16 * (stored is rows_out)
                sp.dma_start(dst, src).then_inc(stored, 16)
            outs = [k.dram["p_kv_cmp"], k.dram["p_kv_sel"], k.dram["p_kv_win"]]
            for t in range(NT):
                sp.wait_ge(left_act, NQ + t + 1)
                sp.wait_ge(left_dve, NQ + t + 1)
                for n, out in enumerate(outs):
                    first = 0 if n < 2 else SEQ - WIN
                    if t * P >= first:
                        rows_to(out[0, 0, t * P - first:(t + 1) * P - first].rearrange("t a h d -> t (a h d)"),
                                k.kv[:, t, n * KVW:(n + 1) * KVW], cmp_out if n == 0 else rows_out)
            sp.wait_ge(left_act, NQ + NT + 1)
            sp.wait_ge(left_dve, NQ + NT + 1)
            for n, out in enumerate((k.dram["s_kv_cmp"], k.dram["s_kv_sel"], None)):
                dst = k.dram["s_kv_win"][0, :, WIN - 1] if out is None else out[0, :, 0]
                rows_to(dst.rearrange("b a h d -> b (a h d)"), k.kv[0:NB, NT, n * KVW:(n + 1) * KVW])
            rows_to(k.dram["s_kv_win"][0, :, 0:WIN - 1].rearrange("b t a h d -> b t (a h d)"),
                    k.dram["cache_kv_win"][0, :, 1:WIN].rearrange("b t a h d -> b t (a h d)"))

        @block.tensor
        def _(pe):
            for j, (kind, t) in enumerate(JOBS):
                bank = 4 * (j % 2)
                if j >= 2:
                    pe.wait_ge(left_act, j - 1)
                    pe.wait_ge(left_dve, j - 1)
                if t == 0:
                    pe.wait_ge({"q": w_q, "kv": w_kv, "u": w_u}[kind], 16)
                for a in range(KD):
                    on = dict(start=(a == 0), stop=(a == KD - 1))
                    if kind == "q":
                        for c in range(3):
                            mm = pe.matmul(k.ps[:, bank + c, 0:TG], k.w_qu[:, a, t * P:t * P + P],
                                           hT[:, a, c * TG:c * TG + TG], **on)
                    elif kind == "kv":
                        n = P if t < NT else NB
                        for c in range(2):
                            mm = pe.matmul(k.ps[0:n, bank + c, 0:KVH], hT[:, a, t * P:t * P + n],
                                           k.w_kvg[:, a, c * KVH:(c + 1) * KVH], **on)
                    else:
                        n = P if t < CH else NB
                        tokens = hT[:, a, t:SEQ:CH] if t < CH else hT[:, a, SEQ:TOK]
                        for c in range(2):
                            mm = pe.matmul(k.ps[0:n, bank + c, 0:256], tokens, k.w_qu[:, a, c * 256:c * 256 + 256], **on)
                mm.then_inc(projected, 1)

        def leave(eng, copy, half, left):
            for j, (kind, t) in enumerate(JOBS):
                bank = 4 * (j % 2)
                eng.wait_ge(projected, j + 1)
                if kind == "q":
                    ins = copy(k.qT[:, 2 * t + half].rearrange("p (c t) -> p c t", c=3),
                               k.ps[HD * half:HD * half + HD, bank:bank + 3, 0:TG])
                elif kind == "kv":
                    n = P if t < NT else NB
                    ins = copy(k.kv[0:n, t, half * KVH:(half + 1) * KVH], k.ps[0:n, bank + half, 0:KVH])
                else:
                    s = slice(half * SSMW // 2, (half + 1) * SSMW // 2)
                    src = k.ps[0:(P if t < CH else NB), bank + half, 0:256]
                    if t < CH:
                        ins = copy(k.U[:, half * G // 2:(half + 1) * G // 2, CH - 1 - t, :],
                                   src.rearrange("p (g c) -> p g c", c=GC))
                    else:
                        ins = copy(k.us[:, s], src)
                ins.then_inc(left, 1)

        @block.scalar
        def _(act):
            leave(act, lambda o, i: act.activation(o, i, ACT.Copy), 0, left_act)

        @block.vector
        def _(dve):
            leave(dve, dve.tensor_copy, 1, left_dve)
    k.stores.append((rows_out, n_rows_out[0]))


class Link:

    def __init__(self, nc, eng, name):
        self.eng, self.sem, self.count = eng, nc.alloc_semaphore(name), 0

    def __call__(self, ins):
        self.count += 1
        ins.then_inc(self.sem, 1)
        self.eng.wait_ge(self.sem, self.count)


def stage_compress(nc, k):
    at = k.at
    k.tile, _ = at("tile", [P, 2, SUB, 2 * NKV, HD], F32, k.off_mix)
    k.kcs, o = at("kcs", [P, 2, NB, NSUB], F32, k.off_tmp)
    k.off_kcp = o
    k.kcp, o = at("kcp", [HD, 2 * NKV, 2, NSUBP], F32, o)
    k.cbias, o = at("cbias", [HD, 2], F32, o)
    k.off_att = o
    k.w_c, o = at("w_c", [P, 2, SUB // 2, 2, HD], F32, o)
    k.rowsT, o = at("rowsT", [P, 4, NKV, 2, P], F32, o)
    k.late, o = at("late", [HD, 2, NKV, 2, P], F32, o)
    k.page_of, o = at("page_of", [P, NB], I32, o)
    k.lane, o = at("lane", [P, 1], I32, o)
    k.lanef, o = at("lanef", [P, 1], F32, o)
    NP_ROWS = NSUBP + 2
    wc_loaded = nc.alloc_semaphore("wc_loaded")
    pages_loaded = nc.alloc_semaphore("pages_loaded")
    lane_made = nc.alloc_semaphore("lane_made")
    rows_known = nc.alloc_semaphore("rows_known")
    prompt_in = nc.alloc_semaphore("prompt_in")
    tile_in = [nc.alloc_semaphore(f"tile_in{n}") for n in range(2)]
    transposed = nc.alloc_semaphore("c_transposed")
    moved_act = nc.alloc_semaphore("c_moved_act")
    moved_dve = nc.alloc_semaphore("c_moved_dve")
    multiplied = nc.alloc_semaphore("c_multiplied")
    shifted = nc.alloc_semaphore("c_shifted")
    combined = nc.alloc_semaphore("c_combined")
    FILLS = 8
    width = {0: NP_ROWS}
    with nc.Block() as block:
        @block.sync
        def _(sp):
            wv = k.dram["w_cmp"][0]
            for s2 in range(2):
                for x in range(2):
                    for r in range(2):
                        src = wv[x, r * SUB + s2:(r + 1) * SUB:2].rearrange("s d e -> d s e")
                        sp.dma_start(k.w_c[HD * s2:HD * s2 + HD, x, :, r, :], src).then_inc(wc_loaded, 16)
            for x in range(2):
                for h in range(NKV):
                    sp.dma_start(k.tile[NSUBP:NP_ROWS, 0, :, 2 * x + h, :],
                                 k.dram["pe_cmp"][0, x].rearrange("(r s) d -> r s d", r=2)).then_inc(prompt_in, 16)
            sp.wait_ge(*k.cmp_rows_stored)
            sp.dma_start(k.tile[0:NSUBP, 0].rearrange("n s c d -> n (s c d)"),
                         k.dram["p_kv_cmp"][0, 0].rearrange("(n s) x h d -> n (s x h d)", s=SUB)).then_inc(prompt_in, 16)
            for g in range(NPAGE):
                sp.dma_start(k.page_of[8 * g:8 * g + 8, :], k.dram["page_table"][:, g:g + 1].rearrange("b o -> o b").broadcast_to([8, NB]),
                             allow_slow_non_contiguous=True
                             ).then_inc(pages_loaded, 16)

        @block.gpsimd
        def _(pool):
            pool.iota(k.lane[:], pattern=[[0, 1]], base=0, channel_multiplier=1).then_inc(lane_made, 1)
            pool.wait_ge(rows_known, 1)
            rows = k.dram["cache_kv_cmp"][0].rearrange("n (r s) x h d -> (n r) (s x h d)", s=SUB)
            for b in range(NB):
                j = b + 1
                if j >= 2:
                    pool.wait_ge(transposed, FILLS * (j - 1))
                pool.indirect_dma_start(k.tile[:, j % 2].rearrange("n s c d -> n (s c d)"), None, rows,
                                        bass.IndirectOffsetOnAxis(ap=k.rows_of[:, b:b + 1], axis=0)
                                        ).then_inc(tile_in[j % 2], 16)

        @block.tensor
        def _(pe):
            def turn(j, f, n):
                x, quad = f // 4, f % 4
                for a in range(4):
                    mm = pe.transpose(k.ps[:, f % 4, a * P:a * P + n],
                                      k.tile[0:n, j % 2, 4 * quad + a, 2 * x:2 * x + 2, :].rearrange("n h d -> n (h d)"),
                                      k.ident[0:n, 0:n])
                mm.then_inc(transposed, 1)

            def multiply(j, f, n):
                x, quad = f // 4, f % 4
                for h in range(NKV):
                    for a in range(2):
                        mm = pe.matmul(k.ps[:, 4 + 2 * (j % 2) + h, x * P:x * P + n],
                                       k.w_c[:, x, 2 * quad + a].rearrange("p r e -> p (r e)"),
                                       k.rowsT[:, f % 4, h, a, 0:n], start=(quad == 0 and a == 0), stop=(quad == 3 and a == 1))
                mm.then_inc(multiplied, 1)
            pe.wait_ge(wc_loaded, 8 * 16)
            for j in range(NB + 1):
                n = width.get(j, P)
                if j == 0:
                    pe.wait_ge(prompt_in, 5 * 16)
                else:
                    pe.wait_ge(tile_in[j % 2], 16 * ((j + 1) // 2))
                for f in range(FILLS + 2):
                    F = FILLS * j + f
                    if f < FILLS:
                        if F >= 4:
                            pe.wait_ge(moved_act, F - 3)
                            pe.wait_ge(moved_dve, F - 3)
                        turn(j, f, n)
                    if f >= 2:
                        if f == 2 and j >= 2:
                            pe.wait_ge(combined, j - 1)
                        pe.wait_ge(moved_act, F - 1)
                        pe.wait_ge(moved_dve, F - 1)
                        multiply(j, f - 2, n)

        def move(eng, copy, h, moved, finish):
            for j in range(NB + 1):
                n = width.get(j, P)
                for f in range(FILLS):
                    F = FILLS * j + f
                    eng.wait_ge(transposed, F + 1)
                    if F >= 4:
                        eng.wait_ge(multiplied, F - 3)
                    rows = k.ps[HD * h:HD * h + HD, f % 4, :].rearrange("p (a s n) -> p s a n", a=2, s=2)
                    for s2 in range(2):
                        ins = copy(k.rowsT[HD * s2:HD * s2 + HD, f % 4, h, :, 0:n], rows[:, s2, :, 0:n])
                    ins.then_inc(moved, 1)
                finish(j, n)

        @block.scalar
        def _(act):
            def shift(j, n):
                act.wait_ge(multiplied, FILLS * (j + 1))
                if j >= 2:
                    act.wait_ge(combined, j - 1)
                act.activation(k.late[:, j % 2, :, :, 0:n],
                               k.ps[HD:P, 4 + 2 * (j % 2):6 + 2 * (j % 2), 0:2 * P].rearrange("p h (x n) -> p h x n", x=2)[:, :, :, 0:n],
                               ACT.Copy).then_inc(shifted, 1)
            move(act, lambda o, i: act.activation(o, i, ACT.Copy), 0, moved_act, shift)

        @block.vector
        def _(dve):
            link = Link(nc, dve, "c_link")
            dve.memset(k.kcp[:], 0.0)
            dve.wait_ge(lane_made, 1)
            link(dve.tensor_scalar(k.lane[:], k.lane[:], 7, None, ALU.bitwise_and))
            link(dve.tensor_copy(k.lanef[:], k.lane[:]))
            dve.wait_ge(pages_loaded, 16 * NPAGE)
            dve.tensor_scalar(k.rows_of[:], k.page_of[:], float(PAGE // SUB), k.lanef[:], ALU.mult, ALU.add
                              ).then_inc(rows_known, 1)

            def combine(j, n):
                dve.wait_ge(shifted, j + 1)
                if j == 0:
                    link(dve.tensor_tensor(k.cbias[:], k.ps[0:HD, 4, NSUBP:2 * P:P], k.late[:, 0, 0, :, NSUBP + 1], ALU.add))
                    n = NSUBP
                for c in range(4):
                    x, h = c // 2, c % 2
                    first = k.ps[0:HD, 4 + 2 * (j % 2) + h, x * P:x * P + n - 1]
                    last = k.late[:, j % 2, h, x, 1:n]
                    if j == 0:
                        for copy in range(2):
                            ins = dve.scalar_tensor_tensor(k.kcp[:, c, copy, 0:n - 1], first, k.cbias[:, x:x + 1], last,
                                                           ALU.add, ALU.add)
                    else:
                        ins = dve.scalar_tensor_tensor(k.kcs[HD * h:HD * h + HD, x, j - 1, 0:n - 1], first,
                                                       k.cbias[:, x:x + 1], last, ALU.add, ALU.add)
                ins.then_inc(combined, 1)
            move(dve, dve.tensor_copy, 1, moved_dve, combine)


def stage_prompt_compressed(nc, k):
    at = k.at
    k.oacc, _ = at("oacc", [P, NT, NSAW], F32, k.off_mix + 4 * TOK * 4)
    k.vcp, o = at("vcp", [P, NKV, HD], F32, k.off_att)
    k.sc, o = at("sc", [P, 2, NH, 64], F32, o)
    k.pc, o = at("pc", [P, 2, NH, 64], F32, o)
    k.pcT, o = at("pcT", [P, 2, 4, P], F32, o)
    k.st, o = at("st", [P, NT, 4, NH], F32, o)
    k.glog, o = at("glog", [P, NT + 1, NGATE], F32, o)
    scored = nc.alloc_semaphore("pc_scored")
    less_max = nc.alloc_semaphore("pc_less_max")
    powered = nc.alloc_semaphore("pc_powered")
    weighed = nc.alloc_semaphore("pc_weighed")
    turned = nc.alloc_semaphore("pc_turned")
    turned_out = nc.alloc_semaphore("pc_turned_out")
    valued = nc.alloc_semaphore("pc_valued")
    kept = nc.alloc_semaphore("pc_kept")
    gated = nc.alloc_semaphore("gated")
    v_turned = nc.alloc_semaphore("pc_v_turned")
    with nc.Block() as block:
        @block.tensor
        def _(pe):
            for kvh in range(NKV):
                mm = pe.transpose(k.ps[:, 6, kvh * HD:kvh * HD + HD],
                                  k.kcp[:, NKV + kvh].rearrange("d c n -> d (c n)"), k.ident[0:HD, 0:HD])
            mm.then_inc(v_turned, 1)

            def scores(i):
                if i >= 2:
                    pe.wait_ge(less_max, i - 1)
                bank = i % 2
                for h in range(NH):
                    pe.matmul(k.ps[:, bank, h * 64:h * 64 + 64], k.identb[:], k.mask_cmp[:, i, :], start=True, stop=False)
                    mm = pe.matmul(k.ps[:, bank, h * 64:h * 64 + 64], k.qT[:, h, i * P:i * P + P],
                                   k.kcp[:, h // GQA, 0, :], start=False, stop=True)
                mm.then_inc(scored, 1)

            def values(i):
                pe.wait_ge(weighed, i + 1)
                if i >= 2:
                    pe.wait_ge(turned_out, i - 1)
                for a in range(4):
                    mm = pe.transpose(k.ps[:, 2 + i % 2, a * P:a * P + P],
                                      k.pc[:, i % 2, 2 * a:2 * a + 2, :].rearrange("p h n -> p (h n)"), k.ident[:])
                mm.then_inc(turned, 1)
                pe.wait_ge(turned_out, i + 1)
                if i >= 2:
                    pe.wait_ge(kept, i - 1)
                if i == 0:
                    pe.wait_ge(v_turned, 2)
                for h in range(NH):
                    half = slice(64 * (h % 2), 64 * (h % 2) + 64)
                    mm = pe.matmul(k.ps[:, 4 + 2 * (i % 2) + h % 2, h // 2 * HD:h // 2 * HD + HD], k.pcT[half, i % 2, h // 2, :],
                                   k.vcp[half, h // GQA, :], start=True, stop=True)
                mm.then_inc(valued, 1)
            scores(0)
            for i in range(NT):
                if i + 1 < NT:
                    scores(i + 1)
                values(i)

        @block.scalar
        def _(act):
            def keep(i):
                bank = 4 + 2 * (i % 2)
                act.activation(k.oacc[:, i].rearrange("p (a b d) -> p a b d", a=4, b=2),
                               k.ps[:, bank:bank + 2, 0:4 * HD].rearrange("p b (a d) -> p a b d", a=4),
                               ACT.Copy).then_inc(kept, 1)
            act.wait_ge(v_turned, 1)
            act.activation(k.vcp[:], k.ps[:, 6, 0:P].rearrange("p (h d) -> p h d", h=NKV), ACT.Copy).then_inc(v_turned, 1)
            act.activation(k.glog[:, 0:NT], k.kv[:, 0:NT, 3 * KVW:], ACT.Exp, scale=-1.0)
            act.activation(k.glog[0:NB, NT], k.kv[0:NB, NT, 3 * KVW:], ACT.Exp, scale=-1.0).then_inc(gated, 1)
            for i in range(NT):
                act.wait_ge(less_max, i + 1)
                if i >= 2:
                    act.wait_ge(turned, i - 1)
                act.activation(k.pc[:, i % 2], k.sc[:, i % 2], ACT.Exp, scale=SCALE).then_inc(powered, 1)
                if i >= 1:
                    act.wait_ge(valued, i)
                    keep(i - 1)
            act.wait_ge(valued, NT)
            keep(NT - 1)

        @block.vector
        def _(dve):
            link = Link(nc, dve, "pc_link")
            dve.wait_ge(gated, 1)
            link(dve.tensor_scalar(k.glog[:, 0:NT], k.glog[:, 0:NT], 1.0, None, ALU.add))
            link(dve.tensor_scalar(k.glog[0:NB, NT], k.glog[0:NB, NT], 1.0, None, ALU.add))
            dve.reciprocal(k.gates[:, 0:NT], k.glog[:, 0:NT])
            link(dve.reciprocal(k.gates[0:NB, NT], k.glog[0:NB, NT]))

            def less(i):
                dve.wait_ge(scored, i + 1)
                s = k.ps[:, i % 2, :].rearrange("p (h n) -> p h n", h=NH)
                link(dve.tensor_reduce(k.st[:, i, 0], s, AX.X, ALU.max))
                if i >= 2:
                    dve.wait_ge(powered, i - 1)
                dve.tensor_tensor(k.sc[:, i % 2], s, bc(k.st[:, i, 0], 2, 64), ALU.subtract).then_inc(less_max, 1)

            def weigh(i):
                dve.wait_ge(powered, i + 1)
                p = k.pc[:, i % 2]
                if i == 0:
                    link(dve.tensor_tensor(p, p, bc(k.seen_cmp[:], 1, NH), ALU.mult))
                link(dve.tensor_reduce(k.st[:, i, 1], p, AX.X, ALU.add))
                link(dve.tensor_scalar(k.st[:, i, 2], k.st[:, i, 1], 1e-30, None, ALU.max))
                link(dve.reciprocal(k.st[:, i, 3], k.st[:, i, 2]))
                link(dve.tensor_tensor(k.st[:, i, 1], k.st[:, i, 3], k.gates[:, i, 0::3], ALU.mult))
                dve.tensor_tensor(p, p, bc(k.st[:, i, 1], 2, 64), ALU.mult).then_inc(weighed, 1)

            def turn_out(i):
                dve.wait_ge(turned, i + 1)
                if i >= 2:
                    dve.wait_ge(valued, i - 1)
                dve.tensor_copy(k.pcT[:, i % 2], k.ps[:, 2 + i % 2, :].rearrange("p (a q) -> p a q", a=4)).then_inc(turned_out, 1)
            less(0)
            for i in range(NT):
                if i + 1 < NT:
                    less(i + 1)
                weigh(i)
                turn_out(i)


def stage_attend(nc, k):
    at = k.at
    k.kT, _ = at("kT", [P, 2, NKV, SEQ], F32R, k.off_mix)
    k.topT, _ = at("topT", [P, 2, 2 * GQA, P], F32R, k.off_q)
    k.q_up, o = at("q_up", [P, 2, GQA, P], F32R, k.off_kcp)
    k.q_rest, o = at("q_rest", [P, 2, GQA, P], F32R, o)
    k.v1, o = at("v1", [P, NT, 2, NKV, HD + 1], F32, o)
    k.prob_sel, o = at("prob_sel", [P, NT, GQA, P], F32, o)
    k.prob_win, o = at("prob_win", [P, WIN // P + 1, GQA, P], F32, o)
    k.k_up, _ = at("k_up", [P, 4, 4 * P], F32R, o - 8192)
    k.minus1, o = at("minus1", [P, P], F32R, o)
    k.top, o = at("top", [P, 2, 2, GQA], F32, o)
    k.norm, o = at("norm", [P, 2, 2, GQA], F32, o)
    k.part, o = at("part", [P, 2, GQA, HD], F32, o)
    probs = [k.prob_sel, k.prob_win]
    TOPT = slice(HD, HD + 2 * GQA)
    k_turned = nc.alloc_semaphore("k_turned")
    k_upper = nc.alloc_semaphore("k_upper")
    k_split = nc.alloc_semaphore("k_split")
    v_set = nc.alloc_semaphore("v_set")
    rest_low = nc.alloc_semaphore("q_rest_low")
    rest_high = nc.alloc_semaphore("q_rest_high")
    q_upper = nc.alloc_semaphore("q_upper")
    looked = nc.alloc_semaphore("a_looked")
    reduced = nc.alloc_semaphore("a_reduced")
    scored = nc.alloc_semaphore("a_scored")
    powered = nc.alloc_semaphore("a_powered")
    valued = nc.alloc_semaphore("a_valued")
    weighed = nc.alloc_semaphore("a_weighed")
    added = nc.alloc_semaphore("a_added")

    GROUPS = [(i, kvh) for i in range(NT) for kvh in range(NKV)]

    def q_of(g):
        i, kvh = GROUPS[g]
        return k.qT[:, GQA * kvh:GQA * (kvh + 1), i * P:i * P + P]

    def blocks_of(i):
        return [list(range(i + 1)), list(range(max(0, i - WIN // P), i + 1))]

    def looks_of(i):
        out = []
        for br, bl in enumerate(blocks_of(i)):
            n = 1 if len(bl) > 4 else 2 if len(bl) > 2 else 4
            out += [(br, h, n) for h in range(0, GQA, n)]
        return out

    ORDER = [("split", 0)] + [("look", 0, *s) for s in looks_of(0)] + [("turn", 0)]
    for g, (i, kvh) in enumerate(GROUPS):
        nxt = [("look", g + 1, *s) for s in looks_of(GROUPS[g + 1][0])] if g + 1 < len(GROUPS) else []
        both = blocks_of(i)
        n_scores, n_looks = len(both[0]) + len(both[1]), len(nxt)
        scores = looks = 0
        if nxt:
            ORDER.append(("split", g + 1))
        for br in range(2):
            for b in both[br]:
                ORDER.append(("score", g, br, b))
                scores += 1
                while looks * n_scores < n_looks * scores:
                    ORDER.append(nxt[looks])
                    looks += 1
            if br == 0 and g:
                ORDER.append(("value", g - 1, 1))
        if g + 1 < len(GROUPS):
            ORDER.append(("turn", g + 1))
        ORDER.append(("value", g, 0))
    ORDER.append(("value", len(GROUPS) - 1, 1))
    grow_in = nc.alloc_semaphore("grow_in")
    SCORES = [step[1:] for step in ORDER if step[0] == "score"]
    VALUES = [step[1:] for step in ORDER if step[0] == "value"]
    LOOKS = [step for step in ORDER if step[0] in ("look", "turn")]
    looks_before = {step[1]: n for n, step in enumerate(LOOKS) if step[0] == "turn"}

    def scores_to(g, br):
        return max(n for n, s in enumerate(SCORES) if s[:2] == (g, br)) + 1

    def look_banks(n):
        return 2 * (n % 2)

    with nc.Block() as block:
        @block.sync
        def _(sp):
            for b in range(NB):
                for h in range(NH):
                    r = NH * (b % (NB // 2)) + h
                    sp.dma_start(k.grow[r:r + 1, b // (NB // 2), :], k.gates[b:b + 1, NT, 3 * h:3 * h + 3]).then_inc(grow_in, 16)
            sp.wait_ge(grow_in, 16 * NB * NH)

        @block.tensor
        def _(pe):
            for c in range(4):
                src = KVW * (1 + c // 2)
                for a in range(4):
                    t = 4 * (c % 2) + a
                    mm = pe.transpose(k.ps[:, c, a * P:a * P + P], k.kv[:, t, src:src + P], k.ident[:])
                mm.then_inc(k_turned, 1)
            pe.wait_ge(k_split, 16)
            looks = scores = 0
            for kind, g, *rest in ORDER:
                i, kvh = GROUPS[g]
                if kind == "look":
                    br, h0, nh = rest
                    if h0 == 0 and br == 0:
                        pe.wait_ge(q_upper, 2 * g + 2)
                    if looks >= 2:
                        pe.wait_ge(reduced, looks - 1)
                    bl = blocks_of(i)[br]
                    masks = {i: k.mask_new, **({i - WIN // P: k.mask_old} if br else {})}
                    for h in range(nh):
                        col = h * 2 * 4 * P // nh
                        for b0, nb in runs(bl, masks):
                            for lo in range(b0, b0 + nb, 4):
                                n = min(4, b0 + nb - lo)
                                for p0, p1 in pieces(col + (lo - bl[0]) * P, n * P):
                                    out = k.ps[:, look_banks(looks) + p0 // 512, p0 % 512:p0 % 512 + p1 - p0]
                                    tok = (bl[0] * P) + p0 - col
                                    mm = pe.matmul(out, k.q_up[:, g % 2, h0 + h, :], k.kT[:, br, kvh, tok:tok + p1 - p0],
                                                   start=True, stop=b0 not in masks)
                                    if b0 in masks:
                                        mm = pe.matmul(out, k.identb[:], masks[b0][:], start=False, stop=True)
                    mm.then_inc(looked, 1)
                    looks += 1
                elif kind == "turn":
                    pe.wait_ge(reduced, looks)
                    pe.transpose(k.ps[0:2 * GQA, look_banks(looks), 0:P], k.top[:, g % 2].rearrange("p b h -> p (b h)"),
                                 k.ident[:]).then_inc(looked, 1)
                    looks += 1
                elif kind == "score":
                    br, b = rest
                    if scores >= 2:
                        pe.wait_ge(powered, scores - 1)
                    if br == 0 and b == 0:
                        pe.wait_ge(rest_low, g + 1)
                        pe.wait_ge(rest_high, g + 1)
                        pe.wait_ge(reduced, looks_before[g] + 1)
                    out = k.ps[:, 4 + scores % 2, :]
                    ks = k.kT[:, br, kvh, b * P:b * P + P]
                    mask = k.mask_old if b == i else k.mask_new if br and b == i - WIN // P else None
                    pe.matmul(out, ks, k.q_up[:, g % 2].rearrange("p h q -> p (h q)"), start=True, stop=False)
                    pe.matmul(out, ks, k.q_rest[:, g % 2].rearrange("p h q -> p (h q)"), start=False, stop=False)
                    if mask is not None:
                        pe.matmul(out, k.identb[:], bc(mask[:], 1, GQA), start=False, stop=False)
                    pe.matmul(out, k.minus1[HD:P, :], k.topT[HD:P, g % 2, GQA * br:GQA * (br + 1), :].rearrange("r h q -> r (h q)"),
                              start=False, stop=True).then_inc(scored, 1)
                    scores += 1
                elif kind == "value":
                    br, = rest
                    bl = blocks_of(i)[br]
                    pe.wait_ge(powered, scores_to(g, br))
                    if g:
                        pe.wait_ge(weighed, VALUES.index((g - 1, br)) + 1)
                    for h in range(GQA):
                        for b in bl:
                            mm = pe.matmul(k.ps[:, 6 + br, h * (HD + 1):(h + 1) * (HD + 1)], probs[br][:, b - bl[0], h, :],
                                           k.v1[:, b, br, kvh, :], start=(b == bl[0]), stop=(b == i))
                    mm.then_inc(valued, 1)

        @block.scalar
        def _(act):
            for c in range(4):
                act.wait_ge(k_turned, c + 1)
                act.activation(k.k_up[:, c], k.ps[:, c, :], ACT.Copy).then_inc(k_upper, 1)
                act.wait_ge(k_upper, c + 1)
                for kvh in range(NKV):
                    act.activation(k.kT[0:HD, c // 2, kvh, 4 * P * (c % 2):4 * P * (c % 2 + 1)], k.k_up[HD * kvh:HD * (kvh + 1), c],
                                   ACT.Copy).then_inc(k_split, 1)

            def upper(g):
                if g >= 2:
                    act.wait_ge(scored, scores_to(g - 2, 1))
                for half in range(2):
                    act.activation(k.q_up[HD * half:HD * half + HD, g % 2], q_of(g), ACT.Copy).then_inc(q_upper, 1)
            act.activation(k.minus1[:], k.ones[:], ACT.Copy, scale=-1.0)
            upper(0)
            act.wait_ge(k_split, 16)
            for n, (g, br, b) in enumerate(SCORES):
                first = blocks_of(GROUPS[g][0])[br][0]
                if br == 0 and b == first and g + 1 < len(GROUPS):
                    upper(g + 1)
                act.wait_ge(scored, n + 1)
                if b == first and g:
                    act.wait_ge(valued, VALUES.index((g - 1, br)) + 1)
                act.activation(probs[br][:, b - first].rearrange("p h q -> p (h q)"), k.ps[:, 4 + n % 2, :], ACT.Exp,
                               scale=SCALE).then_inc(powered, 1)

        @block.gpsimd
        def _(pool):
            for g in range(len(GROUPS)):
                pool.wait_ge(q_upper, 2 * g + 2)
                if g >= 2:
                    pool.wait_ge(scored, scores_to(g - 2, 1))
                pool.tensor_tensor(k.q_rest[HD:P, g % 2], q_of(g), k.q_up[0:HD, g % 2].bitcast(F32), ALU.subtract
                                   ).then_inc(rest_high, 1)

        @block.vector
        def _(dve):
            for c in range(4):
                dve.wait_ge(k_upper, c + 1)
                for kvh in range(NKV):
                    rows = slice(HD * kvh, HD * (kvh + 1))
                    dve.tensor_tensor(k.kT[HD:P, c // 2, kvh, 4 * P * (c % 2):4 * P * (c % 2 + 1)], k.ps[rows, c, :],
                                      k.k_up[rows, c].bitcast(F32), ALU.subtract).then_inc(k_split, 1)
            for br in range(2):
                v = KVW * (1 + br) + P
                dve.tensor_copy(k.v1[:, :, br, :, 0:HD], k.kv[:, 0:NT, v:v + P].rearrange("p t (h d) -> p t h d", h=NKV))
            dve.memset(k.topT[HD:P].bitcast(F32), 0.0)
            dve.memset(k.v1[:].rearrange("p t b h d -> p (t b h) d")[:, :, HD:HD + 1], 1.0).then_inc(v_set, 1)
            dve.wait_ge(v_set, 1)
            looks = values = 0
            for kind, g, *rest in ORDER:
                i, kvh = GROUPS[g]
                if kind == "split":
                    dve.wait_ge(q_upper, 2 * g + 2)
                    dve.tensor_tensor(k.q_rest[0:HD, g % 2], q_of(g), k.q_up[0:HD, g % 2].bitcast(F32), ALU.subtract
                                      ).then_inc(rest_low, 1)
                elif kind == "look":
                    br, h0, nh = rest
                    w = len(blocks_of(i)[br]) * P
                    dve.wait_ge(looked, looks + 1)
                    s = k.ps[:, look_banks(looks):look_banks(looks) + 2, :].rearrange("p a n -> p (a n)")
                    dve.tensor_reduce(k.top[:, g % 2, br, h0:h0 + nh], s.rearrange("p (h n) -> p h n", h=nh)[:, :, 0:w], AX.X, ALU.max
                                      ).then_inc(reduced, 1)
                    looks += 1
                elif kind == "turn":
                    dve.wait_ge(looked, looks + 1)
                    if g >= 2:
                        dve.wait_ge(scored, scores_to(g - 2, 1))
                    dve.tensor_tensor(k.topT[TOPT, g % 2], bc(k.ps[0:2 * GQA, look_banks(looks), 0:P], 1, 2 * GQA),
                                      bc(k.ident[0:2 * GQA, 0:2 * GQA], 2, P), ALU.mult).then_inc(reduced, 1)
                    looks += 1
                elif kind == "value":
                    br, = rest
                    dve.wait_ge(valued, values + 1)
                    o = k.ps[:, 6 + br, 0:GQA * (HD + 1)].rearrange("p (h d) -> p h d", h=GQA)
                    steps = 4 * values
                    dve.reciprocal(k.norm[:, br, 0], o[:, :, HD]).then_inc(added, 1)
                    dve.wait_ge(added, steps + 1)
                    gate = k.gates[:, i, 3 * GQA * kvh:3 * GQA * (kvh + 1)].rearrange("p (h z) -> p h z", z=3)[:, :, 1 + br]
                    dve.tensor_tensor(k.norm[:, br, 1], k.norm[:, br, 0], gate, ALU.mult).then_inc(added, 1)
                    dve.wait_ge(added, steps + 2)
                    dve.tensor_tensor(k.part[:, br], o[:, :, 0:HD], bc(k.norm[:, br, 1], 2, HD), ALU.mult).then_inc(weighed, 1)
                    dve.wait_ge(weighed, values + 1)
                    acc = k.oacc[:, i, GQA * HD * kvh:GQA * HD * (kvh + 1)].rearrange("p (h d) -> p h d", h=GQA)
                    dve.tensor_tensor(acc, k.part[:, br], acc, ALU.add).then_inc(added, 2)
                    dve.wait_ge(added, steps + 4)
                    values += 1


def runs(blocks, masks):
    out = []
    for b in blocks:
        if b not in masks and out and out[-1][0] not in masks:
            out[-1] = (out[-1][0], out[-1][1] + 1)
        else:
            out.append((b, 1))
    return out


def pieces(start, size):
    out, end = [], start + size
    while start < end:
        stop = min(end, (start // 512 + 1) * 512)
        out.append((start, stop))
        start = stop
    return out


def stage_turn_attention(nc, k):
    turned = nc.alloc_semaphore("t_turned")
    kept_act = nc.alloc_semaphore("t_kept_act")
    kept_dve = nc.alloc_semaphore("t_kept_dve")
    with nc.Block() as block:
        @block.tensor
        def _(pe):
            for i in range(NT):
                for a in range(4):
                    mm = pe.transpose(k.ps[:, i, a * P:a * P + P], k.oacc[:, i, a * P:a * P + P], k.ident[:])
                mm.then_inc(turned, 1)

        @block.scalar
        def _(act):
            for i in range(0, NT, 2):
                act.wait_ge(turned, i + 1)
                act.activation(k.mixT[:, 0:4, i * P:i * P + P], k.ps[:, i, :].rearrange("p (a q) -> p a q", a=4), ACT.Copy)

        @block.vector
        def _(dve):
            for i in range(1, NT, 2):
                dve.wait_ge(turned, i + 1)
                dve.tensor_copy(k.mixT[:, 0:4, i * P:i * P + P], k.ps[:, i, :].rearrange("p (a q) -> p a q", a=4))


class Steps:

    def __init__(self, nc, name, steps):
        self.sem, self.steps, self.base = nc.alloc_semaphore(name), steps, 0

    def mark(self, ins, step):
        ins.then_inc(self.sem, 1)

    def wait(self, eng, step):
        eng.wait_ge(self.sem, self.base + self.steps.index(step) + 1)

    def again(self):
        self.base += len(self.steps)


NH2 = NB // 2
R = NH2 * NH
SLOTS = SUB + WIN // P


def stage_sample_prepare(nc, k):
    at = k.at
    o = k.off_q + 33024 + NT * KVG * 4
    k.off_s1 = k.off_q + 0
    o = (k.off_att + 31) // 32 * 32
    k.qsm, o = at("qsm", [P, NB, NH], F32, o)
    k.knT, o = at("knT", [P, 2, NB], F32, o)
    k.diag, o = at("diag", [R, 2, NB], F32, o)
    k.smap, o = at("smap", [P, NSEL], F32, o)
    k.off_s2 = o
    made = nc.alloc_semaphore("s_made")
    kn_turned = nc.alloc_semaphore("kn_turned")
    zeroed = nc.alloc_semaphore("qsm_zeroed")
    with nc.Block() as block:
        @block.gpsimd
        def _(pool):
            pool.memset(k.smap[:], 1.0)
            pool.memset(k.diag[:], 1.0).then_inc(made, 1)
            pool.wait_ge(made, 1)
            pool.affine_select(out=k.smap[:], in_=k.smap[:], compare_op=ALU.is_ge, fill=0.0, base=63,
                               pattern=[[64, NSEL]], channel_multiplier=-SUB)
            pool.affine_select(out=k.diag[:], in_=k.diag[:], compare_op=ALU.is_ge, fill=0.0, base=0,
                               pattern=[[NH * NH2, 2], [-NH, NB]], channel_multiplier=1).then_inc(made, 1)
            pool.wait_ge(made, 2)
            pool.affine_select(out=k.smap[:], in_=k.smap[:], compare_op=ALU.is_ge, fill=0.0, base=31,
                               pattern=[[-64, NSEL]], channel_multiplier=SUB)
            pool.affine_select(out=k.diag[:], in_=k.diag[:], compare_op=ALU.is_ge, fill=0.0, base=NH - 1,
                               pattern=[[-NH * NH2, 2], [NH, NB]], channel_multiplier=-1)

        @block.tensor
        def _(pe):
            for br in range(2):
                mm = pe.transpose(k.ps[:, 0, br * NB:br * NB + NB], k.kv[0:NB, NT, KVW * (1 + br):KVW * (1 + br) + P],
                                  k.ident[0:NB, 0:NB])
            mm.then_inc(kn_turned, 1)

        @block.vector
        def _(dve):
            dve.memset(k.qsm[:], 0.0).then_inc(zeroed, 1)
            dve.wait_ge(zeroed, 1)
            for kvh in range(NKV):
                hs = slice(kvh * GQA, (kvh + 1) * GQA)
                dve.tensor_copy(k.qsm[HD * kvh:HD * kvh + HD, :, hs], k.qT[:, hs, SEQ:TOK].rearrange("d h b -> d b h"))
            dve.wait_ge(kn_turned, 1)
            dve.tensor_copy(k.knT[:].rearrange("p a b -> p (a b)"), k.ps[:, 0, 0:2 * NB])


def stage_sample_attention(nc, k):
    at = k.at
    k.vrows, o = at("vrows", [P, NH2, SUB, P], F32, k.off_q)
    k.stile0, o = at("stile0", [P, SUB, 2 * P], F32, o)
    assert o <= k.off_kv + NT * KVG * 4, o
    k.stile1, o = at("stile1", [P, SUB, 2 * P], F32, k.off_s2)
    k.wrows, o = at("wrows", [P, NH2, WIN // P, 2 * P], F32, o)
    k.sT, o = at("sT", [P, SLOTS, R], F32, o)
    k.scT, o = at("scT", [P, R], F32, o)
    k.pcs, o = at("pcs", [R, 2, P], F32, o)
    k.pcsT, o = at("pcsT", [P, 3, R], F32, o)
    k.dT, o = at("dT", [NB, 2, R], F32, o)
    k.imp, o = at("imp", [R, 4, 40], F32, o)
    k.m8, o = at("m8", [R, 2, 8], F32, o)
    k.ss, o = at("ss", [R, 3, 8], F32, o)
    k.sd, o = at("sd", [R, 4, NB], F32, o)
    k.sbuf, _ = at("sbuf", [R, PAST + 32], F32, k.off_mix + 4 * TOK * 4)
    k.keyT, _ = at("keyT", [P, 4, 4, P], F32, k.off_mix + 4 * TOK * 4 + (PAST + 32) * 4)
    k.wbuf, o = at("wbuf", [R, WIN + 32], F32, o)
    k.vcs, o = at("vcs", [P, NH2, P], F32, o)
    k.pT = k.sT
    tiles = [k.stile0, k.stile1]
    t_in = [nc.alloc_semaphore(f"s_tile_in{n}") for n in range(2)]
    w_in = nc.alloc_semaphore("s_win_in")
    turned = nc.alloc_semaphore("s_turned")
    moved_act = nc.alloc_semaphore("s_moved_act")
    moved_dve = nc.alloc_semaphore("s_moved_dve")
    scored = nc.alloc_semaphore("s_scored")
    taken = nc.alloc_semaphore("s_taken")
    v_kept = nc.alloc_semaphore("s_v_kept")
    vt = nc.alloc_semaphore("s_mix")
    FILLS = SLOTS // 4
    tensor = Steps(nc, "s_pe", ["cmp scores", "new scores", "cmp rows", "probT", "importance", "rows", "vc", "probabilities", "values"])
    vector = Steps(nc, "s_dve", ["cmp kept", "cmp max", "cmp p", "probT kept", "heads summed", "sel max", "win max",
                                 "sel p", "win p", "pT kept", "vc kept", "done"])
    scalar = Steps(nc, "s_act", ["cmp exp", "sel exp", "win exp"])
    own = nc.alloc_semaphore("s_link")

    with nc.Block() as block:
        @block.sync
        def _(sp):
            for n in range(2):
                if n:
                    sp.wait_ge(vt, n)
                sp.dma_start(k.wrows[:].rearrange("p b s c -> p b (s c)"),
                             k.dram["cache_kv_win"][0, NH2 * n:NH2 * n + NH2].rearrange("b (p s) x h d -> p b (s x h d)", p=P)
                             ).then_inc(w_in, 16)

        @block.gpsimd
        def _(pool):
            rows = k.dram["cache_kv_sel"][0].rearrange("n (r s) x h d -> (n r) (s x h d)", s=SUB)

            def gather(b):
                if b >= 2:
                    pool.wait_ge(turned, FILLS * (b - 1))
                pool.indirect_dma_start(tiles[b % 2][:].rearrange("p s c -> p (s c)"), None, rows,
                                        bass.IndirectOffsetOnAxis(ap=k.rows_of[:, b:b + 1], axis=0)
                                        ).then_inc(t_in[b % 2], 16)
            gather(0)
            for b in range(NB):
                if b + 1 < NB:
                    if b >= 1:
                        pool.wait_ge(v_kept, b)
                    gather(b + 1)

        @block.tensor
        def _(pe):
            for n in range(2):
                def fill(F):
                    b, f = F // FILLS, F % FILLS
                    if f == 0:
                        pe.wait_ge(t_in[b % 2], 16 * (b // 2 + 1))
                    if F == n * NH2 * FILLS:
                        pe.wait_ge(w_in, 16 * (n + 1))
                    if F >= 4:
                        pe.wait_ge(moved_act if F % 2 == 0 else moved_dve, (F - 4) // 2 + 1)
                    for a in range(4):
                        src = tiles[b % 2][:, 4 * f + a, 0:P] if f < 4 else k.wrows[:, b % NH2, a, 0:P]
                        mm = pe.transpose(k.ps[:, F % 4, a * P:a * P + P], src, k.ident[:])
                    mm.then_inc(turned, 1)

                def score(F):
                    b, f = F // FILLS, F % FILLS
                    if f == 0 and b >= 2:
                        pe.wait_ge(taken, b - 1)
                    pe.wait_ge(moved_act if F % 2 == 0 else moved_dve, F // 2 + 1)
                    for a in range(4):
                        slot = 4 * f + a
                        mm = pe.matmul(k.ps[:, 4 + b % 2, slot * NH:slot * NH + NH], k.keyT[:, F % 4, a, :], k.qsm[:, b, :],
                                       start=True, stop=True)
                    mm.then_inc(scored, 1)
                F0, F1 = n * NH2 * FILLS, (n + 1) * NH2 * FILLS
                if n:
                    vector.base -= len(vector.steps)
                    vector.wait(pe, "done")
                    vector.base += len(vector.steps)
                for F in range(F0, F1 + 2):
                    if F < F1:
                        fill(F)
                    if F >= F0 + 2:
                        score(F - 2)
                for b in range(NH2):
                    mm = pe.matmul(k.ps[0:NCMP, 6, b * NH:b * NH + NH], k.kcs[:, 0, NH2 * n + b, 0:NCMP],
                                   k.qsm[:, NH2 * n + b, :], start=True, stop=True)
                tensor.mark(mm, "cmp scores")
                q = k.qsm[:, NH2 * n:NH2 * n + NH2, :].rearrange("p b h -> p (b h)")
                for br in range(2):
                    mm = pe.matmul(k.ps[0:R, 7, br * NB:br * NB + NB], q, k.knT[:, br, :], start=True, stop=True)
                tensor.mark(mm, "new scores")
                vector.wait(pe, "cmp kept")
                tensor.mark(pe.transpose(k.ps[0:R, 6, 0:NCMP], k.scT[0:NCMP, :], k.ident[0:NCMP, 0:NCMP]), "cmp rows")
                vector.wait(pe, "cmp p")
                for a in range(2):
                    mm = pe.transpose(k.ps[0:NCMP, 5, a * R:a * R + R], k.pcs[:, a, 0:NCMP], k.ident[0:R, 0:R])
                tensor.mark(mm, "probT")
                vector.wait(pe, "heads summed")
                tensor.mark(pe.matmul(k.ps[0:R, 5, 0:NSEL], k.pcsT[0:NCMP, 2, :], k.smap[0:NCMP, :], start=True, stop=True),
                            "importance")
                pe.wait_ge(taken, NH2 * (n + 1))
                for slot in range(SLOTS):
                    mm = pe.transpose(k.ps[0:R, slot // 4, slot % 4 * P:slot % 4 * P + P], k.sT[:, slot, :], k.ident[:])
                tensor.mark(mm, "rows")
                for b in range(NH2):
                    mm = pe.transpose(k.ps[0:NCMP, 6, b * P:b * P + P], k.kcs[:, 1, NH2 * n + b, 0:NCMP], k.ident[:])
                tensor.mark(mm, "vc")
                vector.wait(pe, "win p")
                for slot in range(SLOTS):
                    src = k.sbuf[:, slot * P:slot * P + P] if slot < SUB else k.wbuf[:, (slot - SUB) * P:(slot - SUB + 1) * P]
                    mm = pe.transpose(k.ps[:, slot // 16, slot % 16 * R:slot % 16 * R + R], src, k.ident[0:R, 0:R])
                for br in range(2):
                    mm = pe.transpose(k.ps[0:NB, 2, br * R:br * R + R], k.sd[:, 2 + br, :], k.ident[0:R, 0:R])
                tensor.mark(mm, "probabilities")
                vector.wait(pe, "vc kept")
                pe.wait_ge(v_kept, NH2 * (n + 1))
                for b in range(NH2):
                    cols = slice(b * NH, b * NH + NH)
                    out = k.ps[:, 7, 64 + b * NH:64 + b * NH + NH]
                    for slot in range(SLOTS):
                        v = k.vrows[:, b, slot, :] if slot < SUB else k.wrows[:, b, slot - SUB, P:2 * P]
                        pe.matmul(out, v, k.pT[:, slot, cols], start=(slot == 0), stop=False)
                    pe.matmul(out, k.vcs[0:NCMP, b, :], k.pcsT[0:NCMP, 1, cols], start=False, stop=False)
                    for br in range(2):
                        mm = pe.matmul(out, k.kv[0:NB, NT, KVW * (1 + br) + P:KVW * (2 + br)], k.dT[:, br, cols],
                                       start=False, stop=(br == 1))
                tensor.mark(mm, "values")
                for st in (tensor, vector, scalar):
                    st.again()
        for st in (tensor, vector, scalar):
            st.base = 0

        @block.scalar
        def _(act):
            for n in range(2):
                for F in range(n * NH2 * FILLS, (n + 1) * NH2 * FILLS, 2):
                    act.wait_ge(turned, F + 1)
                    if F >= 4:
                        act.wait_ge(scored, F - 3)
                    act.activation(k.keyT[:, F % 4], k.ps[:, F % 4, :].rearrange("p (a q) -> p a q", a=4), ACT.Copy
                                   ).then_inc(moved_act, 1)
                    b = F // FILLS
                    if F - b * FILLS < 2:
                        act.wait_ge(t_in[b % 2], 16 * (b // 2 + 1))
                        if b == NH2:
                            act.wait_ge(vt, 1)
                        act.activation(k.vrows[:, b % NH2], tiles[b % 2][:, :, P:2 * P], ACT.Copy).then_inc(v_kept, 1)
                vector.wait(act, "cmp max")
                scalar.mark(act.activation(k.pcs[:, 0, 0:NCMP], k.ps[0:R, 6, 0:NCMP], ACT.Exp, bias=k.ss[:, 0, 1:2], scale=SCALE,
                                           accum_out=k.ss[:, 0, 2:3]), "cmp exp")
                vector.wait(act, "sel max")
                scalar.mark(act.activation(k.sbuf[:, 0:PAST + 1], k.sbuf[:, 0:PAST + 1], ACT.Exp, bias=k.ss[:, 1, 1:2],
                                           scale=SCALE, accum_out=k.ss[:, 1, 2:3]), "sel exp")
                vector.wait(act, "win max")
                scalar.mark(act.activation(k.wbuf[:, 0:WIN + 1], k.wbuf[:, 0:WIN + 1], ACT.Exp, bias=k.ss[:, 2, 1:2],
                                           scale=SCALE, accum_out=k.ss[:, 2, 2:3]), "win exp")
                for st in (tensor, vector, scalar):
                    st.again()
        for st in (tensor, vector, scalar):
            st.base = 0

        @block.vector
        def _(dve):
            links = [0]

            def link(ins):
                links[0] += 1
                ins.then_inc(own, 1)
                dve.wait_ge(own, links[0])

            for n in range(2):
                def take(b):
                    dve.wait_ge(scored, FILLS * (b + 1))
                    dve.tensor_copy(k.sT[:, :, b % NH2 * NH:(b % NH2 + 1) * NH],
                                    k.ps[:, 4 + b % 2, 0:SLOTS * NH].rearrange("p (s h) -> p s h", h=NH)).then_inc(taken, 1)
                for F in range(n * NH2 * FILLS + (n * NH2 * FILLS + 1) % 2, (n + 1) * NH2 * FILLS, 2):
                    dve.wait_ge(turned, F + 1)
                    if F >= 4:
                        dve.wait_ge(scored, F - 3)
                    dve.tensor_copy(k.keyT[:, F % 4], k.ps[:, F % 4, :].rearrange("p (a q) -> p a q", a=4)).then_inc(moved_dve, 1)
                    b = F // FILLS
                    if F % FILLS >= 3 and b > n * NH2 and (F - 2) // FILLS == b:
                        take(b - 1)
                take((n + 1) * NH2 - 1)

                def weight(br, row):
                    link(dve.reciprocal(k.ss[:, row, 3:4], k.ss[:, row, 2:3]))
                    link(dve.tensor_tensor(k.ss[:, row, 4:5], k.ss[:, row, 3:4], k.grow[:, n, br:br + 1], ALU.mult))

                tensor.wait(dve, "cmp scores")
                vector.mark(dve.tensor_copy(k.scT[0:NCMP, :], k.ps[0:NCMP, 6, 0:R]), "cmp kept")
                tensor.wait(dve, "cmp rows")
                link(dve.tensor_reduce(k.ss[:, 0, 0:1], k.ps[0:R, 6, 0:NCMP], AX.X, ALU.max))
                vector.mark(dve.tensor_scalar(k.ss[:, 0, 1:2], k.ss[:, 0, 0:1], -SCALE, None, ALU.mult), "cmp max")
                scalar.wait(dve, "cmp exp")
                weight(0, 0)
                dve.tensor_scalar(k.pcs[:, 1, 0:NCMP], k.pcs[:, 0, 0:NCMP], k.ss[:, 0, 4:5], None, ALU.mult)
                vector.mark(dve.tensor_scalar(k.pcs[:, 0, 0:NCMP], k.pcs[:, 0, 0:NCMP], k.ss[:, 0, 3:4], None, ALU.mult), "cmp p")
                tensor.wait(dve, "probT")
                ins = dve.tensor_copy(k.pcsT[0:NCMP, 0:2, :].rearrange("p a r -> p (a r)"), k.ps[0:NCMP, 5, 0:2 * R])
                vector.mark(ins, "probT kept")
                vector.wait(dve, "probT kept")
                link(dve.tensor_reduce(k.scT[0:NCMP, 0:R // GQA], k.pcsT[0:NCMP, 0, :].rearrange("p (a g) -> p a g", g=GQA),
                                       AX.X, ALU.add))
                vector.mark(dve.tensor_copy(k.pcsT[0:NCMP, 2, :].rearrange("p (a g) -> p a g", g=GQA),
                                            bc(k.scT[0:NCMP, 0:R // GQA], 2, GQA)), "heads summed")
                tensor.wait(dve, "new scores")
                for br in range(2):
                    link(dve.tensor_tensor(k.sd[:, br], k.ps[0:R, 7, br * NB:br * NB + NB], k.diag[:, n], ALU.mult))
                link(dve.tensor_reduce(k.sbuf[:, PAST:PAST + 1], k.sd[:, 0], AX.X, ALU.add))
                link(dve.tensor_reduce(k.wbuf[:, WIN:WIN + 1], k.sd[:, 1], AX.X, ALU.add))
                tensor.wait(dve, "importance")
                link(dve.tensor_copy(k.imp[:, 0, 0:NSEL], k.ps[0:R, 5, 0:NSEL]))
                link(dve.memset(k.imp[:, 0, 0:NSEL:NSEL - 1], -NEG))
                link(dve.max(k.m8[:, 0], k.imp[:, 0, 0:NSEL]))
                link(dve.match_replace(k.imp[:, 1, 0:NSEL], k.m8[:, 0], k.imp[:, 0, 0:NSEL], -1.0))
                link(dve.max(k.m8[:, 1], k.imp[:, 1, 0:NSEL]))
                link(dve.match_replace(k.imp[:, 2, 0:NSEL], k.m8[:, 1], k.imp[:, 1, 0:NSEL], -1.0))
                link(dve.tensor_scalar(k.imp[:, 3, 0:NSEL], k.imp[:, 2, 0:NSEL], -1.0, None, ALU.is_equal))
                link(dve.tensor_scalar(k.imp[:, 3, 0:NSEL], k.imp[:, 3, 0:NSEL], 1.0, -NEG, ALU.subtract, ALU.mult))
                tensor.wait(dve, "rows")
                link(dve.tensor_tensor(k.sbuf[:, 0:PAST].rearrange("r (s a b) -> r s a b", s=SUB, b=4),
                                       k.ps[0:R, 0:4, :].rearrange("r k (s n) -> r (k s) n", s=4).rearrange("r s (a b) -> r s a b", b=4),
                                       bc(bc(k.imp[:, 3, 0:NSEL - 1], 1, SUB), 3, 4), ALU.add))
                link(dve.tensor_reduce(k.ss[:, 1, 0:1], k.sbuf[:, 0:PAST + 1], AX.X, ALU.max))
                vector.mark(dve.tensor_scalar(k.ss[:, 1, 1:2], k.ss[:, 1, 0:1], -SCALE, None, ALU.mult), "sel max")
                link(dve.tensor_copy(k.wbuf[:, 0:WIN], k.ps[0:R, 4, :]))
                link(dve.tensor_reduce(k.ss[:, 2, 0:1], k.wbuf[:, 0:WIN + 1], AX.X, ALU.max))
                vector.mark(dve.tensor_scalar(k.ss[:, 2, 1:2], k.ss[:, 2, 0:1], -SCALE, None, ALU.mult), "win max")
                for br, (buf, last, name) in enumerate(((k.sbuf, PAST, "sel"), (k.wbuf, WIN, "win"))):
                    scalar.wait(dve, name + " exp")
                    weight(br + 1, br + 1)
                    link(dve.tensor_scalar(buf[:, 0:last + 1], buf[:, 0:last + 1], k.ss[:, br + 1, 4:5], None, ALU.mult))
                    vector.mark(dve.tensor_scalar(k.sd[:, 2 + br], k.diag[:, n], buf[:, last:last + 1], None, ALU.mult), name + " p")
                tensor.wait(dve, "probabilities")
                dve.tensor_copy(k.pT[:, 0:SUB].rearrange("p s r -> p (s r)"), k.ps[:, 0, :])
                dve.tensor_copy(k.pT[:, SUB:SLOTS].rearrange("p s r -> p (s r)"), k.ps[:, 1, 0:4 * R])
                vector.mark(dve.tensor_copy(k.dT[:].rearrange("b a r -> b (a r)"), k.ps[0:NB, 2, 0:2 * R]), "pT kept")
                vector.mark(dve.tensor_copy(k.vcs[0:NCMP].rearrange("p b r -> p (b r)"), k.ps[0:NCMP, 6, :]), "vc kept")
                tensor.wait(dve, "values")
                for h in range(NH):
                    src = k.ps[HD * (h // GQA):HD * (h // GQA) + HD, 7, 64:64 + R].rearrange("d (b h) -> d b h", h=NH)[:, :, h]
                    ins = dve.tensor_copy(k.mixT[HD * (h % 2):HD * (h % 2) + HD, h // 2, SEQ + NH2 * n:SEQ + NH2 * n + NH2], src)
                vector.mark(ins, "done")
                vector.wait(dve, "done")
                dve.sem_inc(vt, 1)
                for st in (tensor, vector, scalar):
                    st.again()


def cmul(link, dve, out, a, b, tmp, conj=False):
    link(dve.tensor_tensor(tmp[0], a[0], b[0], ALU.mult))
    link(dve.tensor_tensor(tmp[1], a[1], b[1], ALU.mult))
    link(dve.tensor_tensor(out[0], tmp[0], tmp[1], ALU.add if conj else ALU.subtract))
    link(dve.tensor_tensor(tmp[0], a[0], b[1], ALU.mult))
    link(dve.tensor_tensor(tmp[1], a[1], b[0], ALU.mult))
    link(dve.tensor_tensor(out[1], tmp[0], tmp[1], ALU.subtract if conj else ALU.add))


def plan_ssm(nc, k):
    at = k.at
    k.BT, o = at("BT", [P, 2, NJ, P], F32, k.off_q)
    k.CW, o = at("CW", [P, 2, NJ, CH + 1, GC], F32, o)
    k.TZ, o = at("TZ", [P, G, P], F32, o)
    k.uc, o = at("uc", [P, G, NCH], F32, o)
    k.off_z = o
    k.Z, o = at("Z", [P, 2, NJ, NCH], F32, o)
    k.H, _ = at("H", [P, 2, NJ, NCH + 1], F32, k.off_z)
    k.Bw, _ = at("Bw", [P, 2, NJ, CH, GC], F32, k.off_z)
    k.H_end, o = at("H_end", [P, 2], F32, k.off_z + 2 * NJ * (NCH + 1) * 4)
    k.KK, _ = at("KK", [GC, G, P], F32, k.off_u)
    k.off_tt = o
    k.tt, o = at("tt", [P, 2, NJ, NCH], F32, o)
    k.decay, o = at("decay", [P, NJ, NCH], F32, o)
    k.E, _ = at("E", [P, 2, NJ, NCH], F32, k.off_mix + 4 * TOK * 4)
    k.PB, o = at("PB", [P, 11, NJ], F32, o)
    k.pw, o = at("pw", [P, 2, CH + 1, NJ], F32, o)
    k.ph, o = at("ph", [P, 2, 2, NJ], F32, o)
    k.h0, o = at("h0", [P, 2, NB * NJ], F32, o)
    k.h1, o = at("h1", [P, 2, NJ * NB], F32, o)
    k.usT, o = at("usT", [GC, G, NB], F32, o)
    k.K0, o = at("K0", [GC, G, GC], F32, o)
    k.Bb, o = at("Bb", [P, 2, NJ, GC], F32, o)
    k.off_ssm_end = o
    k.Bin, _ = at("Bin", [P, 2, NJ, GC], F32, k.off_tt + 2 * NJ * NCH * 4)
    k.dd, _ = at("dd", [GC, G, GC], F32, k.off_q)
    k.PA, o = at("PA", [NJ, 20, P], F32, k.off_tt)


def stage_ssm_parameters(nc, k):
    at = k.at
    k.Cin, _ = at("Cin", [GC, 2, G, PS], F32, k.off_mix + 4 * TOK * 4)
    ldt_in = nc.alloc_semaphore("p_in")
    b_in = nc.alloc_semaphore("b_in")
    h_in = nc.alloc_semaphore("h_in")
    sined = nc.alloc_semaphore("sined")
    to_sine = nc.alloc_semaphore("to_sine")
    params = nc.alloc_semaphore("params")
    formed = nc.alloc_semaphore("formed")
    PAR, C_T, H_T, B_T = 1, 2, 3, 4
    made = nc.alloc_semaphore("bc_made")
    phased = nc.alloc_semaphore("phased")
    hb_kept = nc.alloc_semaphore("hb_kept")
    k.hrow, _ = at("hrow", [P, 2, P], F32, k.off_z + 2 * NJ * NCH * 4 - 1024)
    k.dcol, _ = at("dcol", [GC, G], F32, k.off_ssm_end)
    k.ldt, _ = at("ldt", [NJ, 2], F32, k.off_ssm_end + 128)
    DT, X, MAG, TH, COS, SIN, ABR, ABI, FR, FI, DEN, ZR, T0, T1, T2, ARE, AIM = range(17)
    k.pt, _ = at("pt", [P, 2, NJ], F32, k.off_ssm_end + 256)
    SHORT = (ABR, ABI, FR, FI, MAG, COS, SIN)
    with nc.Block() as block:
        @block.sync
        def _(sp):
            for n, a in ((ARE, k.dram["ssm_a_re"]), (AIM, k.dram["ssm_a_im"])):
                sp.dma_start(k.PA[:, n], a[0].rearrange("(j g) p -> j (g p)", g=2)).then_inc(ldt_in, 16)
            sp.dma_start(k.ldt[:], k.dram["ssm_log_dt"][0].rearrange("(j g) -> j g", g=2)).then_inc(ldt_in, 16)
            for n, c in enumerate((k.dram["ssm_c_re"], k.dram["ssm_c_im"])):
                sp.dma_start(k.Cin[:, n], c[0].rearrange("g c p -> c g p")).then_inc(b_in, 16)
            for n, b in enumerate((k.dram["ssm_b_re"], k.dram["ssm_b_im"])):
                for g2 in range(2):
                    sp.dma_start(k.Bin[PS * g2:PS * g2 + PS, n], b[0, g2::2].rearrange("j p c -> p j c")).then_inc(b_in, 16)
            for n, h in enumerate((k.dram["state_ssm_re"], k.dram["state_ssm_im"])):
                sp.dma_start(k.hrow[:, n], h[0].rearrange("b (j g) p -> (b j) (g p)", g=2)).then_inc(h_in, 16)
            sp.dma_start(k.dcol[:], k.dram["ssm_d"][0].rearrange("(g c) -> c g", c=GC), allow_slow_non_contiguous=True).then_inc(h_in, 16)

        @block.scalar
        def _(act):
            act.wait_ge(ldt_in, 48)
            act.activation(k.ldt[:], k.ldt[:], ACT.Exp).then_inc(sined, 1)
            act.wait_ge(to_sine, 1)
            act.activation(k.PA[:, MAG], k.PA[:, X], ACT.Exp).then_inc(sined, 1)
            act.wait_ge(to_sine, 2)
            act.activation(k.PA[:, SIN], k.PA[:, T2], ACT.Sin)
            act.activation(k.PA[:, T1], k.PA[:, T2], ACT.Sin, scale=0.5).then_inc(sined, 1)
            act.wait_ge(formed, H_T)
            act.activation(k.h0[:].rearrange("p a b -> p (a b)"), k.ps[:, 7, 0:2 * P], ACT.Copy).then_inc(hb_kept, 1)
            act.wait_ge(formed, B_T)
            for n in range(2):
                act.activation(k.BT[:, n].rearrange("p (x a) q -> p x (a q)", x=4), k.ps[:, 4 * n:4 * n + 4, :], ACT.Copy
                               ).then_inc(hb_kept, 1)

        @block.tensor
        def _(pe):
            pe.wait_ge(params, 1)
            for n, q in enumerate(SHORT):
                mm = pe.transpose(k.ps[:, 0, n * NJ:n * NJ + NJ], k.PA[:, q], k.ident[0:NJ, 0:NJ])
            mm.then_inc(formed, 1)
            pe.wait_ge(b_in, 16 * 6)
            for n in range(2):
                for j in range(NJ):
                    mm = pe.transpose(k.ps[:, 1 + n, j * GC:j * GC + GC], k.Cin[:, n, 2 * j:2 * j + 2].rearrange("c g p -> c (g p)"),
                                      k.ident[0:GC, 0:GC])
            mm.then_inc(formed, 1)
            pe.wait_ge(h_in, 48)
            for n in range(2):
                mm = pe.transpose(k.ps[:, 7, n * P:n * P + P], k.hrow[:, n], k.ident[:])
            mm.then_inc(formed, 1)
            pe.wait_ge(made, 2)
            pe.wait_ge(hb_kept, 1)
            for n in range(2):
                for j in range(NJ):
                    mm = pe.transpose(k.ps[:, 4 * n + j // 4, j % 4 * P:j % 4 * P + P],
                                      k.Bw[:, n, j].rearrange("p s c -> p (s c)"), k.ident[:])
            mm.then_inc(formed, 1)

        @block.gpsimd
        def _(pool):
            e_link = Link(nc, pool, "e_link")
            pool.wait_ge(phased, 1)
            pool.wait_ge(formed, C_T)
            E = [k.E[:, n] for n in range(2)]
            tmp = [k.TZ[:, 16 * n:16 * n + 16].rearrange("p g q -> p (g q)")[:, 0:NJ * PS].rearrange("p (j c) -> p j c", c=PS) for n in range(2)]
            pool.memset(k.E[:, 0, :, 0:1], 1.0)
            e_link(pool.memset(k.E[:, 1, :, 0:1], 0.0))
            cur = [k.ph[:, 0, n] for n in range(2)]
            for m in range(7):
                w = 1 << m
                cmul(e_link, pool, [e[:, :, w:2 * w] for e in E], [e[:, :, 0:w] for e in E], [bc(c, 2, w) for c in cur],
                     [t[:, :, 0:w] for t in tmp])
                nxt = [k.ph[:, (m + 1) % 2, n] for n in range(2)]
                cmul(e_link, pool, nxt, cur, cur, [k.pt[:, n] for n in range(2)])
                cur = nxt
            e_link(pool.memset(k.TZ[:], 0.0))

        @block.vector
        def _(dve):
            link = Link(nc, dve, "p_link")

            def t(n):
                return k.PA[:, n]

            def tt(o, a, b, op):
                link(dve.tensor_tensor(t(o), t(a), t(b), op))
            MAGIC, TWO_PI = 1.5 * 2.0 ** 23, 6.283185307179586
            C1 = 6.28125
            C2 = 0.0019350051879882812
            C3 = TWO_PI - C1 - C2
            PI = 3.1415925
            dve.wait_ge(sined, 1)
            for dst, a in ((X, ARE), (TH, AIM)):
                ins = dve.tensor_tensor(t(dst).rearrange("j (g p) -> j g p", g=2), t(a).rearrange("j (g p) -> j g p", g=2),
                                        bc(k.ldt[:], 2, PS), ALU.mult)
                if dst == X:
                    ins.then_inc(to_sine, 1)
                else:
                    link(ins)
            link(dve.tensor_scalar(t(T0), t(TH), 1 / TWO_PI, MAGIC, ALU.mult, ALU.add))
            link(dve.tensor_scalar(t(T0), t(T0), MAGIC, None, ALU.subtract))
            link(dve.scalar_tensor_tensor(t(T1), t(T0), -C1, t(TH), ALU.mult, ALU.add))
            link(dve.scalar_tensor_tensor(t(T2), t(T0), -C2, t(T1), ALU.mult, ALU.add))
            link(dve.scalar_tensor_tensor(t(T1), t(T0), -C3, t(T2), ALU.mult, ALU.add))
            dve.tensor_scalar(t(T2), t(T1), PI, -PI, ALU.min, ALU.max).then_inc(to_sine, 1)
            dve.wait_ge(sined, 3)
            tt(T0, T1, T1, ALU.mult)
            link(dve.tensor_scalar(t(COS), t(T0), -2.0, 1.0, ALU.mult, ALU.add))
            tt(ABR, MAG, COS, ALU.mult)
            tt(ABI, MAG, SIN, ALU.mult)
            tt(T0, ARE, ARE, ALU.mult)
            tt(T1, AIM, AIM, ALU.mult)
            tt(T2, T0, T1, ALU.add)
            link(dve.reciprocal(t(DEN), t(T2)))
            link(dve.tensor_scalar(t(ZR), t(ABR), 1.0, None, ALU.subtract))
            tt(T0, ZR, ARE, ALU.mult)
            tt(T1, ABI, AIM, ALU.mult)
            tt(T2, T0, T1, ALU.add)
            tt(FR, T2, DEN, ALU.mult)
            tt(T0, ABI, ARE, ALU.mult)
            tt(T1, ZR, AIM, ALU.mult)
            tt(T2, T0, T1, ALU.subtract)
            dve.tensor_tensor(t(FI), t(T2), t(DEN), ALU.mult).then_inc(params, 1)
            dve.wait_ge(formed, PAR)
            B = lambda n: k.PB[:, n]
            link(dve.tensor_copy(k.PB[:, 0:7].rearrange("p a j -> p (a j)"), k.ps[:, 0, 0:7 * NJ]))
            dve.memset(k.pw[:, 0, 0], 1.0)
            dve.memset(k.pw[:, 1, 0], 0.0)
            dve.tensor_copy(k.pw[:, 0, 1], B(0))
            link(dve.tensor_copy(k.pw[:, 1, 1], B(1)))
            for m in (1, 2, 4):
                a = [k.pw[:, n, 1:m + 1] for n in range(2)]
                b = [bc(k.pw[:, n, m], 1, m) for n in range(2)]
                tmp = [k.tt[:, n].rearrange("p j c -> p (j c)")[:, 1024:1024 + m * NJ].rearrange("p (a j) -> p a j", j=NJ) for n in range(2)]
                cmul(link, dve, [k.pw[:, n, m + 1:2 * m + 1] for n in range(2)], a, b, tmp)
            for n in (4,):
                link(dve.tensor_tensor(B(7), B(4), B(4), ALU.mult))
                link(dve.tensor_tensor(B(8), B(7), B(7), ALU.mult))
                link(dve.tensor_tensor(B(4), B(8), B(8), ALU.mult))
            cur = [B(5), B(6)]
            for m in range(3):
                nxt = [k.ph[:, m % 2, n] for n in range(2)]
                cmul(link, dve, nxt, cur, cur, [B(7), B(8)])
                cur = nxt
            dve.sem_inc(phased, 1)
            dve.wait_ge(b_in, 16 * 6)
            shape = [P, NJ, GC]
            tmp = [k.tt[:, n].rearrange("p j c -> p (j c)")[:, 1024:1024 + NJ * GC].rearrange("p (j c) -> p j c", c=GC) for n in range(2)]
            cmul(link, dve, [k.Bb[:, n] for n in range(2)], [bc(B(2 + n), 2, GC) for n in range(2)], [k.Bin[:, n] for n in range(2)], tmp)
            dve.wait_ge(formed, H_T)
            big = [k.tt[:, n].rearrange("p j (s c) -> p j s c", s=CH) for n in range(2)]

            def powers(n, first):
                return bc(k.pw[:, n, first:first + CH].rearrange("p s j -> p j s"), 3, GC)
            cmul(link, dve, [k.Bw[:, n] for n in range(2)], [powers(n, 0) for n in range(2)],
                 [bc(k.Bb[:, n], 2, CH) for n in range(2)], big)
            dve.sem_inc(made, 1)
            dve.wait_ge(formed, C_T)
            link(dve.tensor_copy(k.Bin[:].rearrange("p a j c -> p a (j c)"), k.ps[:, 1:3, 0:NJ * GC]))
            dve.tensor_copy(k.CW[:, 0, :, 0], k.Bin[:, 0])
            dve.tensor_scalar(k.CW[:, 1, :, 0], k.Bin[:, 1], -1.0, None, ALU.mult)
            cmul(link, dve, [k.CW[:, n, :, 1:] for n in range(2)], [powers(n, 1) for n in range(2)],
                 [bc(k.Bin[:, n], 2, CH) for n in range(2)], big)
            link(dve.tensor_scalar(k.CW[:, 1, :, 1:], k.CW[:, 1, :, 1:], -1.0, None, ALU.mult))
            dve.sem_inc(made, 1)


def stage_ssm_states(nc, k):
    uc_turned = nc.alloc_semaphore("uc_turned")
    uc_kept = nc.alloc_semaphore("uc_kept")
    bu = nc.alloc_semaphore("bu")
    bu_kept = nc.alloc_semaphore("bu_kept")
    bus = nc.alloc_semaphore("bus")
    ends_made = nc.alloc_semaphore("ends_made")
    ends_turned = nc.alloc_semaphore("ends_turned")
    ends_kept = nc.alloc_semaphore("ends_kept")
    decayed = nc.alloc_semaphore("decayed")
    ssm_out = nc.alloc_semaphore("ssm_out")
    at = k.at
    k.ends, _ = at("ends", [P, 3, 2, P], F32, k.off_tt)
    k.stores.append((ssm_out, 64))
    kk_ready = nc.alloc_semaphore("kk_ready")
    tz_in = nc.alloc_semaphore("tz_in")
    kk_kept = nc.alloc_semaphore("kk_kept")
    with nc.Block() as block:
        @block.sync
        def _(sp):
            sp.wait_ge(kk_kept, 5)
            for s in range(CH):
                sp.dma_start(k.TZ[GC * s:GC * s + GC, :, (CH - 1 - s) * GC:], k.KK[:, :, 0:(s + 1) * GC]).then_inc(tz_in, 16)
            sp.wait_ge(tz_in, 16 * CH)

        @block.tensor
        def _(pe):
            for x in range(8):
                for a in range(4):
                    mm = pe.transpose(k.ps[:, x, a * P:a * P + P],
                                      k.U[:].rearrange("p g s c -> p (g s c)")[:, (4 * x + a) * P:(4 * x + a + 1) * P], k.ident[:])
                mm.then_inc(uc_turned, 1)
            pe.wait_ge(uc_kept, 8)
            for g in range(G):
                mm = pe.transpose(k.ps[0:GC, 0, g * NB:g * NB + NB], k.us[:, g * GC:g * GC + GC], k.ident[0:NB, 0:NB])
            mm.then_inc(uc_turned, 1)
            pe.wait_ge(uc_kept, 9)
            for n in range(2):
                for j in range(NJ):
                    for g2 in range(2):
                        mm = pe.matmul(k.ps[PS * g2:PS * g2 + PS, 4 * n + j // 4, j % 4 * P:j % 4 * P + P],
                                       k.BT[:, n, j, PS * g2:PS * g2 + PS], k.uc[:, 2 * j + g2, :], start=True, stop=True)
            mm.then_inc(bu, 1)
            pe.wait_ge(bu_kept, 1)
            for n in range(2):
                for j in range(NJ):
                    for g2 in range(2):
                        c = (n * NJ + j) * NB
                        mm = pe.matmul(k.ps[PS * g2:PS * g2 + PS, 0, c:c + NB], k.BT[0:GC, n, j, PS * g2:PS * g2 + PS],
                                       k.usT[:, 2 * j + g2, :], start=True, stop=True)
            mm.then_inc(bus, 1)
            for x in range(4):
                if x >= 2:
                    pe.wait_ge(kk_kept, x - 1)
                for a in range(4):
                    for g2 in range(2):
                        half = slice(PS * g2, PS * g2 + PS)
                        for n in range(2):
                            mm = pe.matmul(k.ps[0:GC, 4 + 2 * (x % 2) + g2, a * P:a * P + P], k.Bb[half, n, 4 * x + a],
                                           k.CW[half, n, 4 * x + a, 0:CH].rearrange("p s c -> p (s c)"), start=(n == 0), stop=(n == 1))
                mm.then_inc(kk_ready, 1)
            pe.wait_ge(ends_made, 1)
            for n in range(2):
                pe.transpose(k.ps[0:NJ, 1, n * P:n * P + P], k.ends[:, 2, n, 0:NJ], k.ident[:])
            for n in range(2):
                mm = pe.transpose(k.ps[:, 2, n * P:n * P + P], k.ends[:, 0, n, :], k.ident[:])
            mm.then_inc(ends_turned, 1)

        @block.gpsimd
        def _(pool):
            pool.tensor_copy(k.decay[:], bc(k.PB[:, 4], 2, NCH)).then_inc(decayed, 1)
            pool.wait_ge(decayed, 1)
            pool.memset(k.decay[:, :, 0:1], 0.0).then_inc(decayed, 1)

        @block.scalar
        def _(act):
            for x in range(8):
                act.wait_ge(uc_turned, x + 1)
                act.activation(k.uc[:, 4 * x:4 * x + 4, :].rearrange("p g n -> p (g n)"), k.ps[:, x, :], ACT.Copy).then_inc(uc_kept, 1)
            act.wait_ge(uc_turned, 9)
            act.activation(k.usT[:].rearrange("c g b -> c (g b)"), k.ps[0:GC, 0, 0:G * NB], ACT.Copy).then_inc(uc_kept, 1)
            for x in range(4):
                act.wait_ge(kk_ready, x + 1)
                act.activation(k.KK[:, 8 * x:8 * x + 8].rearrange("c (a g) q -> c g a q", g=2),
                               k.ps[0:GC, 4 + 2 * (x % 2):6 + 2 * (x % 2), :].rearrange("c g (a q) -> c g a q", a=4), ACT.Copy
                               ).then_inc(kk_kept, 1)
            act.wait_ge(ends_turned, 1)
            act.activation(k.ends[0:NJ, 1], k.ps[0:NJ, 1, 0:2 * P].rearrange("p (n q) -> p n q", n=2), ACT.Copy).then_inc(ends_kept, 1)
            act.wait_ge(ends_kept, 1)
            for n, out in enumerate((k.dram["p_ssm_re"], k.dram["p_ssm_im"])):
                act.dma_start(out[0, 0].rearrange("(j g) p -> j (g p)", g=2), k.ends[0:NJ, 1, n]).then_inc(ssm_out, 16)
            act.activation(k.ends[:, 2], k.ps[:, 2, 0:2 * P].rearrange("p (n q) -> p n q", n=2), ACT.Copy).then_inc(ends_kept, 1)
            act.wait_ge(ends_kept, 2)
            for n, out in enumerate((k.dram["s_ssm_re"], k.dram["s_ssm_im"])):
                act.dma_start(out[0].rearrange("b (j g) p -> (b j) (g p)", g=2), k.ends[:, 2, n]).then_inc(ssm_out, 16)
            act.wait_ge(ssm_out, 64)

        @block.vector
        def _(dve):
            link = Link(nc, dve, "st_link")
            E = [k.E[:, n] for n in range(2)]
            tmp = [k.tt[:, n] for n in range(2)]
            dve.wait_ge(bu, 1)
            S = [k.ps[:, 4 * n:4 * n + 4, :].rearrange("p x (a c) -> p (x a) c", c=NCH) for n in range(2)]
            Z = [k.Z[:, n] for n in range(2)]
            cmul(link, dve, Z, E, S, tmp, conj=True)
            dve.sem_inc(bu_kept, 1)
            dve.wait_ge(decayed, 2)
            flat = lambda a: a.rearrange("p j c -> p (j c)")
            for n in range(2):
                link(dve.tensor_tensor_scan(flat(tmp[n]), flat(k.decay[:]), flat(Z[n]), 0.0, ALU.mult, ALU.add))
            H = [k.H[:, n, :, 1:] for n in range(2)]
            link(dve.tensor_tensor(k.decay[:], E[0], tmp[0], ALU.mult))
            link(dve.tensor_tensor(H[0], E[1], tmp[1], ALU.mult))
            link(dve.tensor_tensor(H[0], k.decay[:], H[0], ALU.subtract))
            link(dve.tensor_tensor(k.decay[:], E[0], tmp[1], ALU.mult))
            link(dve.tensor_tensor(H[1], E[1], tmp[0], ALU.mult))
            link(dve.tensor_tensor(H[1], k.decay[:], H[1], ALU.add))
            link(dve.memset(k.H[:, :, :, 0:1], 0.0))
            dve.wait_ge(bus, 1)
            h0 = [k.h0[:, n].rearrange("p (b j) -> p b j", j=NJ) for n in range(2)]
            A = [bc(k.PB[:, n], 1, NB) for n in range(2)]
            h1 = [k.h1[:, n].rearrange("p (b j) -> p b j", j=NJ) for n in range(2)]
            t2 = [k.decay[:, n].rearrange("p (b j) -> p b j", j=NJ) for n in range(2)]
            cmul(link, dve, h1, A, h0, t2)
            for n in range(2):
                link(dve.tensor_tensor(k.ends[:, 0, n].rearrange("p (b j) -> p b j", j=NJ), h1[n],
                                       k.ps[:, 0, n * P:n * P + P].rearrange("p (j b) -> p b j", b=NB), ALU.add))
            link(dve.tensor_copy(k.ends[:, 2, :, 0:NJ], k.H[:, :, :, NCH]))
            dve.sem_inc(ends_made, 1)
            dve.wait_ge(kk_kept, 4)
            link(dve.tensor_tensor(k.dd[:], bc(k.ident[0:GC, 0:GC], 1, G), bc(k.dcol[:], 2, GC), ALU.mult))
            link(dve.tensor_tensor(k.K0[:], k.KK[:, :, 0:GC], k.dd[:], ALU.add))
            dve.tensor_copy(k.KK[:, :, 0:GC], k.K0[:]).then_inc(kk_kept, 1)


def stage_ssm_outputs(nc, k):
    at = k.at
    k.Y, _ = at("Y", [P, CH, SSMW], F32, k.off_u)
    k.gT, o = at("gT", [P, 4, TOK], F32, k.off_z + 2 * NJ * (NCH + 1) * 4)
    k.ys, o = at("ys", [NB, SSMW], F32, o)
    k.w_glu_sb, _ = at("w_glu_sb", [P, 4, 2 * SSMW], F32, k.off_q)
    k.sig, _ = at("sig", [P, 2, TOK], F32, k.off_q + 16384)
    y_ready = nc.alloc_semaphore("y_ready")
    y_act = nc.alloc_semaphore("y_act")
    g_turned = nc.alloc_semaphore("g_turned")
    g_act = nc.alloc_semaphore("g_act")
    g_dve = nc.alloc_semaphore("g_dve")
    w_in = nc.alloc_semaphore("w_glu_in")
    glu = nc.alloc_semaphore("glu")
    sigm = nc.alloc_semaphore("sigm")
    glu_out = nc.alloc_semaphore("glu_out")
    with nc.Block() as block:
        @block.sync
        def _(sp):
            sp.dma_start(k.w_glu_sb[:], k.dram["w_glu"][0].rearrange("(a p) n -> p a n", p=P)).then_inc(w_in, 16)

        @block.tensor
        def _(pe):
            for x in range(4):
                for g2 in range(2):
                    for a in range(4):
                        j = 4 * x + a
                        half = slice(PS * g2, PS * g2 + PS)
                        out = k.ps[:, 2 * x + g2, a * P:a * P + P]
                        pe.matmul(out, k.uc[:, 2 * j + g2, :], k.TZ[:, 2 * j + g2, :], start=True, stop=False)
                        for n in range(2):
                            mm = pe.matmul(out, k.H[half, n, j, 0:NCH], k.CW[half, n, j, 1:].rearrange("p s c -> p (s c)"),
                                           start=False, stop=(n == 1))
                    mm.then_inc(y_ready, 1)
            pe.wait_ge(y_act, 2)
            for g2 in range(2):
                for j in range(NJ):
                    half = slice(PS * g2, PS * g2 + PS)
                    out = k.ps[0:NB, g2, j * GC:j * GC + GC]
                    pe.matmul(out, k.usT[:, 2 * j + g2, :], k.K0[:, 2 * j + g2, :], start=True, stop=False)
                    for n in range(2):
                        mm = pe.matmul(out, k.h0[half, n, j::NJ], k.CW[half, n, j, 1], start=False, stop=(n == 1))
                mm.then_inc(y_ready, 1)
            pe.wait_ge(y_act, 10)
            for t in range(CH):
                for a in range(4):
                    mm = pe.transpose(k.ps[:, t, a * P:a * P + P], k.Y[:, t, a * P:a * P + P], k.ident[:])
                mm.then_inc(g_turned, 1)
            pe.wait_ge(g_act, 1)
            for a in range(4):
                mm = pe.transpose(k.ps[:, 0, a * NB:a * NB + NB], k.ys[:, a * P:a * P + P], k.ident[0:NB, 0:NB])
            mm.then_inc(g_turned, 1)
            pe.wait_ge(w_in, 16)
            pe.wait_ge(g_act, 4)
            pe.wait_ge(g_dve, 5)
            for b in range(4):
                if b:
                    pe.wait_ge(glu_out, b)
                for z in range(2):
                    for a in range(4):
                        for c in range(3):
                            mm = pe.matmul(k.ps[:, 4 * z + c, 0:TG], k.w_glu_sb[:, a, z * SSMW + b * P:z * SSMW + (b + 1) * P],
                                           k.gT[:, a, c * TG:c * TG + TG], start=(a == 0), stop=(a == 3))
                mm.then_inc(glu, 1)

        @block.scalar
        def _(act):
            Y = k.Y[:].rearrange("p t (x a g c) -> p x g a t c", x=4, a=4, g=2)
            for x in range(4):
                for g2 in range(2):
                    act.wait_ge(y_ready, 2 * x + g2 + 1)
                    for a in range(4):
                        ins = act.activation(Y[:, x, g2, a], k.ps[:, 2 * x + g2, a * P:a * P + P].rearrange("p (t c) -> p t c", c=GC),
                                             ACT.Gelu_apprx_tanh)
                    ins.then_inc(y_act, 1)
            for g2 in range(2):
                act.wait_ge(y_ready, 9 + g2)
                act.activation(k.ys[:].rearrange("b (j g c) -> b g j c", g=2, c=GC)[:, g2],
                               k.ps[0:NB, g2, 0:NJ * GC].rearrange("b (j c) -> b j c", c=GC), ACT.Gelu_apprx_tanh).then_inc(y_act, 1)
            for t in range(0, CH, 2):
                act.wait_ge(g_turned, t + 1)
                act.activation(k.gT[:, :, t:SEQ:CH], k.ps[:, t, :].rearrange("p (a n) -> p a n", a=4), ACT.Copy).then_inc(g_act, 1)
            for b in range(4):
                act.wait_ge(glu, b + 1)
                if b >= 2:
                    act.wait_ge(glu_out, b - 1)
                act.activation(k.sig[:, b % 2].rearrange("p (c t) -> p c t", c=3), k.ps[:, 4:7, 0:TG], ACT.Sigmoid,
                               bias=k.vcol[:, 28 + b:29 + b]).then_inc(sigm, 1)

        @block.vector
        def _(dve):
            for t in range(1, CH, 2):
                dve.wait_ge(g_turned, t + 1)
                dve.tensor_copy(k.gT[:, :, t:SEQ:CH], k.ps[:, t, :].rearrange("p (a n) -> p a n", a=4)).then_inc(g_dve, 1)
            dve.wait_ge(g_turned, CH + 1)
            dve.tensor_copy(k.gT[:, :, SEQ:TOK], k.ps[:, 0, 0:4 * NB].rearrange("p (a n) -> p a n", a=4)).then_inc(g_dve, 1)
            for b in range(4):
                dve.wait_ge(sigm, b + 1)
                dve.scalar_tensor_tensor(k.mixT[:, 4 + b].rearrange("p (c t) -> p c t", c=3), k.ps[:, 0:3, 0:TG],
                                         k.vcol[:, 24 + b:25 + b], k.sig[:, b % 2].rearrange("p (c t) -> p c t", c=3),
                                         ALU.add, ALU.mult).then_inc(glu_out, 1)


def stage_w_out(nc, k):
    at = k.at
    k.w_out_sb, _ = at("w_out_sb", [P, KD, D_MODEL], F32, k.off_u)
    w_in = nc.alloc_semaphore("w_out_in")
    product = nc.alloc_semaphore("o_product")
    added = nc.alloc_semaphore("o_added")
    with nc.Block() as block:
        @block.sync
        def _(sp):
            for q in range(4):
                sp.dma_start(k.w_out_sb[:, :, 2 * P * q:2 * P * (q + 1)],
                             k.dram["w_out"][0].rearrange("(a p) n -> p a n", p=P)[:, :, 2 * P * q:2 * P * (q + 1)]).then_inc(w_in, 16)
                sp.wait_ge(w_in, 16 * (q + 1))

        @block.tensor
        def _(pe):
            for d in range(KD):
                pe.wait_ge(w_in, 16 * (d // 2 + 1))
                if d >= 2:
                    pe.wait_ge(added, d - 1)
                for a in range(KD):
                    for c in range(3):
                        mm = pe.matmul(k.ps[:, 4 * (d % 2) + c, 0:TG], k.w_out_sb[:, a, d * P:d * P + P],
                                       k.mixT[:, a, c * TG:c * TG + TG], start=(a == 0), stop=(a == KD - 1))
                mm.then_inc(product, 1)

        @block.vector
        def _(dve):
            for d in range(KD):
                dve.wait_ge(product, d + 1)
                x = k.xT[:, d].rearrange("p (c t) -> p c t", c=3)
                dve.tensor_tensor(x, k.ps[:, 4 * (d % 2):4 * (d % 2) + 3, 0:TG], x, ALU.add).then_inc(added, 1)


def plan_ffn(nc, k):
    at = k.at
    k.h_rest, _ = at("h_rest", [P, KD, TOK], F32R, k.off_mix)
    k.h_up, o = at("h_up", [P, KD, TOK], F32R, k.off_u)
    k.w_raw, o = at("w_raw", [P, 2, KD, P], F32, o)
    k.w_split, o = at("w_split", [P, 2, 2, KD, P], F32R, o)
    k.wd_raw, o = at("wd_raw", [P, KD, P], F32, o)
    k.wd_split, o = at("wd_split", [P, 2, KD, P], F32R, o)
    k.hu, o = at("hu", [P, 2, TOK + 2], F32, o)
    k.cv, o = at("cv", [P, 2, TOK], F32, o)
    k.gated, o = at("gated", [P, 2, TOK], F32R, o)
    k.histT, o = at("histT", [P, 2 * NF, NB, 2], F32, o)
    k.last, o = at("last", [P, 2 * NF, NB + 2], F32, o)
    k.hist_row, _ = at("hist_row", [2 * NB, 2 * DFF], F32, o)
    k.last_row, _ = at("last_row", [NB + 2, 2 * DFF], F32, o)


def stage_ffn(nc, k):
    hist_in = nc.alloc_semaphore("hist_in")
    hist_out = nc.alloc_semaphore("hist_out")
    h_upper = nc.alloc_semaphore("h_upper")
    h_split = nc.alloc_semaphore("h_split")
    a_in = nc.alloc_semaphore("w_a_in")
    g_in = nc.alloc_semaphore("w_g_in")
    d_in = nc.alloc_semaphore("w_d_in")
    w_upper = nc.alloc_semaphore("w_upper")
    w_rest = nc.alloc_semaphore("w_rest")
    up_done = nc.alloc_semaphore("up_done")
    down_done = nc.alloc_semaphore("down_done")
    left = nc.alloc_semaphore("u_left")
    begun = nc.alloc_semaphore("u_begun")
    added = nc.alloc_semaphore("d_added")
    noted = nc.alloc_semaphore("u_noted")
    convolved = nc.alloc_semaphore("u_convolved")
    silued = nc.alloc_semaphore("u_silued")
    multiplied = nc.alloc_semaphore("u_multiplied")
    gated_upper = nc.alloc_semaphore("gated_upper")
    gated_rest = nc.alloc_semaphore("gated_rest")
    own = nc.alloc_semaphore("u_own")
    turned = nc.alloc_semaphore("f_turned")
    kept = nc.alloc_semaphore("f_kept")
    out = nc.alloc_semaphore("last_out")
    k.stores.append((hist_out, 16))
    k.stores.append((out, 32))
    w_up = k.dram["w_up"][0].rearrange("(a p) (z f c) -> p a z f c", p=P, z=2, c=P)
    w_down = k.dram["w_down"][0].rearrange("(f p) n -> p f n", p=P)
    NL = 2 * NF // 4
    LAST = NF - 1

    def at_step(f):
        return slice(f, f + 1) if isinstance(f, int) else bass.ds(f, 1)

    def steps(eng, body):
        body(0, True, False)
        with eng.Fori(1, LAST) as f:
            body(f, False, False)
        body(LAST, False, True)

    with nc.Block() as block:
        @block.sync
        def _(sp):
            def load_up(f, z, loaded):
                sp.dma_start(k.w_raw[:, z], w_up[:, :, z, at_step(f), :].rearrange("p a f c -> p a (f c)")).then_inc(loaded, 16)

            def load_down(f):
                sp.dma_start(k.wd_raw[:].rearrange("p a c -> p (a c)"), w_down[:, at_step(f), :].rearrange("p f n -> p (f n)")
                             ).then_inc(d_in, 16)

            def load(f, first):
                sp.wait_ge(w_rest, 1 if first else f * 3 - 3)
                load_up(f, 0, a_in)
                sp.wait_ge(w_rest, 2 if first else f * 3 - 2)
                load_up(f, 1, g_in)
                sp.wait_ge(w_rest, f * 3 + 2)
                load_down(f)
            load_up(0, 0, a_in)
            load_up(0, 1, g_in)
            load_down(0)
            load(1, True)
            with sp.Fori(2, LAST) as f:
                load(f, False)
            load(LAST, False)

        @block.tensor
        def _(pe):
            pe.wait_ge(hist_in, 16)
            for f in range(2 * NF):
                mm = pe.transpose(k.ps[:, 3 + 4 * (f // NF), f % NF * 16:f % NF * 16 + 16], k.hist_row[:, f * P:f * P + P],
                                  k.ident[0:2 * NB, 0:2 * NB])
            mm.then_inc(turned, 1)

            def product(bank, w, x, start, stop):
                for m, (wn, xn) in enumerate(((0, 0), (0, 1), (1, 0))):
                    for c in range(3):
                        mm = pe.matmul(k.ps[:, bank + c, 0:TG], w(wn), x(xn)[:, c * TG:c * TG + TG],
                                       start=start and m == 0, stop=stop and m == 2)
                return mm

            def up(f, z, first):
                for a in range(KD):
                    if first and z == 0:
                        pe.wait_ge(h_split, a + 1)
                    mm = product(4 * z, lambda n: k.w_split[:, z, n, a, :], lambda n: (k.h_up, k.h_rest)[n][:, a], a == 0, a == KD - 1)
                mm.then_inc(up_done, 1)

            def down(d):
                bank = (4, 0, 4, 0, 0, 4, 0, 4)[d]
                product(bank, lambda n: k.wd_split[:, n, d, :], lambda n: k.gated[:, n], True, True).then_inc(down_done, 1)

            def body(f, first, last):
                pe.wait_ge(w_upper, 1 if first else f * 3)
                pe.wait_ge(w_rest, 1 if first else f * 3)
                if not first:
                    pe.wait_ge(added, f * 8 - 1)
                    pe.wait_ge(left, f * 2 - 1)
                up(f, 0, first)
                if not first:
                    pe.wait_ge(w_upper, f * 3 + 2)
                    pe.wait_ge(w_rest, f * 3 + 2)
                    pe.wait_ge(gated_rest, f)
                    pe.wait_ge(left, f * 2)
                    pe.wait_ge(added, f * 8)
                    down(0)
                    pe.wait_ge(left, f * 2 + 1)
                    down(1)
                    pe.wait_ge(added, f * 8 + 1)
                    down(2)
                    pe.wait_ge(added, f * 8 + 2)
                    down(3)
                    pe.wait_ge(added, f * 8 + 3)
                pe.wait_ge(w_upper, 2 if first else f * 3 + 1)
                pe.wait_ge(w_rest, 2 if first else f * 3 + 1)
                up(f, 1, first)
                if not first:
                    pe.wait_ge(added, f * 8 + 4)
                    down(4)
                    pe.wait_ge(left, f * 2 + 2)
                    down(5)
                    pe.wait_ge(added, f * 8 + 5)
                    down(6)
                    pe.wait_ge(added, f * 8 + 6)
                    down(7)
            steps(pe, body)
            pe.wait_ge(noted, 2 * NF)
            for n in range(NL):
                if n >= 2:
                    pe.wait_ge(kept, n + 1)
                for a in range(4):
                    mm = pe.transpose(k.ps[0:NB + 2, 3 + 4 * (n % 2), a * P:a * P + P], k.last[:, 4 * n + a, :], k.ident[:])
                mm.then_inc(turned, 1)
            pe.wait_ge(w_upper, 3 * NF)
            pe.wait_ge(w_rest, 3 * NF)
            pe.wait_ge(gated_rest, NF)
            pe.wait_ge(left, 2 * NF)
            for d in range(KD):
                pe.wait_ge(added, 8 * NF + (-1 if d == 1 else (0, 0, 1, 2, 4, 3, 5, 6)[d]))
                down(d)

        @block.scalar
        def _(act):
            act.dma_start(k.hist_row[:], k.dram["state_ffn_conv"][0].rearrange("b r n -> (b r) n")).then_inc(hist_in, 16)
            act.dma_start(k.dram["s_ffn_conv"][0, :, 0], k.dram["state_ffn_conv"][0, :, 1]).then_inc(hist_out, 16)

            def upper(f, z, loaded):
                act.wait_ge(loaded, f * 16 + 16)
                act.activation(k.w_split[:, z, 0], k.w_raw[:, z], ACT.Copy).then_inc(w_upper, 1)
            for a in range(2):
                act.activation(k.h_up[:, a], k.mixT[:, a], ACT.Copy).then_inc(h_upper, 1)
            upper(0, 0, a_in)
            upper(0, 1, g_in)
            for a in range(2, KD):
                act.activation(k.h_up[:, a], k.mixT[:, a], ACT.Copy).then_inc(h_upper, 1)
            act.wait_ge(turned, 1)
            for z in range(2):
                act.activation(k.histT[:, z * NF:(z + 1) * NF].rearrange("p f b r -> p (f b r)"), k.ps[:, 3 + 4 * z, 0:NF * 16], ACT.Copy
                               ).then_inc(kept, 1)

            def leave(f, z):
                act.wait_ge(up_done, f * 2 + (z + 1))
                src = k.ps[:, 4 * z:4 * z + 3, 0:TG]
                act.activation(k.hu[:, z, 2:].rearrange("p (c t) -> p c t", c=3), src, ACT.Copy).then_inc(left, 1)
                act.wait_ge(left, f * 2 + (z + 1))
                act.activation(k.cv[:, z], k.hu[:, z, 2:], ACT.Identity, bias=k.ccol[:, 3, at_step(f + z * NF)],
                               scale=k.ccol[:, 2, at_step(f + z * NF)]).then_inc(begun, 1)

            def body(f, first, last):
                if not first:
                    act.wait_ge(gated_rest, f)
                    act.wait_ge(noted, f * 2)
                leave(f, 0)
                if not last:
                    upper(f + 1, 0, a_in)
                leave(f, 1)
                if not last:
                    upper(f + 1, 1, g_in)
                act.wait_ge(convolved, f * 2 + 1)
                act.activation(k.cv[:, 0], k.cv[:, 0], ACT.Silu).then_inc(silued, 1)
                act.wait_ge(multiplied, f + 1)
                act.activation(k.gated[:, 0], k.cv[:, 1], ACT.Copy).then_inc(gated_upper, 1)
                act.wait_ge(d_in, f * 16 + 16)
                if not first:
                    act.wait_ge(down_done, f * 8)
                act.activation(k.wd_split[:, 0], k.wd_raw[:], ACT.Copy).then_inc(w_upper, 1)
            steps(act, body)
            for n in range(NL):
                act.wait_ge(turned, n + 2)
                act.activation(k.last_row[:, 4 * P * n:4 * P * (n + 1)], k.ps[0:NB + 2, 3 + 4 * (n % 2), :], ACT.Copy).then_inc(kept, 1)
            act.wait_ge(kept, NL + 2)
            act.dma_start(k.dram["p_ffn_conv"][0, 0], k.last_row[0:2, :]).then_inc(out, 16)
            act.dma_start(k.dram["s_ffn_conv"][0, :, 1], k.last_row[2:, :]).then_inc(out, 16)

        @block.gpsimd
        def _(pool):
            def rest(z):
                pool.tensor_tensor(k.w_split[:, z, 1], k.w_raw[:, z], k.w_split[:, z, 0].bitcast(F32), ALU.subtract).then_inc(w_rest, 1)

            def note(f, z):
                pool.wait_ge(left, f * 2 + (z + 1))
                pool.tensor_copy(k.last[:, at_step(f + z * NF), :].rearrange("p f t -> p (f t)"),
                                 k.hu[:, z, SEQ:TOK + 2]).then_inc(noted, 1)
            for z in range(2):
                pool.wait_ge(w_upper, z + 1)
                rest(z)

            def body(f, first, last):
                note(f, 0)
                if not last:
                    pool.wait_ge(w_upper, f * 3 + 3)
                    rest(0)
                note(f, 1)
                if not last:
                    pool.wait_ge(w_upper, f * 3 + 4)
                    rest(1)
                pool.wait_ge(w_upper, f * 3 + (3 if last else 5))
                pool.tensor_tensor(k.wd_split[:, 1], k.wd_raw[:], k.wd_split[:, 0].bitcast(F32), ALU.subtract).then_inc(w_rest, 1)
            steps(pool, body)

        @block.vector
        def _(dve):
            dve.sem_inc(added, 8)
            dve.memset(k.hu[:, :, 0:2], 0.0).then_inc(own, 1)
            for a in range(KD):
                dve.wait_ge(h_upper, a + 1)
                dve.tensor_tensor(k.h_rest[:, a], k.mixT[:, a], k.h_up[:, a].bitcast(F32), ALU.subtract).then_inc(h_split, 1)
            dve.wait_ge(own, 1)
            dve.wait_ge(kept, 2)

            def add(f, d):
                bank = (4, 0, 4, 0, 0, 4, 0, 4)[d]
                dve.wait_ge(down_done, f * 8 + (d - 7))
                x = k.xT[:, d].rearrange("p (c t) -> p c t", c=3)
                dve.tensor_tensor(x, k.ps[:, bank:bank + 3, 0:TG], x, ALU.add).then_inc(added, 1)

            def convolve(f, z):
                dve.wait_ge(begun, f * 2 + (z + 1))
                w1, w0 = k.ccol[:, 1, at_step(f + z * NF)], k.ccol[:, 0, at_step(f + z * NF)]
                old = k.histT[:, at_step(f + z * NF), :, :].rearrange("p f b r -> p (f b) r")
                for n, (w, done, value) in enumerate(((w1, own, f * 2 + (z + 2)), (w0, convolved, None))):
                    dve.scalar_tensor_tensor(k.cv[:, z, 0:SEQ], k.hu[:, z, 1 - n:SEQ + 1 - n], w, k.cv[:, z, 0:SEQ],
                                             ALU.mult, ALU.add)
                    dve.scalar_tensor_tensor(k.cv[:, z, SEQ:TOK], old[:, :, 1 - n], w, k.cv[:, z, SEQ:TOK],
                                             ALU.mult, ALU.add).then_inc(done, 1)
                    if value is not None:
                        dve.wait_ge(own, value)

            def body(f, first, last):
                if not first:
                    for d in range(4):
                        add(f, d)
                convolve(f, 0)
                if not first:
                    for d in range(4, KD):
                        add(f, d)
                convolve(f, 1)
                dve.wait_ge(silued, f + 1)
                dve.wait_ge(convolved, f * 2 + 2)
                dve.tensor_tensor(k.cv[:, 1], k.cv[:, 0], k.cv[:, 1], ALU.mult).then_inc(multiplied, 1)
                dve.wait_ge(gated_upper, f + 1)
                dve.tensor_tensor(k.gated[:, 1], k.cv[:, 1], k.gated[:, 0].bitcast(F32), ALU.subtract).then_inc(gated_rest, 1)
            steps(dve, body)
            for d in range(KD):
                add(NF, d)


def stage_results(nc, k):
    at = k.at
    k.y_row, o = at("y_row", [P, NT, D_MODEL], F32, k.off_u)
    k.ys_row, _ = at("ys_row", [NB, D_MODEL], F32, o)
    turned = nc.alloc_semaphore("y_turned")
    kept_act = nc.alloc_semaphore("y_kept_act")
    kept_dve = nc.alloc_semaphore("y_kept_dve")
    out = nc.alloc_semaphore("y_out")
    k.stores.append((out, 16 * (NT + 1)))
    with nc.Block() as block:
        @block.tensor
        def _(pe):
            for t in range(NT):
                for half in range(2):
                    if t >= 4:
                        pe.wait_ge(kept_dve if half else kept_act, t - 3)
                    for a in range(4):
                        mm = pe.transpose(k.ps[:, (2 * t + half) % 8, a * P:a * P + P], k.mixT[:, 4 * half + a, t * P:t * P + P], k.ident[:])
                    mm.then_inc(turned, 1)
            for half in range(2):
                pe.wait_ge(kept_dve if half else kept_act, 5)
                for a in range(4):
                    mm = pe.transpose(k.ps[0:NB, half, a * P:a * P + P], k.mixT[:, 4 * half + a, SEQ:TOK], k.ident[:])
                mm.then_inc(turned, 1)

        @block.scalar
        def _(act):
            for t in range(NT):
                act.wait_ge(turned, 2 * t + 1)
                act.activation(k.y_row[:, t, 0:512], k.ps[:, 2 * t % 8, :], ACT.Copy).then_inc(kept_act, 1)
            act.wait_ge(turned, 2 * NT + 1)
            act.activation(k.ys_row[:, 0:512], k.ps[0:NB, 0, :], ACT.Copy).then_inc(kept_act, 1)

        @block.vector
        def _(dve):
            for t in range(NT):
                dve.wait_ge(turned, 2 * t + 2)
                dve.tensor_copy(k.y_row[:, t, 512:], k.ps[:, (2 * t + 1) % 8, :]).then_inc(kept_dve, 1)
            dve.wait_ge(turned, 2 * NT + 2)
            dve.tensor_copy(k.ys_row[:, 512:], k.ps[0:NB, 1, :]).then_inc(kept_dve, 1)

        @block.sync
        def _(sp):
            for t in range(NT):
                sp.wait_ge(kept_act, t + 1)
                sp.wait_ge(kept_dve, t + 1)
                sp.dma_start(k.dram["y_prompt"][0, t * P:t * P + P, :], k.y_row[:, t]).then_inc(out, 16)
            sp.wait_ge(kept_act, NT + 1)
            sp.wait_ge(kept_dve, NT + 1)
            sp.dma_start(k.dram["y_sample"].rearrange("b s d -> (b s) d"), k.ys_row[:]).then_inc(out, 16)


def build(nc, k, upto=99):
    k.ps = nc.alloc_psum_tensor("ps", [P, 8, 512], F32)
    plan(nc, k)
    k.stores = []
    steps = [lambda: stage_load(nc, k),
             lambda: stage_norm(nc, k, "mix", k.mixT, 0, k.off_u),
             lambda: stage_project(nc, k),
             lambda: stage_compress(nc, k),
             lambda: stage_prompt_compressed(nc, k),
             lambda: stage_attend(nc, k),
             lambda: stage_turn_attention(nc, k),
             lambda: stage_sample_prepare(nc, k),
             lambda: stage_sample_attention(nc, k),
             lambda: (plan_ssm(nc, k), stage_ssm_parameters(nc, k)),
             lambda: stage_ssm_states(nc, k),
             lambda: stage_ssm_outputs(nc, k),
             lambda: stage_w_out(nc, k),
             lambda: stage_norm(nc, k, "ffn", k.mixT, 8, k.off_u),
             lambda: (plan_ffn(nc, k), stage_ffn(nc, k)),
             lambda: stage_norm(nc, k, "final", k.mixT, 16, k.off_u),
             lambda: stage_results(nc, k)]
    for n, s in enumerate(steps):
        if n < upto:
            s()
    with nc.Block() as block:
        @block.sync
        def _(sp):
            for stored, count in k.stores:
                sp.wait_ge(stored, count)


INPUTS = ["x_prompt", "x_sample", "cache_kv_cmp", "cache_kv_sel", "cache_kv_win", "state_ssm_re", "state_ssm_im",
          "state_ffn_conv", "page_table", "norm_mix", "w_in", "pe_cmp", "w_cmp", "ssm_a_re", "ssm_a_im", "ssm_log_dt",
          "ssm_b_re", "ssm_b_im", "ssm_c_re", "ssm_c_im", "ssm_d", "w_glu", "b_glu", "w_out", "norm_ffn", "w_up",
          "conv_w", "conv_b", "w_down", "norm_final"]
OUTPUTS = {"y_prompt": (1, SEQ, D_MODEL), "y_sample": (NB, 1, D_MODEL),
           "p_kv_cmp": (1, 1, SEQ, 2, NKV, HD), "p_kv_sel": (1, 1, SEQ, 2, NKV, HD), "p_kv_win": (1, 1, WIN, 2, NKV, HD),
           "p_ssm_re": (1, 1, G, PS), "p_ssm_im": (1, 1, G, PS), "p_ffn_conv": (1, 1, 2, 2 * DFF),
           "s_kv_cmp": (1, NB, 1, 2, NKV, HD), "s_kv_sel": (1, NB, 1, 2, NKV, HD), "s_kv_win": (1, NB, WIN, 2, NKV, HD),
           "s_ssm_re": (1, NB, G, PS), "s_ssm_im": (1, NB, G, PS), "s_ffn_conv": (1, NB, 2, 2 * DFF)}


def kernel(**inputs):
    import numpy as _np
    import concourse.bacc as _bacc
    from concourse import mybir as _mybir
    from concourse.bass_utils import run_bass_kernel_spmd as _run

    nc = _bacc.Bacc("TRN2", target_bir_lowering=False, num_devices=1)
    arrays = {}
    k = Net()
    k.dram = {}
    for name in INPUTS:
        a = _np.ascontiguousarray(inputs[name])
        arrays[f"in_{name}"] = a
        k.dram[name] = nc.dram_tensor(f"in_{name}", a.shape, _mybir.dt.from_np(a.dtype), kind="ExternalInput").ap()
    for name, shape in OUTPUTS.items():
        k.dram[name] = nc.dram_tensor(f"out_{name}", shape, _mybir.dt.float32, kind="ExternalOutput").ap()
    build(nc, k)
    r = _run(nc, [arrays], core_ids=[0])
    return tuple(r.results[0][f"out_{name}"] for name in OUTPUTS)
```
